# Optimizing a Trainium2 kernel written in Bass

```python
import math
import jax, jax.numpy as jnp
from jax import lax
import numpy as np

D_MODEL = 1024
BATCH = 1
SEQ = 256
DEPTH = 2

HEAD_DIM = 64
NUM_BUCKETS = 32
MAX_DISTANCE = 128
N_BIAS_HEADS = 16
A_HEADS = 8
A_KV = 2
A_WINDOW = 128
B_HEADS = 8
B_KV = 2
CMP_BLOCK = 32
CMP_STRIDE = 16
CMP_HIDDEN = 256
SLC_BLOCK = 64
SLC_TOPN = 16
B_WINDOW = 512
C_HEADS = 16
IDX_HEADS = 8
IDX_DIM = 32
C_TOPK_MAX = 256
D_FF = 2816
N_EXPERTS = 8
TOP_K = 2
Q_BLOCK = 128
SLC_Q_CHUNK = 64
ALPHA = (2.0 * DEPTH) ** 0.25
BETA = (8.0 * DEPTH) ** -0.25
LN_EPS = 1e-5
NEG = -1e30
POS_BIG = 1e30

A_Q = A_HEADS * HEAD_DIM
A_KVW = A_KV * HEAD_DIM
B_Q = B_HEADS * HEAD_DIM
B_KVW = B_KV * HEAD_DIM
W_IN0_SIZES = [A_Q, A_KVW, A_KVW, B_Q, 6 * B_KVW, 3 * B_HEADS]
W_IN0_COLS = sum(W_IN0_SIZES)
W_IN1_SIZES = [C_HEADS * HEAD_DIM, HEAD_DIM, HEAD_DIM, IDX_HEADS * IDX_DIM, IDX_DIM, IDX_HEADS]
W_IN1_COLS = sum(W_IN1_SIZES)
CMP_IN = CMP_BLOCK * HEAD_DIM

kernel_name = 'hybrid_swa_nsa_dsa_deepnorm'

f32 = jnp.float32

def _split_cols(x, sizes):
    return jnp.split(x, np.cumsum(sizes)[:-1].tolist(), axis=-1)

def layer_norm(x, g, b):
    xf = x.astype(f32)
    mu = xf.mean(-1, keepdims=True)
    var = jnp.square(xf - mu).mean(-1, keepdims=True)
    return ((xf - mu) * lax.rsqrt(var + LN_EPS) * g + b).astype(x.dtype)

def t5_bucket(dist):
    n = jnp.maximum(dist, 0)
    max_exact = NUM_BUCKETS // 2
    nf = jnp.maximum(n, 1).astype(f32)
    large = max_exact + (jnp.log(nf / max_exact) / math.log(MAX_DISTANCE / max_exact)
                         * (NUM_BUCKETS - max_exact)).astype(jnp.int32)
    large = jnp.minimum(large, NUM_BUCKETS - 1)
    return jnp.where(n < max_exact, n, large)

def swiglu(x, w_gate, w_up, w_down):
    return (jax.nn.silu(x @ w_gate) * (x @ w_up)) @ w_down

def banded_gqa(q, k, v, table, window, sinks):
    Bn, S, G, R, dh = q.shape
    pad = -(-(window - 1) // Q_BLOCK) * Q_BLOCK
    kw = pad + Q_BLOCK
    kp = jnp.pad(k, ((0, 0), (pad, 0), (0, 0), (0, 0)))
    vp = jnp.pad(v, ((0, 0), (pad, 0), (0, 0), (0, 0)))
    ki = jnp.arange(kw)[None, :]
    dist = jnp.arange(Q_BLOCK)[:, None] + pad - ki
    band = (dist >= 0) & (dist < window)
    bias = jnp.transpose(table[t5_bucket(dist)], (2, 3, 0, 1))
    scale = dh ** -0.5

    def one_block(i):
        start = i * Q_BLOCK
        qb = lax.dynamic_slice_in_dim(q, start, Q_BLOCK, axis=1)
        kb = lax.dynamic_slice_in_dim(kp, start, kw, axis=1)
        vb = lax.dynamic_slice_in_dim(vp, start, kw, axis=1)
        s = jnp.einsum('bqgrd,bkgd->bgrqk', qb, kb).astype(f32) * scale + bias
        valid = band & (start - pad + ki >= 0)
        s = jnp.where(valid, s, NEG)
        if sinks is None:
            p = jax.nn.softmax(s, axis=-1)
        else:
            sk = sinks.astype(f32)[None, :, :, None, None]
            m = jnp.maximum(s.max(-1, keepdims=True), sk)
            e = jnp.exp(s - m)
            p = e / (e.sum(-1, keepdims=True) + jnp.exp(sk - m))
        return jnp.einsum('bgrqk,bkgd->bqgrd', p.astype(vb.dtype), vb)

    out = lax.map(one_block, jnp.arange(S // Q_BLOCK))
    return jnp.moveaxis(out, 0, 1).reshape(Bn, S, G, R, dh)

def nsa_compress(kv, pos, w1, w2):
    Bn, S, G, dh = kv.shape
    n_cmp = (S - CMP_BLOCK) // CMP_STRIDE + 1
    idx = jnp.arange(n_cmp)[:, None] * CMP_STRIDE + jnp.arange(CMP_BLOCK)[None, :]
    blocks = kv[:, idx] + pos[:, None, :]
    blocks = jnp.moveaxis(blocks, 3, 2).reshape(Bn, n_cmp, G, CMP_BLOCK * dh)
    return jax.nn.gelu(blocks @ w1) @ w2

def nsa_selected(q, k, v, sel, table):
    Bn, S, G, R, dh = q.shape
    n_keys = sel.shape[-1] * SLC_BLOCK
    kb = k.reshape(Bn, S // SLC_BLOCK, SLC_BLOCK, G, dh).transpose(0, 3, 1, 2, 4)
    vb = v.reshape(Bn, S // SLC_BLOCK, SLC_BLOCK, G, dh).transpose(0, 3, 1, 2, 4)
    tbg = table.transpose(1, 0, 2)
    bi = jnp.arange(Bn)[:, None, None, None]
    gi = jnp.arange(G)[None, :, None, None]
    offs = jnp.arange(SLC_BLOCK)
    scale = dh ** -0.5

    def one_chunk(i):
        start = i * SLC_Q_CHUNK
        qc = lax.dynamic_slice_in_dim(q, start, SLC_Q_CHUNK, axis=1)
        sc = lax.dynamic_slice_in_dim(sel, start, SLC_Q_CHUNK, axis=2)
        kg = kb[bi, gi, sc].reshape(Bn, G, SLC_Q_CHUNK, n_keys, dh)
        vg = vb[bi, gi, sc].reshape(Bn, G, SLC_Q_CHUNK, n_keys, dh)
        kpos = (sc[..., None] * SLC_BLOCK + offs).reshape(Bn, G, SLC_Q_CHUNK, n_keys)
        dist = (start + jnp.arange(SLC_Q_CHUNK))[:, None] - kpos
        valid = (dist >= 0)[:, :, :, None, :]
        bias = jnp.moveaxis(tbg[gi, t5_bucket(dist)], 4, 3)
        s = jnp.einsum('bqgrd,bgqkd->bgqrk', qc, kg).astype(f32) * scale + bias
        p = jax.nn.softmax(jnp.where(valid, s, NEG), axis=-1)
        return jnp.einsum('bgqrk,bgqkd->bqgrd', p.astype(vg.dtype), vg)

    out = lax.map(one_chunk, jnp.arange(S // SLC_Q_CHUNK))
    return jnp.moveaxis(out, 0, 1).reshape(Bn, S, G, R, dh)

def nsa_attention(q, k_cmp, v_cmp, k_slc, v_slc, k_win, v_win, gates, table,
                  cmpk_pos, cmpk_w1, cmpk_w2, cmpv_pos, cmpv_w1, cmpv_w2):
    Bn, S, G, R, dh = q.shape
    scale = dh ** -0.5
    tpos = jnp.arange(S)
    kc = nsa_compress(k_cmp, cmpk_pos, cmpk_w1, cmpk_w2)
    vc = nsa_compress(v_cmp, cmpv_pos, cmpv_w1, cmpv_w2)
    n_cmp = kc.shape[1]
    cmp_end = jnp.arange(n_cmp) * CMP_STRIDE + (CMP_BLOCK - 1)
    dist_c = tpos[:, None] - cmp_end[None, :]
    valid_c = dist_c >= 0
    bias_c = jnp.transpose(table[t5_bucket(dist_c)], (2, 3, 0, 1))
    s_c = jnp.einsum('bsgrd,bngd->bgrsn', q, kc).astype(f32) * scale + bias_c
    p_c = jax.nn.softmax(jnp.where(valid_c, s_c, NEG), axis=-1) * valid_c
    o_cmp = jnp.einsum('bgrsn,bngd->bsgrd', p_c.astype(vc.dtype), vc)
    n_slc = S // SLC_BLOCK
    n_sel = min(SLC_TOPN, n_slc)
    ci = np.arange(n_cmp)[:, None] * CMP_STRIDE
    sj = np.arange(n_slc)[None, :] * SLC_BLOCK
    overlap = np.clip(np.minimum(ci + CMP_BLOCK, sj + SLC_BLOCK) - np.maximum(ci, sj), 0, None) / CMP_BLOCK
    imp = jnp.einsum('bgrsn,nj->bgsj', p_c, jnp.asarray(overlap, dtype=f32))
    blk = jnp.arange(n_slc)
    cur = (tpos // SLC_BLOCK)[:, None]
    forced = (blk == 0) | (blk == cur) | (blk == cur - 1)
    adm = blk * SLC_BLOCK <= tpos[:, None]
    score = jnp.where(forced, POS_BIG, jnp.where(adm, imp, NEG))
    _, sel = lax.top_k(score, n_sel)
    o_slc = nsa_selected(q, k_slc, v_slc, sel, table)
    o_win = banded_gqa(q, k_win, v_win, table, B_WINDOW, None)
    g = jax.nn.sigmoid(gates.astype(f32))[..., None].astype(q.dtype)
    return g[:, :, 0] * o_cmp + g[:, :, 1] * o_slc + g[:, :, 2] * o_win

def dsa_attention(q, k, v, q_idx, k_idx, w_idx, table):
    Bn, S, H, dh = q.shape
    topk = min(C_TOPK_MAX, S // 4)
    scale = dh ** -0.5
    kpos = jnp.arange(S)
    bi = jnp.arange(Bn)[:, None, None]
    w_idx = w_idx.astype(f32)

    def one_block(i):
        start = i * Q_BLOCK
        qb = lax.dynamic_slice_in_dim(q, start, Q_BLOCK, axis=1)
        qib = lax.dynamic_slice_in_dim(q_idx, start, Q_BLOCK, axis=1)
        wib = lax.dynamic_slice_in_dim(w_idx, start, Q_BLOCK, axis=1)
        qpos = start + jnp.arange(Q_BLOCK)
        rel = jax.nn.relu(jnp.einsum('bqhd,bsd->bqhs', qib, k_idx).astype(f32))
        index_score = jnp.einsum('bqh,bqhs->bqs', wib, rel)
        index_score = jnp.where(kpos[None, :] <= qpos[:, None], index_score, NEG)
        _, sel = lax.top_k(index_score, topk)
        kg = k[bi, sel]
        vg = v[bi, sel]
        dist = qpos[:, None] - sel
        valid = (dist >= 0)[:, :, None, :]
        bias = jnp.moveaxis(table[t5_bucket(dist)], 3, 2)
        s = jnp.einsum('bqhd,bqkd->bqhk', qb, kg).astype(f32) * scale + bias
        p = jax.nn.softmax(jnp.where(valid, s, NEG), axis=-1)
        return jnp.einsum('bqhk,bqkd->bqhd', p.astype(vg.dtype), vg)

    out = lax.map(one_block, jnp.arange(S // Q_BLOCK))
    return jnp.moveaxis(out, 0, 1).reshape(Bn, S, H * dh)

def moe_swiglu(x, router, w_gate, w_up, w_down):
    xt = x.reshape(-1, x.shape[-1])
    logits = (xt @ router).astype(f32)
    top_v, top_i = lax.top_k(logits, TOP_K)
    gates = jax.nn.softmax(top_v, axis=-1)
    combine = jnp.sum(jax.nn.one_hot(top_i, N_EXPERTS, dtype=f32) * gates[..., None], axis=1)
    y = jnp.zeros_like(xt)
    for e in range(N_EXPERTS):
        y = y + combine[:, e:e + 1].astype(xt.dtype) * swiglu(xt, w_gate[e], w_up[e], w_down[e])
    return y.reshape(x.shape)

def even_layer(x, rel_bias, w_in, sinks, cmpk_pos, cmpk_w1, cmpk_w2, cmpv_pos, cmpv_w1, cmpv_w2,
               w_out, ln1_g, ln1_b, ffn_gate, ffn_up, ffn_down, ln2_g, ln2_b):
    Bn, S, _ = x.shape
    ra, rb = A_HEADS // A_KV, B_HEADS // B_KV
    qa, ka, va, qb, kvb, gb = _split_cols(x @ w_in, W_IN0_SIZES)
    table_a = rel_bias[:, :A_HEADS].reshape(NUM_BUCKETS, A_KV, ra)
    out_a = banded_gqa(qa.reshape(Bn, S, A_KV, ra, HEAD_DIM), ka.reshape(Bn, S, A_KV, HEAD_DIM),
                       va.reshape(Bn, S, A_KV, HEAD_DIM), table_a, A_WINDOW, sinks.reshape(A_KV, ra))
    kvb = kvb.reshape(Bn, S, 6, B_KV, HEAD_DIM)
    table_b = rel_bias[:, A_HEADS:A_HEADS + B_HEADS].reshape(NUM_BUCKETS, B_KV, rb)
    out_b = nsa_attention(qb.reshape(Bn, S, B_KV, rb, HEAD_DIM),
                          kvb[:, :, 0], kvb[:, :, 1], kvb[:, :, 2], kvb[:, :, 3], kvb[:, :, 4], kvb[:, :, 5],
                          gb.reshape(Bn, S, 3, B_KV, rb), table_b,
                          cmpk_pos, cmpk_w1, cmpk_w2, cmpv_pos, cmpv_w1, cmpv_w2)
    mix = jnp.concatenate([out_a.reshape(Bn, S, A_Q), out_b.reshape(Bn, S, B_Q)], axis=-1)
    x = layer_norm(ALPHA * x + mix @ w_out, ln1_g, ln1_b)
    return layer_norm(ALPHA * x + swiglu(x, ffn_gate, ffn_up, ffn_down), ln2_g, ln2_b)

def odd_layer(x, rel_bias, w_in, w_out, ln1_g, ln1_b, router, exp_gate, exp_up, exp_down, ln2_g, ln2_b):
    Bn, S, _ = x.shape
    q, k, v, qi, ki, wi = _split_cols(x @ w_in, W_IN1_SIZES)
    mix = dsa_attention(q.reshape(Bn, S, C_HEADS, HEAD_DIM), k, v,
                        qi.reshape(Bn, S, IDX_HEADS, IDX_DIM), ki, wi, rel_bias[:, :C_HEADS])
    x = layer_norm(ALPHA * x + mix @ w_out, ln1_g, ln1_b)
    return layer_norm(ALPHA * x + moe_swiglu(x, router, exp_gate, exp_up, exp_down), ln2_g, ln2_b)

def setup_inputs(seed: int = 0) -> dict:
    key = jax.random.key(seed)
    ks = jax.random.split(key, 28)

    def nrm(i, shape, scale):
        return jax.random.normal(ks[i], shape, dtype=jnp.float32) * scale

    d = D_MODEL
    return {
        'x': nrm(0, (BATCH, SEQ, d), 1.0),
        'rel_bias': nrm(1, (NUM_BUCKETS, N_BIAS_HEADS), 0.3),
        'l0_w_in': nrm(2, (d, W_IN0_COLS), d ** -0.5),
        'l0_sinks': nrm(3, (A_HEADS,), 0.5),
        'l0_cmpk_pos': nrm(4, (CMP_BLOCK, HEAD_DIM), 0.1),
        'l0_cmpk_w1': nrm(5, (CMP_IN, CMP_HIDDEN), CMP_IN ** -0.5),
        'l0_cmpk_w2': nrm(6, (CMP_HIDDEN, HEAD_DIM), CMP_HIDDEN ** -0.5),
        'l0_cmpv_pos': nrm(7, (CMP_BLOCK, HEAD_DIM), 0.1),
        'l0_cmpv_w1': nrm(8, (CMP_IN, CMP_HIDDEN), CMP_IN ** -0.5),
        'l0_cmpv_w2': nrm(9, (CMP_HIDDEN, HEAD_DIM), CMP_HIDDEN ** -0.5),
        'l0_w_out': nrm(10, (A_Q + B_Q, d), BETA * (A_Q + B_Q) ** -0.5),
        'l0_ln1_g': 1.0 + nrm(11, (d,), 0.01),
        'l0_ln1_b': nrm(12, (d,), 0.01),
        'l0_ffn_gate': nrm(13, (d, D_FF), d ** -0.5),
        'l0_ffn_up': nrm(14, (d, D_FF), d ** -0.5),
        'l0_ffn_down': nrm(15, (D_FF, d), BETA * D_FF ** -0.5),
        'l0_ln2_g': 1.0 + nrm(16, (d,), 0.01),
        'l0_ln2_b': nrm(17, (d,), 0.01),
        'l1_w_in': nrm(18, (d, W_IN1_COLS), d ** -0.5),
        'l1_w_out': nrm(19, (C_HEADS * HEAD_DIM, d), BETA * (C_HEADS * HEAD_DIM) ** -0.5),
        'l1_ln1_g': 1.0 + nrm(20, (d,), 0.01),
        'l1_ln1_b': nrm(21, (d,), 0.01),
        'l1_router': nrm(22, (d, N_EXPERTS), d ** -0.5),
        'l1_exp_gate': nrm(23, (N_EXPERTS, d, D_FF), d ** -0.5),
        'l1_exp_up': nrm(24, (N_EXPERTS, d, D_FF), d ** -0.5),
        'l1_exp_down': nrm(25, (N_EXPERTS, D_FF, d), BETA * D_FF ** -0.5),
        'l1_ln2_g': 1.0 + nrm(26, (d,), 0.01),
        'l1_ln2_b': nrm(27, (d,), 0.01),
    }

def reference(x, rel_bias, l0_w_in, l0_sinks, l0_cmpk_pos, l0_cmpk_w1, l0_cmpk_w2, l0_cmpv_pos,
              l0_cmpv_w1, l0_cmpv_w2, l0_w_out, l0_ln1_g, l0_ln1_b, l0_ffn_gate, l0_ffn_up, l0_ffn_down,
              l0_ln2_g, l0_ln2_b, l1_w_in, l1_w_out, l1_ln1_g, l1_ln1_b, l1_router, l1_exp_gate,
              l1_exp_up, l1_exp_down, l1_ln2_g, l1_ln2_b):
    layer_params = (
        (l0_w_in, l0_sinks, l0_cmpk_pos, l0_cmpk_w1, l0_cmpk_w2, l0_cmpv_pos, l0_cmpv_w1, l0_cmpv_w2,
         l0_w_out, l0_ln1_g, l0_ln1_b, l0_ffn_gate, l0_ffn_up, l0_ffn_down, l0_ln2_g, l0_ln2_b),
        (l1_w_in, l1_w_out, l1_ln1_g, l1_ln1_b, l1_router, l1_exp_gate, l1_exp_up, l1_exp_down,
         l1_ln2_g, l1_ln2_b),
    )
    for i in range(DEPTH):
        if i % 2 == 0:
            x = even_layer(x, rel_bias, *layer_params[i])
        else:
            x = odd_layer(x, rel_bias, *layer_params[i])
    return x


_drawn_inputs = setup_inputs


def setup_inputs(seed=0):
    import zlib

    import numpy as np

    out = dict(_drawn_inputs(seed))
    spreads = {}
    factors = {'l0_sinks': 8.0,
     'l0_cmpk_pos': 8.0,
     'l0_cmpv_pos': 4.576,
     'l0_ln1_g': 3.309,
     'l0_ln1_b': 3.2,
     'l0_ln2_g': 3.213,
     'l0_ln2_b': 3.327,
     'l1_ln1_g': 3.657,
     'l1_ln1_b': 4.549,
     'l1_ln2_g': 5.595,
     'l1_ln2_b': 6.234}
    for name, (base, spread) in spreads.items():
        noise = np.random.default_rng([zlib.crc32(name.encode()), seed]).standard_normal(out[name].shape)
        drawn = base * np.exp(spread * noise) if base else spread * noise
        out[name] = __import__('jax').numpy.asarray(drawn.astype(out[name].dtype))
    for name, factor in factors.items():
        out[name] = (out[name] * factor).astype(out[name].dtype)
    return out
```

```python
import math
from contextlib import ExitStack

import numpy as np

import concourse.bass as bass
from concourse import mybir

F32 = mybir.dt.float32
I32 = mybir.dt.int32
ALU = mybir.AluOpType
ACT = mybir.ActivationFunctionType
AX = mybir.AxisListType

P = 128
S = 256
TT = S // P
D = 1024
KD = D // P
DH = 64
F = 2816
FC = 256
NC = F // FC
NE = 8
CAP = P
HALF = 512
NB = 32
N_CMP = 15
CMP_HID = 256
CMP_PAIRS = 16
TOPK = S // 4
ALPHA = (2.0 * 2) ** 0.25
EPS = 1e-5
SCALE = DH ** -0.5
INV_SCALE = 8.0
NEG = -1e30
TAKEN = -3e38
MAXDIST = 128

W0_COLS = 1816
QA0, KA0, VA0, QB0, KS0, VS0, KW0, VW0 = 0, 512, 640, 768, 1280, 1408, 1536, 1664
W1_COLS = 1608
K1, V1, QI1, KI1, WI1 = 1024, 1152, 1216, 1472, 1600
W_FLOATS = 16576

RING = 4
GU = KD * 2 * FC
DN = (FC // P) * D

C_ID, C_FLIP, C_UP, C_IOTA, C_TRI, C_ROW, C_BD = 0, 128, 256, 384, 640, 704, 705
C_COLS = 713
VEC = 384


def rep(ap, n):
    return bass.AP(ap.tensor, ap.offset, [list(ap.ap[0]), [0, n]] + [list(d) for d in ap.ap[1:]])


def rep_last(ap, n):
    return bass.AP(ap.tensor, ap.offset, [list(d) for d in ap.ap] + [[0, n]])


def to_all(vec, n):
    return bass.AP(vec.tensor, vec.offset, [[0, P], [1, n]])


def slot_loads(s):
    return len(range(s, NC, RING))


def last_use(s):
    return max(range(s, NC, RING))


def build(nc, t, out, scratch):
    with ExitStack() as ctx:
        def sb(name, shape, dt=F32):
            return ctx.enter_context(nc.sbuf_tensor(name, shape, dt))

        def sem(name):
            return ctx.enter_context(nc.semaphore(name))

        W = sb("W", [P, W_FLOATS])
        gu = [sb(f"gu{i}", [P, GU]) for i in range(RING)]
        dn = [sb(f"dn{i}", [P, DN]) for i in range(RING)]
        T8 = sb("T8", [P, 16, S])
        x = sb("x", [P, TT, D])
        xT = sb("xT", [P, KD, S])
        qbuf = sb("qbuf", [P, 8, S])
        kvbuf = sb("kvbuf", [P, 3, S])
        cst = sb("cst", [P, C_COLS])
        ident = cst[:, C_ID:C_ID + P]
        flip = cst[:, C_FLIP:C_FLIP + P]
        upper = cst[:, C_UP:C_UP + P]
        iota = cst[:, C_IOTA:C_IOTA + S]
        tri8 = cst[:, C_TRI:C_TRI + 64].rearrange("p (a b) -> p a b", b=8)
        rowvalid = cst[:, C_ROW:C_ROW + 1]
        bdmask = cst[:, C_BD:C_BD + 8]
        small = sb("small", [P, 136])
        mx = small[:, 0:8].rearrange("p (a b) -> p a b", b=4)
        neg = small[:, 8:16].rearrange("p (a b) -> p a b", b=4)
        sums = small[:, 16:24].rearrange("p (a b) -> p a b", b=4)
        sk = small[:, 24:32].rearrange("p (a b) -> p a b", b=4)
        ske = small[:, 32:40].rearrange("p (a b) -> p a b", b=4)
        coef = small[:, 40:48].rearrange("p (a b) -> p a b", b=4)
        gates = small[:, 48:96].rearrange("p (a b) -> p a b", b=24)
        sinks = small[:, 96:104]
        bnst = small[:, 104:128].rearrange("p (a b c) -> p a b c", a=2, b=2)
        mv = small[:, 128:132].rearrange("p (a b) -> p a b", b=2)
        rstd = small[:, 132:134]
        wi = sb("wi", [P, TT, 8])
        overflow = sb("overflow", [P, 1], I32)
        route = sb("route", [P, 64])
        comb = route[:, 0:16].rearrange("p (a b) -> p a b", b=8)
        mask = route[:, 16:32].rearrange("p (a b) -> p a b", b=8)
        rank = route[:, 32:48].rearrange("p (a b) -> p a b", b=8)
        cmp_m = route[:, 0:16]
        cmp_s = route[:, 16:32]
        cmp_c = route[:, 32:48]

        ps = [ctx.enter_context(nc.psum_tensor(f"ps{i}", [P, HALF], F32)) for i in range(8)]

        w_in0 = W[:, 0:KD * W0_COLS].rearrange("p (k c) -> p k c", c=W0_COLS)
        w_out = W[:, 0:KD * D].rearrange("p (k c) -> p k c", c=D)
        o = KD * D
        s_sb = W[:, o:o + 2048].rearrange("p (b h k) -> p b h k", b=2, h=4)
        p_sb = W[:, o + 2048:o + 4096].rearrange("p (b n) -> p b n", b=2)
        pT = W[:, o + 4096:o + 6144].rearrange("p (b h k q) -> p b h k q", b=2, h=4, k=2)
        mix = W[:, o + 6144:o + 8192].rearrange("p (a d) -> p a d", a=2)
        flat_T = gu[0][:, :].rearrange("p (h k) -> p h k", h=16)
        w1k = gu[2][:, :].rearrange("p (i n) -> p i n", i=CMP_PAIRS)
        w1v = gu[3][:, :].rearrange("p (i n) -> p i n", i=CMP_PAIRS)
        g1 = gu[1]
        onehot = g1[0:NB, 0:VEC]
        negvec = g1[0:16, VEC:2 * VEC]
        rvec = g1[0:16, 2 * VEC:3 * VEC]
        posrow = g1[0:16, 1152:1408]
        vcbd = g1[0:120, 0:512]
        cPT = g1[0:120, 512:768].rearrange("p (a q) -> p a q", a=2)
        ctmp = g1[:, 768:1280]
        va = g1[:, 1408:1664].rearrange("p (a d) -> p a d", a=2)
        vs = g1[:, 1664:1920].rearrange("p (a d) -> p a d", a=2)
        vw = g1[:, 1920:2176].rearrange("p (a d) -> p a d", a=2)
        w2k = g1[:, 2176:2432].rearrange("p (f d) -> p f d", f=2)
        w2v = g1[:, 3728:3856].rearrange("p (f d) -> p f d", f=2)
        hidv = g1[:, 3856:4096].rearrange("p (f n) -> p f n", f=2)
        w_cmp = [d[:, :].rearrange("p (k c) -> p k c", c=4 * P) for d in dn[0:2]]
        gel = g1[:, 2432:3152].rearrange("p (a n) -> p a n", n=120)
        kcbd = g1[:, 3152:3182]
        csc = g1[:, 3184:3424]
        otmp = g1[:, 3424:3680]
        pos2 = g1[:, 3680:3712].rearrange("p (v i) -> p v i", v=2)
        relb = g1[0:NB, 3712:3728]
        T8a = dn[2][:, :].rearrange("p (h k) -> p h k", h=8)
        kt2 = dn[3][:, 0:1024].rearrange("p (v g s) -> p v g s", v=2, g=2)
        blk = dn[3][:, 1024:1984].rearrange("p (v i n) -> p v i n", v=2, i=CMP_PAIRS)
        qaT, qbT = qbuf[:, 0:4, :], qbuf[:, 4:8, :]
        kaT, ksT, kwT = kvbuf[:, 0, :], kvbuf[:, 1, :], kvbuf[:, 2, :]
        lnp = qbuf[:, :, :].rearrange("p (a h) s -> p a (h s)", a=2)
        gu_v = [g[:, :].rearrange("p (k u f) -> p k u f", k=KD, u=2) for g in gu]
        dn_v = [d[:, :].rearrange("p (s n) -> p s n", n=D) for d in dn]
        o = 14848
        sg = W[:, o:o + 512].rearrange("p (b f) -> p b f", b=2)
        hh = W[:, o + 512:o + 1024].rearrange("p (b f) -> p b f", b=2)
        hT = W[:, o + 1024:o + 1536].rearrange("p (b s q) -> p b s q", b=2, s=2)
        w_in1 = W[:, 0:KD * W1_COLS].rearrange("p (k c) -> p k c", c=W1_COLS)
        kT1, kiT = kvbuf[:, 0, :], kvbuf[:, 1, :]
        v1 = kvbuf[:, 2, 0:TT * DH].rearrange("p (a d) -> p a d", a=2)
        g3 = gu[3]
        ts8 = g3[:, 0:2048].rearrange("p (b n) -> p b n", b=2)
        sel = g3[:, 2048:2560].rearrange("p (a k) -> p a k", a=2)
        qiT = g3[:, 2560:3072].rearrange("p (a k) -> p a k", a=2)
        relu = g3[:, 3072:4096].rearrange("p (b h k) -> p b h k", b=2, h=2)
        score = dn[3][:, 0:512].rearrange("p (a k) -> p a k", a=2)
        m8 = dn[3][:, 512:520]
        y = W[:, 0:2048].rearrange("p (a d) -> p a d", a=2)
        xgT = W[:, 2048:3072].rearrange("p (k q) -> p k q", k=KD)
        pick = W[:, 3072:3328].rearrange("p (a q) -> p a q", a=2)
        pickw = W[:, 3328:3584].rearrange("p (a q) -> p a q", a=2)
        pickwT = W[:, 3584:3840].rearrange("p (a q) -> p a q", a=2)
        ye = W[:, 3840:4864]
        rt = W[:, 4864:5888].rearrange("p (b n) -> p b n", b=4)
        wr = W[:, 5888:5952].rearrange("p (k e) -> p k e", e=8)
        ones = W[:, 5952:6080]

        ld_x, ld_cst, ld_vec, ld_pos, ld_w2, ld_w1, ld_flat = [sem(n) for n in (
            "ld_x", "ld_cst", "ld_vec", "ld_pos", "ld_w2", "ld_w1", "ld_flat")]
        ld_win = [sem(f"ld_win_part{i}") for i in range(4)]
        ld_wout, ld_win1, ld_lnp, ld_wr, rvec_stored = [sem(n) for n in (
            "ld_wout", "ld_win1", "ld_lnp", "ld_wr", "rvec_stored")]
        gu_loaded = [sem(f"gu_loaded{i}") for i in range(RING)]
        dn_loaded = [sem(f"dn_loaded{i}") for i in range(RING)]
        gu_used, dn_used = sem("gu_used"), sem("dn_used")
        front_pe, front_v, front_a = sem("front_pe"), sem("front_v"), sem("front_a")
        t8a_made, vec_step = sem("t8a_made"), sem("vec_step")
        blk_made, cmp_pe, cmp_v, cmp_a = sem("blk_made"), sem("cmp_pe"), sem("cmp_v"), sem("cmp_a")
        gates_exp, gates_made = sem("gates_exp"), sem("gates_made")
        at = [{n: sem(f"at{layer}_{n}") for n in (
            "scores", "biased", "negmax", "sink_arg", "exp", "sink_exp", "pt", "pt_v", "pt_a", "o", "o_out")} for layer in range(2)]
        lnx = [{n: sem(f"ln{i}_{n}") for n in ("var", "sd", "x")} for i in range(4)]
        tr = [{n: sem(f"tr{i}_{n}") for n in ("pe", "v", "a")} for i in range(5)]
        outp = [sem("outp0"), sem("outp1")]
        ffn_g0, ffn_silu, ffn_h, ffn_t, ffn_hT = [sem(n) for n in ("ffn_g0", "ffn_silu", "ffn_h", "ffn_t", "ffn_hT")]
        pr_pe, pr_v, pr_a = sem("pr_pe"), sem("pr_v"), sem("pr_a")
        idx_pe, idx_relu, idx_acc, idx_causal, idx_sel, ts_made = [sem(n) for n in (
            "idx_pe", "idx_relu", "idx_acc", "idx_causal", "idx_sel", "ts_made")]
        logits_pe, logits_v, route_exp, mask_made, rank_pe, route_done, moe_ones = [sem(n) for n in (
            "logits_pe", "logits_v", "route_exp", "mask_made", "rank_pe", "route_done", "moe_ones")]
        moe_silu, moe_h, moe_t, moe_hT = [sem(n) for n in ("moe_silu", "moe_h", "moe_t", "moe_hT")]
        pick_made, pickw_made, gathered, xgT_a, xgT_v = [sem(n) for n in (
            "pick_made", "pickw_made", "gathered", "xgT_a", "xgT_v")]
        pwT_pe, pwT_a, ye_a, ye_v, scattered, y_added = [sem(n) for n in (
            "pwT_pe", "pwT_a", "ye_a", "ye_v", "scattered", "y_added")]
        stored = sem("stored")

        front = [("rvec",), ("pos",)] + [("xT", j) for j in range(4)]
        front += [("colsA", qaT, j, QA0 + P * j, 0) for j in range(4)] + [("cols", kaT, KA0, 0)]
        front += [("colsA", qbT, j, QB0 + P * j, 1) for j in range(4)]
        front += [("dup", kv, g, 2 * kv + g, 2) for kv in range(2) for g in range(2)]
        front += [("cols", ksT, KS0, 3), ("cols", kwT, KW0, 3)]
        front += [("v", tt) for tt in range(TT)] + [("flip", j) for j in range(8)]
        NF = len(front)

        def v_jobs(n):
            return (n + 1) // 2

        def a_jobs(n):
            return n // 2

        units0 = [(kind, qt, g) for kind in "ASW" for qt in range(2) for g in range(2)]
        units1 = [("C", qt, c) for qt in range(2) for c in range(4)]

        def heads_of(u):
            kind, qt, g = u
            return [4 * g, 4 * g + 2, 4 * g + 1, 4 * g + 3] if kind == "C" else list(range(4 * g, 4 * g + 4))

        proj1 = [("q", m) for m in range(8)] + [("k",), ("qi", 0), ("qi", 1), ("ki",), ("v", 0), ("v", 1)]
        NP1 = len(proj1)
        CMP_DONE = {"z": 4, "gelu": 9, "kv": 12, "centred": 16, "coef": 20, "turned": 21, "taken0": 22, "mixed1": 25}

        block = ctx.enter_context(nc.Block())

        @block.sync
        def _(sp):
            w = t["l0_w_in"].rearrange("(k p) c -> p k c", p=P)
            sp.dma_start(cst[:, :], t["consts"]).then_inc(ld_cst, 16)
            sp.dma_start(x[:, :, :], t["x"][0].rearrange("(a p) d -> p a d", p=P)).then_inc(ld_x, 16)
            for i in range(4):
                if i == 2:
                    wc = t["l0_w_cmp"].rearrange("(k p) c -> p k c", p=P)
                    for n in range(2):
                        sp.dma_start(w_cmp[n], wc[:, 4 * n:4 * n + 4, :]).then_inc(ld_win[2], 16)
                    continue
                a, b = (0, QB0, 0, KS0)[i], (QB0, KS0, 0, W0_COLS)[i]
                sp.dma_start(w_in0[:, :, a:b], w[:, :, a:b]).then_inc(ld_win[i], 16)
                if i == 1:
                    sp.wait_ge(front_v, 1)
                    sp.dma_start(scratch, rvec).then_inc(rvec_stored, 16)
                    sp.wait_ge(rvec_stored, 16)
                    src = bass.AP(scratch.tensor, scratch.offset, [[1, P], [VEC, 16], [1, S]])
                    sp.dma_start(flat_T, src).then_inc(ld_flat, 16)
            sp.dma_start(w1k, t["l0_cmpk_w1"].rearrange("(i p) n -> p i n", p=P)).then_inc(ld_w1, 16)
            sp.dma_start(w1v, t["l0_cmpv_w1"].rearrange("(i p) n -> p i n", p=P)).then_inc(ld_w1, 16)

            def ring(gate_up, down, q, block_at):
                s = q % RING
                if not (isinstance(block_at, int) and block_at == 0 and q < RING):
                    used = NC * block_at + q - RING if q >= RING else NC * block_at - NC + last_use(s)
                    sp.wait_ge(gu_used, used + 1)
                sp.dma_start(gu[s][:, :], gate_up[q]).then_inc(gu_loaded[s], 16)
                if not (isinstance(block_at, int) and block_at == 0 and q < RING):
                    sp.wait_ge(dn_used, used + 1)
                sp.dma_start(dn[s][:, :], down[q]).then_inc(dn_loaded[s], 16)

            sp.wait_ge(tr[1]["pe"], 4)
            for q in range(NC):
                if q == RING:
                    sp.wait_ge(outp[0], 4)
                    w = t["l1_w_in"].rearrange("(k p) c -> p k c", p=P)
                    sp.dma_start(w_in1, w).then_inc(ld_win1, 16)
                ring(t["l0_ffn_gate_up"], t["l0_ffn_down"], q, 0)

            def expert(e, block_at, borrowed=False):
                def of(name):
                    return t[name][bass.ds(e, 1)] if not isinstance(e, int) else t[name][e:e + 1]
                gate_up = of("l1_exp_gate_up").rearrange("o c p n -> (o c) p n")
                down = of("l1_exp_down").rearrange("o c p n -> (o c) p n")
                for q in range(NC):
                    if borrowed and q == RING - 1:
                        sp.wait_ge(tr[3]["pe"], 4)
                    ring(gate_up, down, q, block_at)

            expert(0, 1, borrowed=True)
            with sp.Fori(1, NE) as e:
                expert(e, e + 1)

            sp.wait_ge(route_done, 1)
            over = sp.value_load(overflow[0:1, 0:1], min_val=0, max_val=S)
            with sp.If(over > CAP):
                with sp.Fori(0, NE) as e:
                    expert(e, e + 1 + NE)
            for tt in range(TT):
                sp.wait_ge(lnx[3]["x"], tt + 1)
                sp.dma_start(out[0].rearrange("(a p) d -> p a d", p=P)[:, tt, :], y[:, tt, :]).then_inc(stored, 16)
            sp.wait_ge(stored, 16 * TT)

        @block.gpsimd
        def _(pool):
            pool.wait_ge(front_v, v_jobs(NF))
            pool.wait_ge(front_a, a_jobs(NF))
            nc.gpsimd.affine_select(out=T8a[:, :, 0:P], in_=T8[:, 0:8, 0:P], pattern=[[0, 8], [1, P]],
                                    compare_op=ALU.is_gt, fill=INV_SCALE * NEG, base=0,
                                    channel_multiplier=-1).then_inc(t8a_made, 1)
            nc.gpsimd.tensor_copy(T8a[:, :, P:S], T8[:, 0:8, P:S]).then_inc(t8a_made, 1)
            for qt in range(TT):
                wk = P * (qt + 1)
                pool.wait_ge(idx_acc, 8 * (qt + 1))
                nc.gpsimd.affine_select(out=score[:, qt, 0:wk], in_=score[:, qt, 0:wk], pattern=[[-1, wk]],
                                        compare_op=ALU.is_ge, fill=NEG, base=P * qt,
                                        channel_multiplier=1).then_inc(idx_causal, 1)
            for i, (_, qt, c) in enumerate(units1):
                wk = P * (qt + 1)
                pool.wait_ge(idx_sel, qt + 1)
                if i >= 2:
                    pool.wait_ge(at[1]["biased"], 4 * (i - 1))
                dst = ts8[:, i % 2, 0:4 * wk].rearrange("p (h k) -> p h k", h=4)
                nc.gpsimd.tensor_tensor(dst, T8[:, 4 * c:4 * c + 4, S - wk:S], rep(sel[:, qt, 0:wk], 4),
                                        ALU.add).then_inc(ts_made, 1)

        def copy_front(eng, copy, j, ready):
            bank, job = ps[j % 8], front[j]
            eng.wait_ge(front_pe, j + 1)
            kind = job[0]
            if kind == "pos":
                copy(pos2, bank[:, 0:32].rearrange("p (v i) -> p v i", v=2)).then_inc(ready, 1)
            elif kind == "xT":
                copy(xT[:, 2 * job[1]:2 * job[1] + 2, :], bank[:, :].rearrange("p (k s) -> p k s", k=2))\
                    .then_inc(ready, 1)
            elif kind == "colsA":
                copy(job[1][:, job[2], :], bank[:, 0:S]).then_inc(ready, 1)
            elif kind == "cols":
                copy(job[1], bank[:, 0:S]).then_inc(ready, 1)
            elif kind == "dup":
                dst = kt2[:, job[1], job[2], :]
                copy(dst[0:DH, :], bank[0:DH, 0:S])
                copy(dst[DH:P, 0:S - 1], bank[DH:P, 1:S]).then_inc(ready, 1)
            elif kind == "v":
                tt = job[1]
                copy(va[:, tt, :], bank[:, 0:P])
                copy(vs[:, tt, :], bank[:, P:2 * P])
                copy(vw[:, tt, :], bank[:, 2 * P:3 * P])
                copy(gates[:, tt, :], bank[:, 3 * P:3 * P + 24]).then_inc(ready, 1)
            elif kind == "flip":
                copy(T8[:, 2 * job[1]:2 * job[1] + 2, :], bank[:, :].rearrange("p (h k) -> p h k", h=2))\
                    .then_inc(ready, 1)

        def copy_p1(eng, copy, j, ready):
            bank, job = ps[j % 8], proj1[j]
            eng.wait_ge(pr_pe, j + 1)
            if job[0] == "q":
                copy(qbuf[:, job[1], :], bank[:, 0:S]).then_inc(ready, 1)
            elif job[0] == "k":
                copy(kT1, bank[:, 0:S]).then_inc(ready, 1)
            elif job[0] == "qi":
                copy(qiT[:, job[1], :], bank[:, 0:S]).then_inc(ready, 1)
            elif job[0] == "ki":
                copy(kiT, bank[:, 0:S]).then_inc(ready, 1)
            else:
                copy(v1[:, job[1], :], bank[:, 0:DH])
                copy(wi[:, job[1], :], bank[:, DH:DH + 8]).then_inc(ready, 1)

        def copy_tr(eng, copy, i, j, ready):
            eng.wait_ge(tr[i]["pe"], j + 1)
            copy(xT[:, 2 * j:2 * j + 2, :], ps[j][:, :].rearrange("p (k s) -> p k s", k=2)).then_inc(ready, 1)

        def unit_p(u, i):
            wk = P * (u[1] + 1)
            return p_sb[:, i % 2, 0:4 * wk].rearrange("p (h k) -> p h k", h=4)

        @block.scalar
        def _(act):
            def copy(dst, src):
                return nc.scalar.copy(dst, src)

            act.dma_start(relb, t["rel_bias"]).then_inc(ld_vec, 16)
            act.dma_start(onehot, t["vecs"][:, 0:VEC]).then_inc(ld_vec, 16)
            act.dma_start(negvec, t["vecs"][0:16, VEC:2 * VEC]).then_inc(ld_vec, 16)
            act.dma_start(posrow[:, 0:P], t["l0_cmpk_pos"].rearrange("(i j) d -> i (j d)", j=2)).then_inc(ld_pos, 16)
            act.dma_start(posrow[:, P:2 * P], t["l0_cmpv_pos"].rearrange("(i j) d -> i (j d)", j=2))\
                .then_inc(ld_pos, 16)
            act.dma_start(w2k, t["l0_cmpk_w2"].rearrange("(f p) d -> p f d", p=P)).then_inc(ld_w2, 16)
            act.dma_start(w2v, t["l0_cmpv_w2"].rearrange("(f p) d -> p f d", p=P)).then_inc(ld_w2, 16)
            act.dma_start(sinks, to_all(t["l0_sinks"], 8)).then_inc(ld_w2, 16)
            for j in range(1, NF, 2):
                copy_front(act, copy, j, front_a)
            act.wait_ge(front_pe, NF)
            act.dma_start(w_out, t["l0_w_out"].rearrange("(k p) c -> p k c", p=P)).then_inc(ld_wout, 16)
            act.wait_ge(front_v, v_jobs(NF))
            act.wait_ge(front_a, a_jobs(NF))
            nc.scalar.activation(gates, gates, ACT.Exp, scale=-1.0).then_inc(gates_exp, 1)

            def exps(a, units, i):
                u = units[i]
                wk = P * (u[1] + 1)
                act.wait_ge(a["negmax"], i + 1)
                if i >= 2:
                    act.wait_ge(a["pt"], i - 1)
                    act.wait_ge(a["o_out"], i - 1)
                for h in range(4):
                    nc.scalar.activation(unit_p(u, i)[:, h, :], s_sb[:, i % 2, h, 0:wk], ACT.Exp,
                                         bias=neg[:, i % 2, h:h + 1],
                                         accum_out=sums[:, i % 2, h:h + 1]).then_inc(a["exp"], 1)
                if u[0] == "A":
                    act.wait_ge(a["sink_arg"], i + 1)
                    nc.scalar.activation(ske[:, i % 2, :], sk[:, i % 2, :], ACT.Exp).then_inc(a["sink_exp"], 1)

            def pt_copy(a, units, i):
                nk = units[i][1] + 1
                act.wait_ge(a["pt"], i + 1)
                if i >= 2:
                    act.wait_ge(a["o"], i - 1)
                src = ps[5][:, :].rearrange("p (h k q) -> p h k q", h=2, k=2)[:, :, 0:nk, :]
                copy(pT[:, i % 2, 2:4, 0:nk, :], src).then_inc(a["pt_a"], 1)

            for i in range(len(units0) + 1):
                if i < len(units0):
                    exps(at[0], units0, i)
                if i >= 1:
                    pt_copy(at[0], units0, i - 1)
                if i == 3:
                    act.wait_ge(cmp_v, CMP_DONE["z"])
                    nc.scalar.activation(gel[:, 3, :], gel[:, 2, :], ACT.Exp,
                                         scale=-2.0 * math.sqrt(2.0 / math.pi)).then_inc(cmp_a, 1)
                if i == 7:
                    act.wait_ge(cmp_v, CMP_DONE["centred"])
                    nc.scalar.activation(csc, csc, ACT.Exp, scale=SCALE).then_inc(cmp_a, 1)

            def layer_norm_sd(i):
                act.wait_ge(lnx[i]["var"], 1)
                nc.scalar.activation(rstd, rstd, ACT.Sqrt).then_inc(lnx[i]["sd"], 1)

            def ln_params(i, g, b):
                act.dma_start(lnp[:, 0, :], to_all(t[g], D)).then_inc(ld_lnp, 16)
                act.dma_start(lnp[:, 1, :], to_all(t[b], D)).then_inc(ld_lnp, 16)

            act.wait_ge(tr[1]["pe"], 4)
            ln_params(0, "l0_ln1_g", "l0_ln1_b")
            for j in (1, 3):
                copy_tr(act, copy, 1, j, tr[1]["a"])
            layer_norm_sd(0)
            for j in (1, 3):
                copy_tr(act, copy, 0, j, tr[0]["a"])
            act.wait_ge(lnx[0]["x"], TT)
            ln_params(1, "l0_ln2_g", "l0_ln2_b")

            def ffn_silu_step(q):
                c, tt = q // 2, q % 2
                act.wait_ge(gu_used if tt else ffn_g0, c + 1)
                if q >= 2:
                    act.wait_ge(ffn_h, q - 1)
                nc.scalar.activation(sg[:, q % 2, :], ps[q % 3][:, 0:FC], ACT.Silu).then_inc(ffn_silu, 1)

            def ffn_hT_step(q):
                c = q // 2
                act.wait_ge(ffn_t, q + 1)
                if c >= 1:
                    act.wait_ge(dn_used, c)
                copy(hT[:, q % 2, :, :], ps[3][:, 0:2 * P].rearrange("p (s q) -> p s q", s=2)).then_inc(ffn_hT, 1)

            for q in range(2 * NC + 1):
                if q < 2 * NC:
                    ffn_silu_step(q)
                if q >= 1:
                    ffn_hT_step(q - 1)
            layer_norm_sd(1)
            for j in (1, 3):
                copy_tr(act, copy, 2, j, tr[2]["a"])
            for j in range(1, NP1, 2):
                copy_p1(act, copy, j, pr_a)
            act.wait_ge(pr_pe, NP1)
            act.dma_start(w_out, t["l1_w_out"].rearrange("(k p) c -> p k c", p=P)).then_inc(ld_wout, 16)
            for qt in range(TT):
                wk = P * (qt + 1)
                for i in range(4):
                    n = 4 * qt + i
                    act.wait_ge(idx_pe, qt + 1)
                    if n >= 2:
                        act.wait_ge(idx_acc, 2 * (n - 1))
                    src = ps[i][:, :].rearrange("p (h k) -> p h k", h=2)[:, :, 0:wk]
                    nc.scalar.activation(relu[:, n % 2, :, 0:wk], src, ACT.Relu).then_inc(idx_relu, 1)
            for i in range(len(units1) + 1):
                if i < len(units1):
                    exps(at[1], units1, i)
                if i >= 1:
                    pt_copy(at[1], units1, i - 1)
            act.wait_ge(tr[3]["pe"], 4)
            ln_params(2, "l1_ln1_g", "l1_ln1_b")
            for j in (1, 3):
                copy_tr(act, copy, 3, j, tr[3]["a"])
            act.wait_ge(outp[1], 4)
            act.dma_start(wr, t["l1_router"].rearrange("(k p) e -> p k e", p=P)).then_inc(ld_wr, 16)
            layer_norm_sd(2)
            for j in (1, 3):
                copy_tr(act, copy, 4, j, tr[4]["a"])
            act.wait_ge(lnx[2]["x"], TT)
            ln_params(3, "l1_ln2_g", "l1_ln2_b")
            for tt in range(TT):
                act.wait_ge(logits_v, tt + 1)
                nc.scalar.activation(comb[:, tt, :], comb[:, tt, :], ACT.Exp,
                                     bias=rank[:, tt, 0:1]).then_inc(route_exp, 1)

            def moe_silu_step(e, q, nxt=False):
                base = NC * e + (NC if nxt else 0)
                act.wait_ge(gu_used, base + NC + q + 1)
                if q >= 2:
                    act.wait_ge(moe_h, base + q - 1)
                elif nxt:
                    act.wait_ge(moe_h, base)
                nc.scalar.activation(sg[:, q % 2, :], ps[q % 2][:, 0:FC], ACT.Silu).then_inc(moe_silu, 1)

            def moe_hT_step(e, q):
                act.wait_ge(moe_t, NC * e + q + 1)
                act.wait_ge(dn_used, NC * e + NC + (q - 1 if q >= 2 else 0))
                copy(hT[:, q % 2, :, :], ps[2][:, 0:2 * P].rearrange("p (s q) -> p s q", s=2)).then_inc(moe_hT, 1)

            def take_xgT(n):
                act.wait_ge(gathered, n)
                copy(xgT[:, 0:4, :], ps[6][:, :].rearrange("p (k q) -> p k q", k=4)).then_inc(xgT_a, 1)

            def expert(e, last):
                for q in range(1, NC):
                    moe_silu_step(e, q)
                    moe_hT_step(e, q - 1)
                    if q == 3:
                        act.wait_ge(pwT_pe, e + 1)
                        copy(pickwT, ps[3][:, 0:2 * P].rearrange("p (a q) -> p a q", a=2)).then_inc(pwT_a, 1)
                if not last:
                    take_xgT(e + 2)
                moe_hT_step(e, NC - 1)
                act.wait_ge(dn_used, NC * e + 2 * NC)
                copy(ye[:, 0:HALF], ps[4][:, :]).then_inc(ye_a, 1)
                if not last:
                    moe_silu_step(e, 0, nxt=True)

            def moe_pass(n):
                take_xgT(NE * n + 1)
                moe_silu_step(NE * n, 0)
                with act.Fori(NE * n, NE * n + NE - 1) as e:
                    expert(e, False)
                expert(NE * n + NE - 1, True)

            moe_pass(0)
            act.wait_ge(route_done, 1)
            over = act.value_load(overflow[0:1, 0:1], min_val=0, max_val=S)
            with act.If(over > CAP):
                moe_pass(1)
            layer_norm_sd(3)

        @block.vector
        def _(dve):
            steps = [0]

            def link(ins):
                steps[0] += 1
                ins.then_inc(vec_step, 1)
                dve.wait_ge(vec_step, steps[0])

            def copy(dst, src):
                return nc.vector.tensor_copy(dst, src)

            v = nc.vector
            link(v.memset(kcbd, 0.0))
            link(v.memset(csc, INV_SCALE * NEG))
            dve.wait_ge(front_pe, 1)
            dve.wait_ge(ld_vec, 48)
            v.scalar_tensor_tensor(out=rvec, in0=ps[0][0:16, 0:VEC], scalar=INV_SCALE, in1=negvec,
                                   op0=ALU.mult, op1=ALU.add).then_inc(front_v, 1)
            for j in range(2, NF, 2):
                copy_front(dve, copy, j, front_v)
            dve.wait_ge(front_v, v_jobs(NF))
            dve.wait_ge(front_a, a_jobs(NF))
            for kv in range(2):
                for half in range(2):
                    src = kt2[:, kv].rearrange("p g (n i two) -> p i g n two", i=8, two=2)
                    src = src[:, :, :, half:half + N_CMP, 0]
                    dst = blk[:, kv, 8 * half:8 * half + 8, :].rearrange("p i (g n) -> p i g n", g=2)
                    pos = rep_last(pos2[:, kv, 8 * half:8 * half + 8], N_CMP)
                    for g in range(2):
                        v.tensor_tensor(dst[:, :, g, :], src[:, :, g, :], pos, ALU.add)\
                            .then_inc(blk_made, 1)
            dve.wait_ge(gates_exp, 1)
            link(v.tensor_scalar(gates, gates, 1.0, None, ALU.add))
            v.reciprocal(gates, gates).then_inc(gates_made, 1)

            def bias_scores(a, units, i):
                u = units[i]
                kind, qt, g = u
                wk = P * (qt + 1)
                dve.wait_ge(a["scores"], i + 1)
                if i >= 2:
                    dve.wait_ge(a["exp"], 4 * (i - 1))
                if kind == "A" and i < 4:
                    if qt:
                        dve.wait_ge(t8a_made, 2)
                    if i == 0:
                        dve.wait_ge(ld_w2, 48)
                if kind == "C":
                    dve.wait_ge(ts_made, i + 1)
                for s, h in enumerate(heads_of(u)):
                    if kind == "A":
                        bias = T8a[:, h, :] if qt else T8[:, h, P:S]
                    elif kind == "C":
                        bias = ts8[:, i % 2, (h - 4 * g) * wk:(h - 4 * g + 1) * wk]
                    else:
                        bias = T8[:, 8 + h, S - wk:S]
                    src = ps[2 * (i % 2) + s // 2][:, (s % 2) * S:(s % 2) * S + wk]
                    init = sinks[:, h:h + 1] if kind == "A" else -3e38
                    v.tensor_tensor_reduce(out=s_sb[:, i % 2, s, 0:wk], in0=src, in1=bias, scale=SCALE, scalar=init,
                                           op0=ALU.add, op1=ALU.max, accum_out=mx[:, i % 2, s:s + 1])\
                        .then_inc(a["biased"], 1)
                dve.wait_ge(a["biased"], 4 * (i + 1))
                v.tensor_scalar(neg[:, i % 2, :], mx[:, i % 2, :], -1.0, None, ALU.mult).then_inc(a["negmax"], 1)
                if kind == "A":
                    dve.wait_ge(a["negmax"], i + 1)
                    if i >= 2:
                        dve.wait_ge(a["sink_exp"], i - 1)
                    v.tensor_tensor(sk[:, i % 2, :], sinks[:, 4 * g:4 * g + 4], neg[:, i % 2, :], ALU.add)\
                        .then_inc(a["sink_arg"], 1)

            def pt_copy(a, units, i):
                nk = units[i][1] + 1
                dve.wait_ge(a["pt"], i + 1)
                if i >= 2:
                    dve.wait_ge(a["o"], i - 1)
                src = ps[4][:, :].rearrange("p (h k q) -> p h k q", h=2, k=2)[:, :, 0:nk, :]
                copy(pT[:, i % 2, 0:2, 0:nk, :], src).then_inc(a["pt_v"], 1)

            def mix_out(a, units, i):
                kind, qt, g = units[i]
                dve.wait_ge(a["exp"], 4 * (i + 1))
                cf = coef[:, i % 2, :]
                if kind == "A":
                    dve.wait_ge(a["sink_exp"], i + 1)
                    link(v.tensor_tensor(cf, sums[:, i % 2, :], ske[:, i % 2, :], ALU.add))
                    link(v.reciprocal(cf, cf))
                else:
                    link(v.reciprocal(cf, sums[:, i % 2, :]))
                if kind in "SW":
                    dve.wait_ge(gates_made, 1)
                    br = 8 * (1 if kind == "S" else 2) + 4 * g
                    link(v.tensor_tensor(cf, cf, gates[:, qt, br:br + 4], ALU.mult))
                dve.wait_ge(a["o"], i + 1)
                src = ps[6][:, 0:S].rearrange("p (h d) -> p h d", h=4)
                cfb = rep_last(cf, DH)
                if kind == "C":
                    dst = mix[:, qt, S * g:S * (g + 1)].rearrange("p (r f d) -> p f r d", r=2, f=2)
                    v.tensor_tensor(dst, src.rearrange("p (f r) d -> p f r d", f=2),
                                    cfb.rearrange("p (f r) d -> p f r d", f=2), ALU.mult).then_inc(a["o_out"], 1)
                    return
                base = (0 if kind == "A" else HALF) + S * g
                dst = mix[:, qt, base:base + S].rearrange("p (h d) -> p h d", h=4)
                if kind == "W":
                    tmp = otmp.rearrange("p (h d) -> p h d", h=4)
                    v.tensor_tensor(tmp, src, cfb, ALU.mult).then_inc(a["o_out"], 1)
                    dve.wait_ge(a["o_out"], i + 1)
                    link(v.tensor_tensor(dst, dst, tmp, ALU.add))
                else:
                    v.tensor_tensor(dst, src, cfb, ALU.mult).then_inc(a["o_out"], 1)

            cn = [0]

            def cstep(ins):
                cn[0] += 1
                ins.then_inc(cmp_v, 1)
                dve.wait_ge(cmp_v, cn[0])

            def cmp_step(k):
                if k == 0:
                    dve.wait_ge(cmp_pe, 1)
                    cstep(copy(gel[:, 0, :], ps[7][:, 0:120]))
                    cstep(v.tensor_tensor(gel[:, 1, :], gel[:, 0, :], gel[:, 0, :], ALU.mult))
                    cstep(v.tensor_scalar(gel[:, 2, :], gel[:, 1, :], 0.044715, 1.0, ALU.mult, ALU.add))
                    cstep(v.tensor_tensor(gel[:, 2, :], gel[:, 2, :], gel[:, 0, :], ALU.mult))
                elif k == 1:
                    dve.wait_ge(cmp_a, 1)
                    cstep(v.tensor_scalar(gel[:, 4, :], gel[:, 3, :], 1.0, None, ALU.add))
                    cstep(v.reciprocal(gel[:, 4, :], gel[:, 4, :]))
                    cstep(v.tensor_tensor(gel[:, 5, :], gel[:, 4, :], gel[:, 0, :], ALU.mult))
                    src = gel[:, 5, 60:120].rearrange("p (f n) -> p f n", f=2)
                    dst = hidv.rearrange("p f (r n) -> p f r n", r=4)
                    for f in range(2):
                        cstep(copy(dst[:, f], rep(src[:, f, :], 4)))
                elif k == 2:
                    dve.wait_ge(cmp_pe, 2)
                    cstep(copy(kcbd[0:DH, 0:N_CMP], ps[7][0:DH, 0:N_CMP]))
                    cstep(copy(kcbd[DH:P, N_CMP:2 * N_CMP], ps[7][DH:P, N_CMP:2 * N_CMP]))
                    cstep(v.tensor_tensor(vcbd.rearrange("p (h d) -> p h d", h=8), rep(ps[7][0:120, DH:2 * DH], 8),
                                          rep_last(bdmask[0:120, :], DH), ALU.mult))
                elif k == 3:
                    dve.wait_ge(cmp_pe, 3)
                    sc = csc.rearrange("p (a j g n) -> p a j g n", a=2, j=4, g=2)
                    src = ps[7][:, 0:240].rearrange("p (a j g n) -> p a j g n", a=2, j=4, g=2)
                    first = 2 * 16 - 1
                    bias = T8[:, 8:16, :].rearrange("p (g j) k -> p j g k", g=2)
                    cstep(v.tensor_tensor(sc[:, 0, :, :, 0:7], src[:, 0, :, :, 0:7],
                                          bias[:, :, :, P + first::16], ALU.add))
                    cstep(v.tensor_tensor(sc[:, 1], src[:, 1], bias[:, :, :, first::16], ALU.add))
                    sc3 = csc.rearrange("p (h n) -> p h n", n=N_CMP)
                    cstep(v.tensor_reduce(cmp_m, sc3, AX.X, ALU.max))
                    cstep(v.tensor_tensor(sc3, sc3, rep_last(cmp_m, N_CMP), ALU.subtract))
                elif k == 4:
                    dve.wait_ge(cmp_a, 2)
                    sc3 = csc.rearrange("p (h n) -> p h n", n=N_CMP)
                    cstep(v.tensor_reduce(cmp_s, sc3, AX.X, ALU.add))
                    cstep(v.reciprocal(cmp_c, cmp_s))
                    gate = gates[:, :, 0:8].rearrange("p a (g j) -> p a j g", g=2)
                    c4 = cmp_c.rearrange("p (a j g) -> p a j g", a=2, j=4)
                    dve.wait_ge(gates_made, 1)
                    cstep(v.tensor_tensor(c4, c4, gate, ALU.mult))
                    cstep(v.tensor_scalar(cmp_c[:, 0:8], cmp_c[:, 0:8], rowvalid, None, ALU.mult))
                elif k == 5:
                    dve.wait_ge(cmp_pe, 4)
                    cstep(copy(cPT, ps[7][0:120, 0:2 * P].rearrange("p (a q) -> p a q", a=2)))
                else:
                    qt = k - 6
                    dve.wait_ge(cmp_pe, 5 + qt)
                    cstep(v.tensor_tensor(ctmp.rearrange("p (h d) -> p h d", h=8),
                                          ps[7][:, :].rearrange("p (h d) -> p h d", h=8),
                                          rep_last(cmp_c[:, 8 * qt:8 * qt + 8], DH), ALU.mult))
                    dst = mix[:, qt, HALF:D].rearrange("p (g j d) -> p j g d", g=2, j=4)
                    cstep(v.tensor_tensor(dst, dst, ctmp.rearrange("p (j g d) -> p j g d", j=4, g=2), ALU.add))

            CMP_AT = {2: 0, 4: 1, 5: 2, 6: 3, 8: 4, 10: 5, 12: 6, 13: 7}
            n0 = len(units0)
            for i in range(n0 + 2):
                if i < n0:
                    bias_scores(at[0], units0, i)
                if 1 <= i <= n0:
                    pt_copy(at[0], units0, i - 1)
                if i >= 2:
                    mix_out(at[0], units0, i - 2)
                if i in CMP_AT:
                    cmp_step(CMP_AT[i])

            def out_add(i, sems, need, banks=4):
                for tt in range(TT):
                    for half in range(2):
                        n = 2 * tt + half
                        dve.wait_ge(sems, need(n))
                        dst = x[:, tt, half * HALF:(half + 1) * HALF]
                        link(v.scalar_tensor_tensor(out=dst, in0=dst, scalar=ALPHA, in1=ps[banks + n][:, :],
                                                    op0=ALU.mult, op1=ALU.add))

            def layer_norm(i, z):
                for tt in range(TT):
                    for half in range(2):
                        link(v.bn_stats(bnst[:, tt, half, :], z[:, tt, half * HALF:(half + 1) * HALF]))
                    link(v.bn_aggr(mv[:, tt, :], bnst[:, tt, :, :]))
                v.tensor_scalar(rstd, mv[:, :, 1], EPS, None, ALU.add).then_inc(lnx[i]["var"], 1)
                dve.wait_ge(lnx[i]["sd"], 1)
                link(v.reciprocal(rstd, rstd))
                dve.wait_ge(ld_lnp, 32 * (i + 1))
                for tt in range(TT):
                    link(v.tensor_scalar(z[:, tt, :], z[:, tt, :], mv[:, tt, 0:1], rstd[:, tt:tt + 1],
                                         ALU.subtract, ALU.mult))
                    link(v.tensor_tensor(z[:, tt, :], z[:, tt, :], lnp[:, 0, :], ALU.mult))
                    v.tensor_tensor(z[:, tt, :], z[:, tt, :], lnp[:, 1, :], ALU.add).then_inc(lnx[i]["x"], 1)

            for j in (0, 2):
                copy_tr(dve, copy, 1, j, tr[1]["v"])
            out_add(0, outp[0], lambda n: n + 1)
            layer_norm(0, x)
            for j in (0, 2):
                copy_tr(dve, copy, 0, j, tr[0]["v"])

            for q in range(2 * NC):
                dve.wait_ge(ffn_silu, q + 1)
                if q >= 2:
                    dve.wait_ge(ffn_t, q - 1)
                v.tensor_tensor(hh[:, q % 2, :], sg[:, q % 2, :], ps[q % 3][:, FC:2 * FC], ALU.mult)\
                    .then_inc(ffn_h, 1)
            dve.wait_ge(lnx[0]["x"], TT)
            out_add(1, dn_used, lambda n: NC)
            layer_norm(1, x)
            for j in (0, 2):
                copy_tr(dve, copy, 2, j, tr[2]["v"])
            for j in range(0, NP1, 2):
                copy_p1(dve, copy, j, pr_v)
            dve.wait_ge(pr_v, v_jobs(NP1))
            dve.wait_ge(pr_a, a_jobs(NP1))
            for qt in range(TT):
                wk = P * (qt + 1)
                sc = score[:, qt, 0:wk]
                for i in range(4):
                    n = 4 * qt + i
                    dve.wait_ge(idx_relu, n + 1)
                    for r in range(2):
                        h = i + 4 * r
                        src, w = relu[:, n % 2, r, 0:wk], wi[:, qt, h:h + 1]
                        if i == 0 and r == 0:
                            ins = v.tensor_scalar(sc, src, w, None, ALU.mult)
                        else:
                            ins = v.scalar_tensor_tensor(out=sc, in0=src, scalar=w, in1=sc, op0=ALU.mult,
                                                         op1=ALU.add)
                        ins.then_inc(idx_acc, 1)
                        dve.wait_ge(idx_acc, 2 * n + r + 1)
            for qt in range(TT):
                wk = P * (qt + 1)
                sc = score[:, qt, 0:wk]
                dve.wait_ge(idx_causal, qt + 1)
                for _ in range(TOPK // 8):
                    link(v.max(m8, sc))
                    link(v.match_replace(sc, m8, sc, TAKEN))
                v.tensor_scalar(sel[:, qt, 0:wk], sc, -2e38, INV_SCALE * NEG, ALU.is_gt, ALU.mult).then_inc(idx_sel, 1)
            n1 = len(units1)
            for i in range(n1 + 2):
                if i < n1:
                    bias_scores(at[1], units1, i)
                if 1 <= i <= n1:
                    pt_copy(at[1], units1, i - 1)
                if i >= 2:
                    mix_out(at[1], units1, i - 2)
            for j in (0, 2):
                copy_tr(dve, copy, 3, j, tr[3]["v"])
            dve.wait_ge(lnx[1]["x"], TT)
            out_add(2, outp[1], lambda n: n + 1)
            layer_norm(2, x)
            for j in (0, 2):
                copy_tr(dve, copy, 4, j, tr[4]["v"])
            dve.wait_ge(outp[1], 4)
            dve.wait_ge(lnx[2]["x"], TT)
            v.memset(ones, 1.0).then_inc(moe_ones, 1)
            for tt in range(TT):
                for half in range(2):
                    cols = slice(half * HALF, (half + 1) * HALF)
                    v.tensor_scalar(y[:, tt, cols], x[:, tt, cols], ALPHA, None, ALU.mult).then_inc(y_added, 1)
            dve.wait_ge(logits_pe, 1)
            link(copy(mask, ps[4][:, 0:16].rearrange("p (a e) -> p a e", a=2)))
            for tt in range(TT):
                lg = mask[:, tt, :]
                other, own = rep(lg, 8), rep_last(lg, 8)
                r8 = rt[:, 2 * tt, 0:64].rearrange("p (a b) -> p a b", b=8)
                e8 = rt[:, 2 * tt + 1, 0:64].rearrange("p (a b) -> p a b", b=8)
                link(v.tensor_tensor(r8, other, own, ALU.is_gt))
                link(v.tensor_tensor(e8, other, own, ALU.is_equal))
                link(v.tensor_tensor(e8, e8, tri8, ALU.mult))
                link(v.tensor_tensor(r8, r8, e8, ALU.add))
                link(v.tensor_reduce(rank[:, tt, 0:1], lg, AX.X, ALU.max))
                link(v.tensor_scalar(rank[:, tt, 0:1], rank[:, tt, 0:1], -1.0, None, ALU.mult))
                copy(comb[:, tt, :], lg).then_inc(logits_v, 1)
                dve.wait_ge(route_exp, tt + 1)
                link(v.tensor_reduce(rank[:, tt, :], r8, AX.X, ALU.add))
                link(v.tensor_scalar(mask[:, tt, :], rank[:, tt, :], 1.5, None, ALU.is_lt))
                link(v.tensor_tensor(comb[:, tt, :], comb[:, tt, :], mask[:, tt, :], ALU.mult))
                s1 = rt[:, 2 * tt, 64:65]
                link(v.tensor_reduce(s1, comb[:, tt, :], AX.X, ALU.add))
                link(v.reciprocal(s1, s1))
                v.tensor_scalar(comb[:, tt, :], comb[:, tt, :], s1, None, ALU.mult).then_inc(mask_made, 1)
            dve.wait_ge(mask_made, 2)
            dve.wait_ge(rank_pe, 1)
            link(copy(rank, ps[5][:, 0:16].rearrange("p (a e) -> p a e", a=2)))
            cnt = rt[:, 0, 66:67]
            link(v.tensor_reduce(cnt, ps[5][:, 16:24], AX.X, ALU.max))
            copy(overflow[:, :], cnt).then_inc(route_done, 1)

            def make_picks(dst, scale_by, e, base, ready, count):
                for tt in range(TT):
                    ex = e if isinstance(e, int) else None
                    col = slice(ex, ex + 1) if ex is not None else bass.ds(e, 1)
                    v.tensor_scalar(dst[:, tt, :], iota[:, base:base + P], rank[:, tt, col], scale_by[:, tt, col],
                                    ALU.is_equal, ALU.mult).then_inc(ready, 1)

            def moe_h_step(e, q, nxt=False):
                base = NC * e + (NC if nxt else 0)
                dve.wait_ge(moe_silu, base + q + 1)
                if q >= 2:
                    dve.wait_ge(moe_t, base + q - 1)
                elif nxt:
                    dve.wait_ge(moe_t, base)
                v.tensor_tensor(hh[:, q % 2, :], sg[:, q % 2, :], ps[q % 2][:, FC:2 * FC], ALU.mult)\
                    .then_inc(moe_h, 1)

            def take_xgT(n):
                dve.wait_ge(gathered, n)
                copy(xgT[:, 4:8, :], ps[7][:, :].rearrange("p (k q) -> p k q", k=4)).then_inc(xgT_v, 1)

            def add_scattered(e):
                for n in range(4):
                    tt, half = n // 2, n % 2
                    dve.wait_ge(scattered, 4 * e + n + 1)
                    dst = y[:, tt, half * HALF:(half + 1) * HALF]
                    v.tensor_tensor(dst, dst, ps[6 + half][:, :], ALU.add).then_inc(y_added, 1)

            def expert(e, ex, base, last):
                for q in range(1, NC):
                    moe_h_step(e, q)
                    if q == 1:
                        make_picks(pickw, comb, ex, base, pickw_made, None)
                    if q == 5 and not last:
                        dve.wait_ge(gathered, e + 1)
                        make_picks(pick, mask, ex + 1, base, pick_made, None)
                if not last:
                    take_xgT(e + 2)
                dve.wait_ge(dn_used, NC * e + 2 * NC)
                copy(ye[:, HALF:D], ps[5][:, :]).then_inc(ye_v, 1)
                if not last:
                    moe_h_step(e, 0, nxt=True)
                dve.wait_ge(y_added, 4 * e + 4)
                add_scattered(e)

            def moe_pass(n):
                base = P * n
                make_picks(pick, mask, 0, base, pick_made, None)
                take_xgT(NE * n + 1)
                moe_h_step(NE * n, 0)
                with dve.Fori(0, NE - 1) as e:
                    expert(e + NE * n if n else e, e, base, False)
                expert(NE * n + NE - 1, NE - 1, base, True)
                dve.wait_ge(y_added, 4 * NE * (n + 1) + 4)

            dve.wait_ge(vec_step, steps[0])
            moe_pass(0)
            dve.wait_ge(route_done, 1)
            over = dve.value_load(overflow[0:1, 0:1], min_val=0, max_val=S)
            with dve.If(over > CAP):
                moe_pass(1)
            layer_norm(3, y)

        @block.tensor
        def _(pe):
            mm = nc.tensor.matmul

            def over_k(dst, lhsT, rhs):
                for k in range(KD):
                    last = mm(dst, lhsT(k), rhs(k), start=(k == 0), stop=(k == KD - 1))
                return last

            def transposes(i, src):
                for j in range(4):
                    for kk in range(2):
                        for tt in range(TT):
                            n = 2 * kk + tt
                            last = nc.tensor.transpose(ps[j][:, n * P:(n + 1) * P],
                                                       src[:, tt, (2 * j + kk) * P:(2 * j + kk + 1) * P], ident)
                    last.then_inc(tr[i]["pe"], 1)

            pe.wait_ge(ld_cst, 16)
            seen = set()
            for j, job in enumerate(front):
                kind, bank = job[0], ps[j % 8]
                if j >= 8:
                    pe.wait_ge(front_v if j % 2 == 0 else front_a, (j - 8) // 2 + 1)
                if kind in ("colsA", "cols", "dup", "v") and "xT" not in seen:
                    seen.add("xT")
                    pe.wait_ge(front_v, v_jobs(6))
                    pe.wait_ge(front_a, a_jobs(6))
                piece = job[-1] if kind in ("colsA", "cols", "dup") else 3 if kind == "v" else None
                if piece is not None and piece not in seen:
                    seen.add(piece)
                    pe.wait_ge(ld_win[piece], 32 if piece == 2 else 16)
                if kind == "rvec":
                    pe.wait_ge(ld_vec, 48)
                    last = mm(bank[0:16, 0:VEC], relb, onehot, start=True, stop=True)
                elif kind == "pos":
                    pe.wait_ge(ld_pos, 32)
                    for n in range(2):
                        last = nc.tensor.transpose(bank[:, 16 * n:16 * n + 16], posrow[:, P * n:P * n + P],
                                                   ident[0:16, 0:16])
                elif kind == "xT":
                    pe.wait_ge(ld_x, 16)
                    for kk in range(2):
                        for tt in range(TT):
                            n = 2 * kk + tt
                            last = nc.tensor.transpose(bank[:, n * P:(n + 1) * P],
                                                       x[:, tt, (2 * job[1] + kk) * P:(2 * job[1] + kk + 1) * P],
                                                       ident)
                elif kind in ("colsA", "cols"):
                    c = job[-2]
                    last = over_k(bank[:, 0:S], lambda k: w_in0[:, k, c:c + P], lambda k: xT[:, k, :])
                elif kind == "dup":
                    c = P * job[3]
                    last = over_k(bank[:, 0:S], lambda k: w_cmp[k // 4][:, k % 4, c:c + P], lambda k: xT[:, k, :])
                elif kind == "v":
                    tt = job[1]
                    for at_col, c, n in ((0, VA0, P), (P, VS0, P), (2 * P, VW0, P + 24)):
                        last = over_k(bank[:, at_col:at_col + n], lambda k: xT[:, k, tt * P:(tt + 1) * P],
                                      lambda k: w_in0[:, k, c:c + n])
                elif kind == "flip":
                    pe.wait_ge(ld_flat, 16)
                    last = mm(bank[:, :], flip, flat_T[:, 2 * job[1]:2 * job[1] + 2, :], start=True, stop=True)
                last.then_inc(front_pe, 1)
            pe.wait_ge(front_v, v_jobs(NF))
            pe.wait_ge(front_a, a_jobs(NF))

            def scores(a, units, i):
                kind, qt, g = units[i]
                wk = P * (qt + 1)
                if i >= 2:
                    pe.wait_ge(a["biased"], 4 * (i - 1))
                order = (0, 2, 1, 3) if kind == "C" else range(4)
                for s in order:
                    h = heads_of(units[i])[s]
                    if kind == "C":
                        r = slice(DH * (h % 2), DH * (h % 2) + DH)
                        q, k = qbuf[r, h // 2, qt * P:(qt + 1) * P], kT1[r, 0:wk]
                    else:
                        r = slice(DH * g, DH * g + DH)
                        q = (qaT if kind == "A" else qbT)[r, s, qt * P:(qt + 1) * P]
                        k = {"A": kaT, "S": ksT, "W": kwT}[kind][r, 0:wk]
                    last = mm(ps[2 * (i % 2) + s // 2][:, (s % 2) * S:(s % 2) * S + wk], q, k, start=True, stop=True)
                last.then_inc(a["scores"], 1)

            def turn(a, units, i):
                u = units[i]
                pe.wait_ge(a["exp"], 4 * (i + 1))
                if i >= 1:
                    pe.wait_ge(a["pt_v"], i)
                    pe.wait_ge(a["pt_a"], i)
                for s in range(4):
                    for kt in range(u[1] + 1):
                        n = 2 * (s % 2) + kt
                        last = nc.tensor.transpose(ps[4 + s // 2][:, n * P:(n + 1) * P],
                                                   unit_p(u, i)[:, s, kt * P:(kt + 1) * P], ident)
                last.then_inc(a["pt"], 1)

            def sum_values(a, units, i):
                kind, qt, g = units[i]
                pe.wait_ge(a["pt_v"], i + 1)
                pe.wait_ge(a["pt_a"], i + 1)
                if i >= 1:
                    pe.wait_ge(a["o_out"], i)
                for s in range(4):
                    for kt in range(qt + 1):
                        vv = v1[:, kt, :] if kind == "C" else \
                            {"A": va, "S": vs, "W": vw}[kind][:, kt, DH * g:DH * g + DH]
                        last = mm(ps[6][:, s * DH:(s + 1) * DH], pT[:, i % 2, s, kt, :], vv,
                                  start=(kt == 0), stop=(kt == qt))
                last.then_inc(a["o"], 1)

            def compressed(k):
                if k == 0:
                    pe.wait_ge(blk_made, 8)
                    pe.wait_ge(ld_w1, 32)
                    for kv in range(2):
                        for f in range(2):
                            n = 30 * (2 * kv + f)
                            for i in range(CMP_PAIRS):
                                last = mm(ps[7][:, n:n + 30], (w1k, w1v)[kv][:, i, f * P:(f + 1) * P],
                                          blk[:, kv, i, :], start=(i == 0), stop=(i == CMP_PAIRS - 1))
                elif k == 1:
                    pe.wait_ge(cmp_v, CMP_DONE["gelu"])
                    pe.wait_ge(ld_w2, 48)
                    hid = gel[:, 5, :].rearrange("p (v f n) -> p v f n", v=2, f=2)
                    for f in range(2):
                        mm(ps[7][:, 0:30], w2k[:, f, :], hid[:, 0, f, :], start=(f == 0), stop=(f == 1))
                    for f in range(2):
                        last = mm(ps[7][0:120, DH:2 * DH], hidv[:, f, :], w2v[:, f, :],
                                  start=(f == 0), stop=(f == 1))
                elif k == 2:
                    pe.wait_ge(cmp_v, CMP_DONE["kv"])
                    for qt in range(TT):
                        for j in range(4):
                            n = 120 * qt + 30 * j
                            last = mm(ps[7][:, n:n + 30], qbT[:, j, qt * P:(qt + 1) * P], kcbd, start=True, stop=True)
                elif k == 3:
                    pe.wait_ge(cmp_a, 2)
                    for qt in range(TT):
                        last = nc.tensor.transpose(ps[7][0:120, qt * P:(qt + 1) * P], csc[:, 120 * qt:120 * qt + 120],
                                                   ident)
                else:
                    qt = k - 4
                    pe.wait_ge(cmp_v, CMP_DONE["taken0" if qt else "turned"])
                    last = mm(ps[7][:, :], cPT[:, qt, :], vcbd, start=True, stop=True)
                last.then_inc(cmp_pe, 1)

            CMP_AT = {1: 0, 4: 1, 5: 2, 8: 3, 11: 4, 12: 5}
            n0 = len(units0)
            for i in range(n0 + 2):
                if i < n0:
                    scores(at[0], units0, i)
                if 1 <= i <= n0:
                    turn(at[0], units0, i - 1)
                if i >= 2:
                    sum_values(at[0], units0, i - 2)
                if i in CMP_AT:
                    compressed(CMP_AT[i])

            def out_proj(i):
                pe.wait_ge(tr[2 * i + 1]["v"], 2)
                pe.wait_ge(tr[2 * i + 1]["a"], 2)
                pe.wait_ge(ld_wout, 16 * (i + 1))
                for tt in range(TT):
                    for half in range(2):
                        over_k(ps[4 + 2 * tt + half][:, :], lambda k: xT[:, k, tt * P:(tt + 1) * P],
                               lambda k: w_out[:, k, half * HALF:(half + 1) * HALF]).then_inc(outp[i], 1)

            pe.wait_ge(cmp_v, CMP_DONE["mixed1"])
            transposes(1, mix)
            out_proj(0)

            pe.wait_ge(lnx[0]["x"], TT)
            transposes(0, x)
            pe.wait_ge(tr[0]["v"], 2)
            pe.wait_ge(tr[0]["a"], 2)

            def loaded(sems, block_at, q):
                s = q % RING
                pe.wait_ge(sems[s], 16 * (slot_loads(s) * block_at + q // RING + 1))

            def ffn_up(q):
                c, tt = q // 2, q % 2
                if tt == 0:
                    loaded(gu_loaded, 0, c)
                if q >= 3:
                    pe.wait_ge(ffn_h, q - 2)
                over_k(ps[q % 3][:, :], lambda k: xT[:, k, tt * P:(tt + 1) * P],
                       lambda k: gu_v[c % RING][:, k, :, :]).then_inc(gu_used if tt else ffn_g0, 1)

            def ffn_turn(q):
                pe.wait_ge(ffn_h, q + 1)
                if q >= 1:
                    pe.wait_ge(ffn_hT, q)
                for s in range(2):
                    last = nc.tensor.transpose(ps[3][:, s * P:(s + 1) * P], hh[:, q % 2, s * P:(s + 1) * P], ident)
                last.then_inc(ffn_t, 1)

            def ffn_down(q):
                c, tt = q // 2, q % 2
                pe.wait_ge(ffn_hT, q + 1)
                if tt == 0:
                    loaded(dn_loaded, 0, c)
                for s in range(2):
                    for half in range(2):
                        last = mm(ps[4 + 2 * tt + half][:, :], hT[:, q % 2, s, :],
                                  dn_v[c % RING][:, s, half * HALF:(half + 1) * HALF],
                                  start=(c == 0 and s == 0), stop=(c == NC - 1 and s == 1))
                if tt:
                    last.then_inc(dn_used, 1)

            for q in range(2 * NC + 2):
                if q < 2 * NC:
                    ffn_up(q)
                if 1 <= q <= 2 * NC:
                    ffn_turn(q - 1)
                if q >= 2:
                    ffn_down(q - 2)

            pe.wait_ge(lnx[1]["x"], TT)
            transposes(2, x)
            pe.wait_ge(tr[2]["v"], 2)
            pe.wait_ge(tr[2]["a"], 2)
            pe.wait_ge(ld_win1, 16)
            for j, job in enumerate(proj1):
                bank = ps[j % 8]
                if j >= 8:
                    pe.wait_ge(pr_v if j % 2 == 0 else pr_a, (j - 8) // 2 + 1)
                if job[0] == "v":
                    tt = job[1]
                    for at_col, c, n in ((0, V1, DH), (DH, WI1, 8)):
                        last = over_k(bank[:, at_col:at_col + n], lambda k: xT[:, k, tt * P:(tt + 1) * P],
                                      lambda k: w_in1[:, k, c:c + n])
                else:
                    if job[0] == "q":
                        def lhsT(k):
                            return w_in1[:, k, job[1] * P:(job[1] + 1) * P]
                    elif job[0] == "k":
                        def lhsT(k):
                            return w_in1[:, k, K1:K1 + P]
                    elif job[0] == "qi":
                        def lhsT(k):
                            return w_in1[:, k, QI1 + job[1] * P:QI1 + (job[1] + 1) * P]
                    else:
                        def lhsT(k):
                            return w_in1[:, k, KI1:KI1 + P]
                    last = over_k(bank[:, 0:S], lhsT, lambda k: xT[:, k, :])
                last.then_inc(pr_pe, 1)
            pe.wait_ge(pr_v, v_jobs(NP1))
            pe.wait_ge(pr_a, a_jobs(NP1))
            for qt in range(TT):
                wk = P * (qt + 1)
                if qt:
                    pe.wait_ge(idx_relu, 4)
                for h in range(8):
                    r = slice(32 * (h % 4), 32 * (h % 4) + 32)
                    last = mm(ps[h % 4][:, (h // 4) * S:(h // 4) * S + wk], qiT[r, h // 4, qt * P:(qt + 1) * P],
                              kiT[r, 0:wk], start=True, stop=True)
                last.then_inc(idx_pe, 1)
            pe.wait_ge(idx_relu, 8)
            n1 = len(units1)
            for i in range(n1 + 2):
                if i < n1:
                    scores(at[1], units1, i)
                if 1 <= i <= n1:
                    turn(at[1], units1, i - 1)
                if i >= 2:
                    sum_values(at[1], units1, i - 2)
            pe.wait_ge(at[1]["o_out"], n1)
            transposes(3, mix)
            out_proj(1)

            pe.wait_ge(lnx[2]["x"], TT)
            transposes(4, x)
            pe.wait_ge(tr[4]["v"], 2)
            pe.wait_ge(tr[4]["a"], 2)
            pe.wait_ge(ld_wr, 16)
            for tt in range(TT):
                last = over_k(ps[4][:, 8 * tt:8 * tt + 8], lambda k: xT[:, k, tt * P:(tt + 1) * P],
                              lambda k: wr[:, k, :])
            last.then_inc(logits_pe, 1)
            pe.wait_ge(mask_made, 2)
            pe.wait_ge(moe_ones, 1)
            mm(ps[5][:, 0:8], upper, mask[:, 0, :], start=True, stop=True)
            mm(ps[5][:, 8:16], ones, mask[:, 0, :], start=True, stop=False)
            mm(ps[5][:, 8:16], upper, mask[:, 1, :], start=False, stop=True)
            mm(ps[5][:, 16:24], ones, mask[:, 0, :], start=True, stop=False)
            mm(ps[5][:, 16:24], ones, mask[:, 1, :], start=False, stop=True).then_inc(rank_pe, 1)

            def moe_up(e, q):
                loaded(gu_loaded, e + 1, q)
                if q >= 2:
                    pe.wait_ge(moe_h, NC * e + q - 1)
                over_k(ps[q % 2][:, :], lambda k: xgT[:, k, :],
                       lambda k: gu_v[q % RING][:, k, :, :]).then_inc(gu_used, 1)

            def moe_turn(e, q):
                pe.wait_ge(moe_h, NC * e + q + 1)
                if q:
                    pe.wait_ge(moe_hT, NC * e + q)
                for s in range(2):
                    last = nc.tensor.transpose(ps[2][:, s * P:(s + 1) * P], hh[:, q % 2, s * P:(s + 1) * P], ident)
                last.then_inc(moe_t, 1)

            def moe_down(e, q):
                pe.wait_ge(moe_hT, NC * e + q + 1)
                loaded(dn_loaded, e + 1, q)
                for s in range(2):
                    for half in range(2):
                        last = mm(ps[4 + half][:, :], hT[:, q % 2, s, :],
                                  dn_v[q % RING][:, s, half * HALF:(half + 1) * HALF],
                                  start=(q == 0 and s == 0), stop=(q == NC - 1 and s == 1))
                last.then_inc(dn_used, 1)

            def gather(e):
                pe.wait_ge(pick_made, 2 * e + 2)
                for k in range(KD):
                    for tt in range(TT):
                        last = mm(ps[6 + k // 4][:, (k % 4) * P:(k % 4 + 1) * P], x[:, tt, k * P:(k + 1) * P],
                                  pick[:, tt, :], start=(tt == 0), stop=(tt == TT - 1))
                last.then_inc(gathered, 1)

            def turn_picks(e):
                pe.wait_ge(pickw_made, 2 * e + 2)
                for tt in range(TT):
                    last = nc.tensor.transpose(ps[3][:, tt * P:(tt + 1) * P], pickw[:, tt, :], ident)
                last.then_inc(pwT_pe, 1)

            def scatter(e):
                pe.wait_ge(y_added, 4 * e + 4)
                pe.wait_ge(ye_a, e + 1)
                pe.wait_ge(ye_v, e + 1)
                pe.wait_ge(pwT_a, e + 1)
                for n in range(4):
                    tt, half = n // 2, n % 2
                    if n >= 2:
                        pe.wait_ge(y_added, 4 * e + n + 3)
                    mm(ps[6 + half][:, :], pickwT[:, tt, :], ye[:, half * HALF:(half + 1) * HALF],
                       start=True, stop=True).then_inc(scattered, 1)

            def expert(e, last):
                for q in range(1, NC):
                    moe_up(e, q)
                    moe_turn(e, q - 1)
                    if q >= 2:
                        moe_down(e, q - 2)
                    if q == 2:
                        turn_picks(e)
                if not last:
                    pe.wait_ge(y_added, 4 * e + 4)
                    gather(e + 1)
                moe_turn(e, NC - 1)
                moe_down(e, NC - 2)
                moe_down(e, NC - 1)
                if not last:
                    pe.wait_ge(xgT_a, e + 2)
                    pe.wait_ge(xgT_v, e + 2)
                    moe_up(e + 1, 0)
                scatter(e)

            def moe_pass(n):
                pe.wait_ge(y_added, 4 * NE * n + 4)
                gather(NE * n)
                pe.wait_ge(xgT_a, NE * n + 1)
                pe.wait_ge(xgT_v, NE * n + 1)
                moe_up(NE * n, 0)
                with pe.Fori(NE * n, NE * n + NE - 1) as e:
                    expert(e, False)
                expert(NE * n + NE - 1, True)

            moe_pass(0)
            pe.wait_ge(route_done, 1)
            over = pe.value_load(overflow[0:1, 0:1], min_val=0, max_val=S)
            with pe.If(over > CAP):
                moe_pass(1)


def constants():
    c = np.zeros((P, C_COLS), np.float32)
    i = np.arange(P)
    c[:, C_ID:C_ID + P] = np.eye(P)
    c[:, C_FLIP:C_FLIP + P] = np.eye(P)[::-1]
    c[:, C_UP:C_UP + P] = i[:, None] < i[None, :]
    c[:, C_IOTA:C_IOTA + S] = np.arange(S)
    c[:, C_TRI:C_TRI + 64] = (np.arange(8)[None, :] < np.arange(8)[:, None]).reshape(-1)
    c[:, C_ROW] = i >= 31
    c[:, C_BD:C_BD + 8] = (i[:, None] // N_CMP) == np.arange(8)[None, :]
    return c


def bias_vectors():
    dist = S - 1 - np.arange(VEC)
    n = np.maximum(dist, 0)
    large = NB // 2 + (np.log(np.maximum(n, 1).astype(np.float32) / np.float32(NB // 2))
                       / np.float32(math.log(MAXDIST / (NB // 2))) * (NB - NB // 2)).astype(np.int32)
    bucket = np.where(n < NB // 2, n, np.minimum(large, NB - 1))
    v = np.zeros((NB, 2 * VEC), np.float32)
    v[:, 0:VEC] = (bucket[None, :] == np.arange(NB)[:, None]) & (dist >= 0)[None, :]
    v[0:16, VEC:2 * VEC] = np.where(dist >= 0, 0.0, INV_SCALE * NEG)
    return v


def laid_out(a):
    w0 = a.pop("l0_w_in")
    cuts = np.cumsum([512, 128, 128, 512, 128, 128, 128, 128, 128, 128])
    qa, ka, va, qb, kc, vc, ks, vs, kw, vw, g = np.split(w0, cuts, axis=1)

    def by_pair(q):
        return q.reshape(D, 2, 4, DH).transpose(0, 2, 1, 3).reshape(D, 8 * DH)

    a["l0_w_in"] = np.concatenate([by_pair(qa), ka, va, by_pair(qb), ks, vs, kw, vw, g], axis=1)
    a["l0_w_cmp"] = np.concatenate([c[:, DH * i:DH * i + DH] for c in (kc, vc) for i in (0, 0, 1, 1)], axis=1)
    a["l0_cmpk_w2"] = np.concatenate([a["l0_cmpk_w2"]] * 2, axis=1)
    q, k, v, qi, ki, wi = np.split(a["l1_w_in"], np.cumsum([D, DH, DH, 256, 32]), axis=1)
    a["l1_w_in"] = np.concatenate([q, k, k, v, qi, ki, ki, ki, ki, wi], axis=1)

    def up_chunks(gate, up):
        both = np.stack([w.reshape(*w.shape[:-2], KD, P, NC, FC) for w in (gate, up)], axis=-2)
        n = both.ndim
        order = list(range(n - 5)) + [n - 3, n - 4, n - 5, n - 2, n - 1]
        return np.ascontiguousarray(both.transpose(order)).reshape(*gate.shape[:-2], NC, P, GU)

    def down_chunks(w):
        w = w.reshape(*w.shape[:-2], NC, FC // P, P, D)
        return np.ascontiguousarray(np.swapaxes(w, -3, -2)).reshape(*w.shape[:-4], NC, P, DN)

    a["l0_ffn_gate_up"] = up_chunks(a.pop("l0_ffn_gate"), a.pop("l0_ffn_up"))
    a["l1_exp_gate_up"] = up_chunks(a.pop("l1_exp_gate"), a.pop("l1_exp_up"))
    a["l0_ffn_down"] = down_chunks(a["l0_ffn_down"])
    a["l1_exp_down"] = down_chunks(a["l1_exp_down"])
    return {n: np.ascontiguousarray(w) for n, w in a.items()}


def kernel(**inputs):
    import concourse.bacc as bacc
    from concourse.bass_utils import run_bass_kernel_spmd

    nc = bacc.Bacc("TRN2", target_bir_lowering=False, num_devices=1)
    arrays = laid_out({n: np.asarray(a) for n, a in inputs.items()})
    arrays["consts"] = constants()
    arrays["vecs"] = bias_vectors()
    t = {n: nc.dram_tensor(f"in_{n}", a.shape, mybir.dt.from_np(a.dtype), kind="ExternalInput").ap()
         for n, a in arrays.items()}
    out = nc.dram_tensor("out", (1, S, D), F32, kind="ExternalOutput").ap()
    scratch = nc.dram_tensor("bias_rows", (16, VEC), F32, kind="Internal").ap()
    build(nc, t, out, scratch)
    r = run_bass_kernel_spmd(nc, [{f"in_{n}": a for n, a in arrays.items()}], core_ids=[0])
    return r.results[0]["out"]
```

```python
import math
from contextlib import ExitStack

import numpy as np

import concourse.bass as bass
from concourse import mybir

F32 = mybir.dt.float32
F32R = mybir.dt.float32r
I32 = mybir.dt.int32
ALU = mybir.AluOpType
ACT = mybir.ActivationFunctionType
AX = mybir.AxisListType

P = 128
S = 256
TT = S // P
D = 1024
KD = D // P
DH = 64
F = 2816
FC = 256
NC = F // FC
NE = 8
CAP = P
HALF = 512
NB = 32
N_CMP = 15
CMP_HID = 256
CMP_PAIRS = 16
TOPK = S // 4
ALPHA = (2.0 * 2) ** 0.25
EPS = 1e-5
SCALE = DH ** -0.5
INV_SCALE = 8.0
NEG = -1e30
TAKEN = -3e38
MAXDIST = 128

W0_COLS = 1816
QA0, KA0, VA0, QB0, KS0, VS0, KW0, VW0 = 0, 512, 640, 768, 1280, 1408, 1536, 1664
W1_COLS = 1608
K1, V1, QI1, KI1, WI1 = 1024, 1152, 1216, 1472, 1600
W_FLOATS = 16576

RING = 4
UP_SLOT = (0, 1, 2, 3, 0, 1, 2, 0, 3, 1, 2)
HI_BUF = (0, 1, 2, 3) * 4 + (0, 1, 2) * 2
DN_SLOT = tuple(q % RING for q in range(NC))
GU = KD * 2 * FC
DN = (FC // P) * D

C_ID, C_FLIP, C_UP, C_IOTA, C_TRI, C_ROW, C_BD = 0, 128, 256, 384, 640, 704, 705
C_COLS = 713
VEC = 384


def rep(ap, n):
    return bass.AP(ap.tensor, ap.offset, [list(ap.ap[0]), [0, n]] + [list(d) for d in ap.ap[1:]])


def rep_last(ap, n):
    return bass.AP(ap.tensor, ap.offset, [list(d) for d in ap.ap] + [[0, n]])


def to_all(vec, n):
    return bass.AP(vec.tensor, vec.offset, [[0, P], [1, n]])


def loads_up_to(slots, q):
    return slots[:q + 1].count(slots[q])


def chunks_before(slots, block, q, size=NC):
    same = [n for n in range(size) if slots[n] == slots[q]]
    at = same.index(q)
    return size * block + same[at - 1] + 1 if at else size * (block - 1) + same[-1] + 1


def build(nc, t, out, scratch):
    with ExitStack() as ctx:
        def sb(name, shape, dt=F32):
            return ctx.enter_context(nc.sbuf_tensor(name, shape, dt))

        starts = {}

        def area(name, shape):
            made = sb(name, shape)
            starts[name] = nc.sbuf_base - 4 * int(np.prod(shape[1:]))
            return made

        def part(name, over, first, size):
            return nc.alloc_sbuf_tensor_at(name, [P, size], F32R, offset=starts[over] + 4 * first)

        def sem(name):
            return ctx.enter_context(nc.semaphore(name))

        W = area("W", [P, W_FLOATS])
        gu = [area(f"gu{i}", [P, GU]) for i in range(RING)]
        dn = [area(f"dn{i}", [P, DN]) for i in range(RING)]
        T8 = area("T8", [P, 16, S])
        x = area("x", [P, TT, D])
        xT = area("xT", [P, KD, S])
        qbuf = sb("qbuf", [P, 8, S])
        kvbuf = sb("kvbuf", [P, 3, S])
        cst = sb("cst", [P, C_COLS])
        ident = cst[:, C_ID:C_ID + P]
        flip = cst[:, C_FLIP:C_FLIP + P]
        upper = cst[:, C_UP:C_UP + P]
        iota = cst[:, C_IOTA:C_IOTA + S]
        tri8 = cst[:, C_TRI:C_TRI + 64].rearrange("p (a b) -> p a b", b=8)
        rowvalid = cst[:, C_ROW:C_ROW + 1]
        bdmask = cst[:, C_BD:C_BD + 8]
        small = sb("small", [P, 136])
        mx = small[:, 0:8].rearrange("p (a b) -> p a b", b=4)
        neg = small[:, 8:16].rearrange("p (a b) -> p a b", b=4)
        sums = small[:, 16:24].rearrange("p (a b) -> p a b", b=4)
        sk = small[:, 24:32].rearrange("p (a b) -> p a b", b=4)
        ske = small[:, 32:40].rearrange("p (a b) -> p a b", b=4)
        coef = small[:, 40:48].rearrange("p (a b) -> p a b", b=4)
        gates = small[:, 48:96].rearrange("p (a b) -> p a b", b=24)
        sinks = small[:, 96:104]
        bnst = small[:, 104:128].rearrange("p (a b c) -> p a b c", a=2, b=2)
        mv = small[:, 128:132].rearrange("p (a b) -> p a b", b=2)
        rstd = small[:, 132:134]
        wi = sb("wi", [P, TT, 8])
        overflow = sb("overflow", [P, 1], I32)
        route = sb("route", [P, 64])
        comb = route[:, 0:16].rearrange("p (a b) -> p a b", b=8)
        mask = route[:, 16:32].rearrange("p (a b) -> p a b", b=8)
        rank = route[:, 32:48].rearrange("p (a b) -> p a b", b=8)
        cmp_m = route[:, 0:16]
        cmp_s = route[:, 16:32]
        cmp_c = route[:, 32:48]

        ps = [ctx.enter_context(nc.psum_tensor(f"ps{i}", [P, HALF], F32)) for i in range(8)]

        w_in0 = W[:, 0:KD * W0_COLS].rearrange("p (k c) -> p k c", c=W0_COLS)
        w_out = W[:, 0:KD * D].rearrange("p (k c) -> p k c", c=D)
        o = KD * D
        s_sb = W[:, o:o + 2048].rearrange("p (b h k) -> p b h k", b=2, h=4)
        p_sb = W[:, o + 2048:o + 4096].rearrange("p (b n) -> p b n", b=2)
        pT = W[:, o + 4096:o + 6144].rearrange("p (b h k q) -> p b h k q", b=2, h=4, k=2)
        mix = W[:, o + 6144:o + 8192].rearrange("p (a d) -> p a d", a=2)
        flat_T = gu[0][:, :].rearrange("p (h k) -> p h k", h=16)
        w1k = gu[2][:, :].rearrange("p (i n) -> p i n", i=CMP_PAIRS)
        w1v = gu[3][:, :].rearrange("p (i n) -> p i n", i=CMP_PAIRS)
        g1 = gu[1]
        onehot = g1[0:NB, 0:VEC]
        negvec = g1[0:16, VEC:2 * VEC]
        rvec = g1[0:16, 2 * VEC:3 * VEC]
        posrow = g1[0:16, 1152:1408]
        vcbd = g1[0:120, 0:512]
        cPT = g1[0:120, 512:768].rearrange("p (a q) -> p a q", a=2)
        ctmp = g1[:, 768:1280]
        va = g1[:, 1408:1664].rearrange("p (a d) -> p a d", a=2)
        vs = g1[:, 1664:1920].rearrange("p (a d) -> p a d", a=2)
        vw = g1[:, 1920:2176].rearrange("p (a d) -> p a d", a=2)
        w2k = g1[:, 2176:2432].rearrange("p (f d) -> p f d", f=2)
        w2v = g1[:, 3728:3856].rearrange("p (f d) -> p f d", f=2)
        hidv = g1[:, 3856:4096].rearrange("p (f n) -> p f n", f=2)
        w_cmp = [d[:, :].rearrange("p (k c) -> p k c", c=4 * P) for d in dn[0:2]]
        gel = g1[:, 2432:3152].rearrange("p (a n) -> p a n", n=120)
        kcbd = g1[:, 3152:3182]
        csc = g1[:, 3184:3424]
        otmp = g1[:, 3424:3680]
        pos2 = g1[:, 3680:3712].rearrange("p (v i) -> p v i", v=2)
        relb = g1[0:NB, 3712:3728]
        T8a = dn[2][:, :].rearrange("p (h k) -> p h k", h=8)
        kt2 = dn[3][:, 0:1024].rearrange("p (v g s) -> p v g s", v=2, g=2)
        blk = dn[3][:, 1024:1984].rearrange("p (v i n) -> p v i n", v=2, i=CMP_PAIRS)
        qaT, qbT = qbuf[:, 0:4, :], qbuf[:, 4:8, :]
        kaT, ksT, kwT = kvbuf[:, 0, :], kvbuf[:, 1, :], kvbuf[:, 2, :]
        lnp = qbuf[:, :, :].rearrange("p (a h) s -> p a (h s)", a=2)
        sg = kvbuf[:, 0:2, :]
        hh = W[:, 14912:15424].rearrange("p (b f) -> p b f", b=2)
        gu_lo = [part(f"gu_lo{i}", f"gu{i}", 0, GU) for i in range(RING)]
        dn_lo = [part(f"dn_lo{i}", f"dn{i}", 0, DN) for i in range(RING)]
        ffn_up_hi = [part(f"ffn_up_hi{h}", "gu2", h * DN, DN) for h in range(2)]
        moe_up_hi = [part(f"moe_up_hi{i}", over, first, DN)
                     for i, (over, first) in enumerate((("W", 0), ("W", DN), ("x", 0), ("xT", 0)))]
        dn_hi = [part("ffn_dn_hi", "gu3", 0, 2 * DN), part("moe_dn_hi", "W", GU, 2 * DN)]
        xTh = part("xT_hi", "xT", 0, KD * S)[:, :].rearrange("p (k s) -> p k s", k=KD)
        xTl = part("xT_lo", "W", KD * W1_COLS, KD * S)[:, :].rearrange("p (k s) -> p k s", k=KD)
        hTh = part("hT_hi", "W", 15424, 512)[:, :].rearrange("p (b s q) -> p b s q", b=2, s=2)
        hTl = part("hT_lo", "W", 15936, 512)[:, :].rearrange("p (b s q) -> p b s q", b=2, s=2)
        w_in1 = W[:, 0:KD * W1_COLS].rearrange("p (k c) -> p k c", c=W1_COLS)
        kT1, kiT = kvbuf[:, 0, :], kvbuf[:, 1, :]
        v1 = kvbuf[:, 2, 0:TT * DH].rearrange("p (a d) -> p a d", a=2)
        g3 = gu[3]
        ts8 = g3[:, 0:2048].rearrange("p (b n) -> p b n", b=2)
        sel = g3[:, 2048:2560].rearrange("p (a k) -> p a k", a=2)
        qiT = g3[:, 2560:3072].rearrange("p (a k) -> p a k", a=2)
        relu = g3[:, 3072:4096].rearrange("p (b h k) -> p b h k", b=2, h=2)
        score = dn[3][:, 0:512].rearrange("p (a k) -> p a k", a=2)
        m8 = dn[3][:, 512:520]
        y = W[:, 8192:10240].rearrange("p (a d) -> p a d", a=2)
        xh = part("x_hi", "T8", 0, 2 * D)[:, :].rearrange("p (a d) -> p a d", a=2)
        xl = part("x_lo", "T8", 2 * D, 2 * D)[:, :].rearrange("p (a d) -> p a d", a=2)
        xgh = part("xg_hi", "W", 10240, D)[:, :].rearrange("p (k q) -> p k q", k=KD)
        xgl = part("xg_lo", "W", 11264, D)[:, :].rearrange("p (k q) -> p k q", k=KD)
        yeh = part("ye_hi", "W", 12288, D)
        yel = part("ye_lo", "W", 13312, D)
        pick = part("pick", "W", 14336, 2 * P)[:, :].rearrange("p (a q) -> p a q", a=2)
        pickT = part("pickT", "W", 14592, 2 * P)[:, :].rearrange("p (a q) -> p a q", a=2)
        rt = W[:, 10240:11264].rearrange("p (b n) -> p b n", b=4)
        wr = W[:, 12288:12352].rearrange("p (k e) -> p k e", e=8)
        ones = W[:, 12352:12480]

        ld_x, ld_cst, ld_vec, ld_pos, ld_w2, ld_w1, ld_flat = [sem(n) for n in (
            "ld_x", "ld_cst", "ld_vec", "ld_pos", "ld_w2", "ld_w1", "ld_flat")]
        ld_win = [sem(f"ld_win_part{i}") for i in range(4)]
        ld_wout, ld_win1, ld_lnp, ld_wr, rvec_stored = [sem(n) for n in (
            "ld_wout", "ld_win1", "ld_lnp", "ld_wr", "rvec_stored")]
        gu_loaded = [sem(f"gu_loaded{i}") for i in range(RING)]
        dn_loaded = [sem(f"dn_loaded{i}") for i in range(RING)]
        gu_used, dn_used = sem("gu_used"), sem("dn_used")
        front_pe, front_v, front_a = sem("front_pe"), sem("front_v"), sem("front_a")
        t8a_made, vec_step = sem("t8a_made"), sem("vec_step")
        blk_made, cmp_pe, cmp_v, cmp_a = sem("blk_made"), sem("cmp_pe"), sem("cmp_v"), sem("cmp_a")
        gates_exp, gates_made = sem("gates_exp"), sem("gates_made")
        at = [{n: sem(f"at{layer}_{n}") for n in (
            "scores", "biased", "negmax", "sink_arg", "exp", "sink_exp", "pt", "pt_v", "pt_a", "o", "o_out")} for layer in range(2)]
        lnx = [{n: sem(f"ln{i}_{n}") for n in ("var", "sd", "x")} for i in range(4)]
        tr = [{n: sem(f"tr{i}_{n}") for n in ("pe", "v", "a")} for i in range(5)]
        outp = [sem("outp0"), sem("outp1")]
        ffn_g0, ffn_silu, ffn_h, ffn_t, ffn_hTh, ffn_hTl = [sem(n) for n in (
            "ffn_g0", "ffn_silu", "ffn_h", "ffn_t", "ffn_hTh", "ffn_hTl")]
        hi_made, lo_made, gu_first_used = sem("hi_made"), sem("lo_made"), sem("gu_first_used")
        xT_hi, xT_lo, x_hi, x_lo = sem("xT_hi"), sem("xT_lo"), sem("x_hi"), sem("x_lo")
        pr_pe, pr_v, pr_a = sem("pr_pe"), sem("pr_v"), sem("pr_a")
        idx_pe, idx_relu, idx_acc, idx_causal, idx_sel, ts_made = [sem(n) for n in (
            "idx_pe", "idx_relu", "idx_acc", "idx_causal", "idx_sel", "ts_made")]
        logits_pe, logits_v, route_exp, mask_made, rank_pe, route_done, moe_ones = [sem(n) for n in (
            "logits_pe", "logits_v", "route_exp", "mask_made", "rank_pe", "route_done", "moe_ones")]
        moe_silu, moe_h, moe_t, moe_hTh, moe_hTl = [sem(n) for n in (
            "moe_silu", "moe_h", "moe_t", "moe_hTh", "moe_hTl")]
        pick_made, gathered, xg_a, xg_v = [sem(n) for n in ("pick_made", "gathered", "xg_a", "xg_v")]
        pickT_pe, pickT_a, ye_a, ye_v, scattered, y_added = [sem(n) for n in (
            "pickT_pe", "pickT_a", "ye_a", "ye_v", "scattered", "y_added")]
        stored = sem("stored")

        front = [("rvec",), ("pos",)] + [("xT", j) for j in range(4)]
        front += [("colsA", qaT, j, QA0 + P * j, 0) for j in range(4)] + [("cols", kaT, KA0, 0)]
        front += [("colsA", qbT, j, QB0 + P * j, 1) for j in range(4)]
        front += [("dup", kv, g, 2 * kv + g, 2) for kv in range(2) for g in range(2)]
        front += [("cols", ksT, KS0, 3), ("cols", kwT, KW0, 3)]
        front += [("v", tt) for tt in range(TT)] + [("flip", j) for j in range(8)]
        NF = len(front)

        def v_jobs(n):
            return (n + 1) // 2

        def a_jobs(n):
            return n // 2

        units0 = [(kind, qt, g) for kind in "ASW" for qt in range(2) for g in range(2)]
        units1 = [("C", qt, c) for qt in range(2) for c in range(4)]

        def heads_of(u):
            kind, qt, g = u
            return [4 * g, 4 * g + 2, 4 * g + 1, 4 * g + 3] if kind == "C" else list(range(4 * g, 4 * g + 4))

        proj1 = [("q", m) for m in range(8)] + [("k",), ("qi", 0), ("qi", 1), ("ki",), ("v", 0), ("v", 1)]
        NP1 = len(proj1)
        CMP_DONE = {"z": 4, "gelu": 9, "kv": 12, "centred": 16, "coef": 20, "turned": 21, "taken0": 22, "mixed1": 25}

        FFN_PARTS = 3 * NC

        def ffn_up_part(c, h):
            return 3 * c + h + 1 if c else h + 1

        def ffn_dn_part(c):
            return 3 * c + 3

        def moe_parts(e):
            return FFN_PARTS + 7 + 3 * NC * e

        def moe_up_part(e, q, h):
            return moe_parts(e) + 3 * (q - 3) + h + 2

        def moe_dn_part(e, q, last):
            return moe_parts(e) + (3 * (NC - 3) + q - (NC - 3) if last and q >= NC - 2 else 3 * q - 2)

        def moe_buffer_chunks(e, q):
            if q < 2:
                e, q = e - 1, q + NC
            n = NC * e + (q - 1 if q < NC else 2 * NC - q)
            return max(n, 0) if isinstance(n, int) else n

        def wait_for_chunks(eng, sem, n):
            if not isinstance(n, int) or n > 0:
                eng.wait_ge(sem, n)

        block = ctx.enter_context(nc.Block())

        @block.sync
        def _(sp):
            w = t["l0_w_in"].rearrange("(k p) c -> p k c", p=P)
            sp.dma_start(cst[:, :], t["consts"]).then_inc(ld_cst, 16)
            sp.dma_start(x[:, :, :], t["x"][0].rearrange("(a p) d -> p a d", p=P)).then_inc(ld_x, 16)
            for i in range(4):
                if i == 2:
                    wc = t["l0_w_cmp"].rearrange("(k p) c -> p k c", p=P)
                    for n in range(2):
                        sp.dma_start(w_cmp[n], wc[:, 4 * n:4 * n + 4, :]).then_inc(ld_win[2], 16)
                    continue
                a, b = (0, QB0, 0, KS0)[i], (QB0, KS0, 0, W0_COLS)[i]
                sp.dma_start(w_in0[:, :, a:b], w[:, :, a:b]).then_inc(ld_win[i], 16)
                if i == 1:
                    sp.wait_ge(front_v, 1)
                    sp.dma_start(scratch, rvec).then_inc(rvec_stored, 16)
                    sp.wait_ge(rvec_stored, 16)
                    src = bass.AP(scratch.tensor, scratch.offset, [[1, P], [VEC, 16], [1, S]])
                    sp.dma_start(flat_T, src).then_inc(ld_flat, 16)
            sp.dma_start(w1k, t["l0_cmpk_w1"].rearrange("(i p) n -> p i n", p=P)).then_inc(ld_w1, 16)
            sp.dma_start(w1v, t["l0_cmpv_w1"].rearrange("(i p) n -> p i n", p=P)).then_inc(ld_w1, 16)

            sp.wait_ge(tr[1]["pe"], 4)
            for q in range(NC):
                if q == RING:
                    sp.wait_ge(outp[0], 4)
                    w = t["l1_w_in"].rearrange("(k p) c -> p k c", p=P)
                    sp.dma_start(w_in1, w).then_inc(ld_win1, 16)
                if q >= 2:
                    sp.wait_ge(gu_used, q - 1)
                sp.dma_start(gu[q % 2][:, :], t["l0_ffn_gate_up"][q]).then_inc(gu_loaded[q % 2], 16)
                if q >= RING:
                    sp.wait_ge(dn_used, q - RING + 1)
                sp.dma_start(dn[q % RING][:, :], t["l0_ffn_down"][q]).then_inc(dn_loaded[q % RING], 16)

            def weights(name, e, q):
                w = t[name][bass.ds(e, 1)] if not isinstance(e, int) else t[name][e:e + 1]
                return w.rearrange("o c p n -> (o c) p n")[q]

            def load_up(e, count, q):
                s = UP_SLOT[q]
                if isinstance(count, int) and count == 0 and q < RING:
                    if s < 2:
                        sp.wait_ge(gu_used, NC if (NC - 1) % 2 == s else NC - 1)
                    else:
                        sp.wait_ge(dn_used, NC)
                else:
                    sp.wait_ge(gu_used, chunks_before(UP_SLOT, count + 1, q))
                sp.dma_start(gu[s][:, :], weights("l1_exp_gate_up", e, q)).then_inc(gu_loaded[s], 16)

            def load_down(e, count, q):
                sp.wait_ge(dn_used, chunks_before(DN_SLOT, count + 1, q))
                sp.dma_start(dn[q % RING][:, :], weights("l1_exp_down", e, q)).then_inc(dn_loaded[q % RING], 16)

            def expert(e, count, last, start=0):
                for q in range(start, NC):
                    if q + 2 < NC:
                        load_up(e, count, q + 2)
                    elif not last:
                        load_up(e + 1, count + 1, q + 2 - NC)
                    load_down(e, count, q)

            for q in range(RING - 1):
                load_up(0, 0, q)
                load_down(0, 0, q)
            sp.wait_ge(tr[3]["pe"], 4)
            load_up(0, 0, RING - 1)
            load_down(0, 0, RING - 1)
            load_up(0, 0, RING)
            load_up(0, 0, RING + 1)
            expert(0, 0, False, start=RING)
            with sp.Fori(1, NE - 1) as e:
                expert(e, e, False)
            expert(NE - 1, NE - 1, True)

            sp.wait_ge(route_done, 1)
            over = sp.value_load(overflow[0:1, 0:1], min_val=0, max_val=S)
            with sp.If(over > CAP):
                for q in range(2):
                    load_up(0, NE, q)
                with sp.Fori(0, NE - 1) as e:
                    expert(e, e + NE, False)
                expert(NE - 1, 2 * NE - 1, True)
            for tt in range(TT):
                sp.wait_ge(lnx[3]["x"], tt + 1)
                sp.dma_start(out[0].rearrange("(a p) d -> p a d", p=P)[:, tt, :], y[:, tt, :]).then_inc(stored, 16)
            sp.wait_ge(stored, 16 * TT)

        @block.gpsimd
        def _(pool):
            pool.wait_ge(front_v, v_jobs(NF))
            pool.wait_ge(front_a, a_jobs(NF))
            nc.gpsimd.affine_select(out=T8a[:, :, 0:P], in_=T8[:, 0:8, 0:P], pattern=[[0, 8], [1, P]],
                                    compare_op=ALU.is_gt, fill=INV_SCALE * NEG, base=0,
                                    channel_multiplier=-1).then_inc(t8a_made, 1)
            nc.gpsimd.tensor_copy(T8a[:, :, P:S], T8[:, 0:8, P:S]).then_inc(t8a_made, 1)
            for qt in range(TT):
                wk = P * (qt + 1)
                pool.wait_ge(idx_acc, 8 * (qt + 1))
                nc.gpsimd.affine_select(out=score[:, qt, 0:wk], in_=score[:, qt, 0:wk], pattern=[[-1, wk]],
                                        compare_op=ALU.is_ge, fill=NEG, base=P * qt,
                                        channel_multiplier=1).then_inc(idx_causal, 1)
            for i, (_, qt, c) in enumerate(units1):
                wk = P * (qt + 1)
                pool.wait_ge(idx_sel, qt + 1)
                if i >= 2:
                    pool.wait_ge(at[1]["biased"], 4 * (i - 1))
                dst = ts8[:, i % 2, 0:4 * wk].rearrange("p (h k) -> p h k", h=4)
                nc.gpsimd.tensor_tensor(dst, T8[:, 4 * c:4 * c + 4, S - wk:S], rep(sel[:, qt, 0:wk], 4),
                                        ALU.add).then_inc(ts_made, 1)

        def copy_front(eng, copy, j, ready):
            bank, job = ps[j % 8], front[j]
            eng.wait_ge(front_pe, j + 1)
            kind = job[0]
            if kind == "pos":
                copy(pos2, bank[:, 0:32].rearrange("p (v i) -> p v i", v=2)).then_inc(ready, 1)
            elif kind == "xT":
                copy(xT[:, 2 * job[1]:2 * job[1] + 2, :], bank[:, :].rearrange("p (k s) -> p k s", k=2))\
                    .then_inc(ready, 1)
            elif kind == "colsA":
                copy(job[1][:, job[2], :], bank[:, 0:S]).then_inc(ready, 1)
            elif kind == "cols":
                copy(job[1], bank[:, 0:S]).then_inc(ready, 1)
            elif kind == "dup":
                dst = kt2[:, job[1], job[2], :]
                copy(dst[0:DH, :], bank[0:DH, 0:S])
                copy(dst[DH:P, 0:S - 1], bank[DH:P, 1:S]).then_inc(ready, 1)
            elif kind == "v":
                tt = job[1]
                copy(va[:, tt, :], bank[:, 0:P])
                copy(vs[:, tt, :], bank[:, P:2 * P])
                copy(vw[:, tt, :], bank[:, 2 * P:3 * P])
                copy(gates[:, tt, :], bank[:, 3 * P:3 * P + 24]).then_inc(ready, 1)
            elif kind == "flip":
                copy(T8[:, 2 * job[1]:2 * job[1] + 2, :], bank[:, :].rearrange("p (h k) -> p h k", h=2))\
                    .then_inc(ready, 1)

        def copy_p1(eng, copy, j, ready):
            bank, job = ps[j % 8], proj1[j]
            eng.wait_ge(pr_pe, j + 1)
            if job[0] == "q":
                copy(qbuf[:, job[1], :], bank[:, 0:S]).then_inc(ready, 1)
            elif job[0] == "k":
                copy(kT1, bank[:, 0:S]).then_inc(ready, 1)
            elif job[0] == "qi":
                copy(qiT[:, job[1], :], bank[:, 0:S]).then_inc(ready, 1)
            elif job[0] == "ki":
                copy(kiT, bank[:, 0:S]).then_inc(ready, 1)
            else:
                copy(v1[:, job[1], :], bank[:, 0:DH])
                copy(wi[:, job[1], :], bank[:, DH:DH + 8]).then_inc(ready, 1)

        def copy_tr(eng, copy, i, j, ready):
            eng.wait_ge(tr[i]["pe"], j + 1)
            copy(xT[:, 2 * j:2 * j + 2, :], ps[j][:, :].rearrange("p (k s) -> p k s", k=2)).then_inc(ready, 1)

        def unit_p(u, i):
            wk = P * (u[1] + 1)
            return p_sb[:, i % 2, 0:4 * wk].rearrange("p (h k) -> p h k", h=4)

        @block.scalar
        def _(act):
            def copy(dst, src):
                return nc.scalar.copy(dst, src)

            act.dma_start(relb, t["rel_bias"]).then_inc(ld_vec, 16)
            act.dma_start(onehot, t["vecs"][:, 0:VEC]).then_inc(ld_vec, 16)
            act.dma_start(negvec, t["vecs"][0:16, VEC:2 * VEC]).then_inc(ld_vec, 16)
            act.dma_start(posrow[:, 0:P], t["l0_cmpk_pos"].rearrange("(i j) d -> i (j d)", j=2)).then_inc(ld_pos, 16)
            act.dma_start(posrow[:, P:2 * P], t["l0_cmpv_pos"].rearrange("(i j) d -> i (j d)", j=2))\
                .then_inc(ld_pos, 16)
            act.dma_start(w2k, t["l0_cmpk_w2"].rearrange("(f p) d -> p f d", p=P)).then_inc(ld_w2, 16)
            act.dma_start(w2v, t["l0_cmpv_w2"].rearrange("(f p) d -> p f d", p=P)).then_inc(ld_w2, 16)
            act.dma_start(sinks, to_all(t["l0_sinks"], 8)).then_inc(ld_w2, 16)
            for j in range(1, NF, 2):
                copy_front(act, copy, j, front_a)
            act.wait_ge(front_pe, NF)
            act.dma_start(w_out, t["l0_w_out"].rearrange("(k p) c -> p k c", p=P)).then_inc(ld_wout, 16)
            act.wait_ge(front_v, v_jobs(NF))
            act.wait_ge(front_a, a_jobs(NF))
            nc.scalar.activation(gates, gates, ACT.Exp, scale=-1.0).then_inc(gates_exp, 1)

            def exps(a, units, i):
                u = units[i]
                wk = P * (u[1] + 1)
                act.wait_ge(a["negmax"], i + 1)
                if i >= 2:
                    act.wait_ge(a["pt"], i - 1)
                    act.wait_ge(a["o_out"], i - 1)
                for h in range(4):
                    nc.scalar.activation(unit_p(u, i)[:, h, :], s_sb[:, i % 2, h, 0:wk], ACT.Exp,
                                         bias=neg[:, i % 2, h:h + 1],
                                         accum_out=sums[:, i % 2, h:h + 1]).then_inc(a["exp"], 1)
                if u[0] == "A":
                    act.wait_ge(a["sink_arg"], i + 1)
                    nc.scalar.activation(ske[:, i % 2, :], sk[:, i % 2, :], ACT.Exp).then_inc(a["sink_exp"], 1)

            def pt_copy(a, units, i):
                nk = units[i][1] + 1
                act.wait_ge(a["pt"], i + 1)
                if i >= 2:
                    act.wait_ge(a["o"], i - 1)
                src = ps[5][:, :].rearrange("p (h k q) -> p h k q", h=2, k=2)[:, :, 0:nk, :]
                copy(pT[:, i % 2, 2:4, 0:nk, :], src).then_inc(a["pt_a"], 1)

            for i in range(len(units0) + 1):
                if i < len(units0):
                    exps(at[0], units0, i)
                if i >= 1:
                    pt_copy(at[0], units0, i - 1)
                if i == 3:
                    act.wait_ge(cmp_v, CMP_DONE["z"])
                    nc.scalar.activation(gel[:, 3, :], gel[:, 2, :], ACT.Exp,
                                         scale=-2.0 * math.sqrt(2.0 / math.pi)).then_inc(cmp_a, 1)
                if i == 7:
                    act.wait_ge(cmp_v, CMP_DONE["centred"])
                    nc.scalar.activation(csc, csc, ACT.Exp, scale=SCALE).then_inc(cmp_a, 1)

            def layer_norm_sd(i):
                act.wait_ge(lnx[i]["var"], 1)
                nc.scalar.activation(rstd, rstd, ACT.Sqrt).then_inc(lnx[i]["sd"], 1)

            def ln_params(i, g, b):
                act.dma_start(lnp[:, 0, :], to_all(t[g], D)).then_inc(ld_lnp, 16)
                act.dma_start(lnp[:, 1, :], to_all(t[b], D)).then_inc(ld_lnp, 16)

            act.wait_ge(tr[1]["pe"], 4)
            ln_params(0, "l0_ln1_g", "l0_ln1_b")
            for j in (1, 3):
                copy_tr(act, copy, 1, j, tr[1]["a"])
            layer_norm_sd(0)
            for j in range(4):
                act.wait_ge(tr[0]["pe"], j + 1)
                copy(xTh[:, 2 * j:2 * j + 2, :], ps[j][:, :].rearrange("p (k s) -> p k s", k=2)).then_inc(xT_hi, 1)
            act.wait_ge(lnx[0]["x"], TT)
            ln_params(1, "l0_ln2_g", "l0_ln2_b")

            def hi_up(slot, dst, h, count, free, free_h):
                act.wait_ge(gu_loaded[slot], 16 * count)
                if free is not None:
                    act.wait_ge(gu_used if free_h else gu_first_used, free)
                copy(dst[:, :], gu[slot][:, h * DN:(h + 1) * DN]).then_inc(hi_made, 1)

            def hi_dn(slot, which, buf, count, free):
                act.wait_ge(dn_loaded[slot], 16 * count)
                if free is not None:
                    act.wait_ge(dn_used, free)
                copy(dn_hi[which][:, buf * DN:(buf + 1) * DN], dn[slot][:, :]).then_inc(hi_made, 1)

            def ffn_hi_up(c, h):
                hi_up(c % 2, ffn_up_hi[h], h, c // 2 + 1, c if c else None, h)

            def ffn_silu_step(q):
                c, tt = q // 2, q % 2
                act.wait_ge(gu_used if tt else ffn_g0, c + 1)
                if q >= 2:
                    act.wait_ge(ffn_h, q - 1)
                nc.scalar.activation(sg[:, q % 2, :], ps[q % 3][:, 0:FC], ACT.Silu).then_inc(ffn_silu, 1)

            def ffn_hT_step(q):
                c = q // 2
                act.wait_ge(ffn_t, q + 1)
                if c >= 1:
                    act.wait_ge(dn_used, c)
                copy(hTh[:, q % 2, :, :], ps[3][:, 0:2 * P].rearrange("p (s q) -> p s q", s=2)).then_inc(ffn_hTh, 1)

            ffn_hi_up(0, 0)
            ffn_hi_up(0, 1)
            for q in range(2 * NC):
                c, tt = q // 2, q % 2
                if tt and c + 1 < NC:
                    ffn_hi_up(c + 1, 0)
                if q >= 1:
                    ffn_hT_step(q - 1)
                if tt and c + 1 < NC:
                    ffn_hi_up(c + 1, 1)
                ffn_silu_step(q)
                if tt == 0:
                    hi_dn(c % RING, 0, c % 2, c // RING + 1, c - 1 if c >= 2 else None)
            ffn_hT_step(2 * NC - 1)
            layer_norm_sd(1)
            for j in (1, 3):
                copy_tr(act, copy, 2, j, tr[2]["a"])
            for j in range(1, NP1, 2):
                copy_p1(act, copy, j, pr_a)
            act.wait_ge(pr_pe, NP1)
            act.dma_start(w_out, t["l1_w_out"].rearrange("(k p) c -> p k c", p=P)).then_inc(ld_wout, 16)
            for qt in range(TT):
                wk = P * (qt + 1)
                for i in range(4):
                    n = 4 * qt + i
                    act.wait_ge(idx_pe, qt + 1)
                    if n >= 2:
                        act.wait_ge(idx_acc, 2 * (n - 1))
                    src = ps[i][:, :].rearrange("p (h k) -> p h k", h=2)[:, :, 0:wk]
                    nc.scalar.activation(relu[:, n % 2, :, 0:wk], src, ACT.Relu).then_inc(idx_relu, 1)
            for i in range(len(units1) + 1):
                if i < len(units1):
                    exps(at[1], units1, i)
                if i >= 1:
                    pt_copy(at[1], units1, i - 1)
            act.wait_ge(tr[3]["pe"], 4)
            ln_params(2, "l1_ln1_g", "l1_ln1_b")
            for j in (1, 3):
                copy_tr(act, copy, 3, j, tr[3]["a"])
            act.wait_ge(outp[1], 4)
            act.dma_start(wr, t["l1_router"].rearrange("(k p) e -> p k e", p=P)).then_inc(ld_wr, 16)
            layer_norm_sd(2)
            for j in (1, 3):
                copy_tr(act, copy, 4, j, tr[4]["a"])
            act.wait_ge(lnx[2]["x"], TT)
            ln_params(3, "l1_ln2_g", "l1_ln2_b")
            for tt in range(TT):
                act.wait_ge(logits_v, tt + 1)
                nc.scalar.activation(comb[:, tt, :], comb[:, tt, :], ACT.Exp,
                                     bias=rank[:, tt, 0:1]).then_inc(route_exp, 1)

            def up_loads(e, q):
                s = UP_SLOT[q]
                return len(range(s, NC, 2)) * (s < 2) + UP_SLOT.count(s) * e + loads_up_to(UP_SLOT, q)

            def moe_hi_up(e, q, h):
                c = q % NC
                n = chunks_before(HI_BUF, 0, 2 * c + h, 2 * NC) + 2 * NC * (q // NC) - 1
                hi_up(UP_SLOT[c], moe_up_hi[HI_BUF[2 * c + h]], h, up_loads(e + q // NC, c),
                      NC * (e + 1) + n // 2 + 1, n % 2)

            def moe_hi_dn(e, q):
                c = q % NC
                s = DN_SLOT[c]
                hi_dn(s, 1, c % 2, DN_SLOT.count(s) * (e + 1 + q // NC) + loads_up_to(DN_SLOT, c),
                      NC + moe_buffer_chunks(e, q))

            def moe_silu_step(e, q):
                c = q % NC
                act.wait_ge(gu_used, NC * (e + 1) + q + 1)
                wait_for_chunks(act, moe_h, moe_buffer_chunks(e, q))
                nc.scalar.activation(sg[:, c % 2, :], ps[3 if c == 0 else c % 2][:, 0:FC], ACT.Silu)\
                    .then_inc(moe_silu, 1)

            def moe_hT_step(e, q):
                act.wait_ge(moe_t, NC * e + q + 1)
                act.wait_ge(dn_used, NC + moe_buffer_chunks(e, q))
                copy(hTh[:, q % NC % 2, :, :], ps[2][:, 0:2 * P].rearrange("p (s q) -> p s q", s=2))\
                    .then_inc(moe_hTh, 1)

            def take_xg(e):
                act.wait_ge(gathered, e + 1)
                act.wait_ge(gu_used, NC * (e + 1))
                for i in range(2):
                    copy(xgh[:, 4 * i:4 * i + 4, :], ps[6 + i][:, :].rearrange("p (k q) -> p k q", k=4))\
                        .then_inc(xg_a, 1)

            def take_ye(e):
                act.wait_ge(dn_used, NC * (e + 2))
                for half in range(2):
                    copy(yeh[:, half * HALF:(half + 1) * HALF], ps[4 + half][:, :]).then_inc(ye_a, 1)

            def expert(e, last):
                for q in range(2, NC + 2):
                    up, more = q < NC or not last, q < NC - 1 or not last
                    if q == NC + 1:
                        take_ye(e)
                    if up or q == NC:
                        moe_hi_dn(e, q - 1)
                    if more:
                        moe_hi_up(e, q + 1, 0)
                    if up or q == NC:
                        moe_hT_step(e, q - 1)
                    if q == NC - 1 and not last:
                        take_xg(e + 1)
                    if more:
                        moe_hi_up(e, q + 1, 1)
                    if up:
                        moe_silu_step(e, q)
                    if q == 4:
                        act.wait_ge(pickT_pe, e + 1)
                        copy(pickT, ps[3][:, 0:2 * P].rearrange("p (a q) -> p a q", a=2)).then_inc(pickT_a, 1)

            def moe_pass(n):
                first = NE * n
                moe_hi_up(first, 0, 0)
                moe_hi_up(first, 0, 1)
                take_xg(first)
                if n == 0:
                    act.wait_ge(x_lo, TT)
                    act.wait_ge(y_added, 4)
                    act.wait_ge(logits_pe, 1)
                moe_hi_up(first, 1, 0)
                moe_hi_up(first, 1, 1)
                moe_silu_step(first, 0)
                moe_hi_dn(first, 0)
                moe_hi_up(first, 2, 0)
                moe_hT_step(first, 0)
                moe_hi_up(first, 2, 1)
                moe_silu_step(first, 1)
                with act.Fori(first, first + NE - 1) as e:
                    expert(e, False)
                expert(first + NE - 1, True)

            act.wait_ge(lnx[2]["x"], TT)
            for tt in range(TT):
                copy(xh[:, tt, :], x[:, tt, :]).then_inc(x_hi, 1)
            moe_pass(0)
            act.wait_ge(route_done, 1)
            over = act.value_load(overflow[0:1, 0:1], min_val=0, max_val=S)
            with act.If(over > CAP):
                moe_pass(1)
            layer_norm_sd(3)

        @block.vector
        def _(dve):
            steps = [0]

            def link(ins):
                steps[0] += 1
                ins.then_inc(vec_step, 1)
                dve.wait_ge(vec_step, steps[0])

            def copy(dst, src):
                return nc.vector.tensor_copy(dst, src)

            v = nc.vector
            link(v.memset(kcbd, 0.0))
            link(v.memset(csc, INV_SCALE * NEG))
            dve.wait_ge(front_pe, 1)
            dve.wait_ge(ld_vec, 48)
            v.scalar_tensor_tensor(out=rvec, in0=ps[0][0:16, 0:VEC], scalar=INV_SCALE, in1=negvec,
                                   op0=ALU.mult, op1=ALU.add).then_inc(front_v, 1)
            for j in range(2, NF, 2):
                copy_front(dve, copy, j, front_v)
            dve.wait_ge(front_v, v_jobs(NF))
            dve.wait_ge(front_a, a_jobs(NF))
            for kv in range(2):
                for half in range(2):
                    src = kt2[:, kv].rearrange("p g (n i two) -> p i g n two", i=8, two=2)
                    src = src[:, :, :, half:half + N_CMP, 0]
                    dst = blk[:, kv, 8 * half:8 * half + 8, :].rearrange("p i (g n) -> p i g n", g=2)
                    pos = rep_last(pos2[:, kv, 8 * half:8 * half + 8], N_CMP)
                    for g in range(2):
                        v.tensor_tensor(dst[:, :, g, :], src[:, :, g, :], pos, ALU.add)\
                            .then_inc(blk_made, 1)
            dve.wait_ge(gates_exp, 1)
            link(v.tensor_scalar(gates, gates, 1.0, None, ALU.add))
            v.reciprocal(gates, gates).then_inc(gates_made, 1)

            def bias_scores(a, units, i):
                u = units[i]
                kind, qt, g = u
                wk = P * (qt + 1)
                dve.wait_ge(a["scores"], i + 1)
                if i >= 2:
                    dve.wait_ge(a["exp"], 4 * (i - 1))
                if kind == "A" and i < 4:
                    if qt:
                        dve.wait_ge(t8a_made, 2)
                    if i == 0:
                        dve.wait_ge(ld_w2, 48)
                if kind == "C":
                    dve.wait_ge(ts_made, i + 1)
                for s, h in enumerate(heads_of(u)):
                    if kind == "A":
                        bias = T8a[:, h, :] if qt else T8[:, h, P:S]
                    elif kind == "C":
                        bias = ts8[:, i % 2, (h - 4 * g) * wk:(h - 4 * g + 1) * wk]
                    else:
                        bias = T8[:, 8 + h, S - wk:S]
                    src = ps[2 * (i % 2) + s // 2][:, (s % 2) * S:(s % 2) * S + wk]
                    init = sinks[:, h:h + 1] if kind == "A" else -3e38
                    v.tensor_tensor_reduce(out=s_sb[:, i % 2, s, 0:wk], in0=src, in1=bias, scale=SCALE, scalar=init,
                                           op0=ALU.add, op1=ALU.max, accum_out=mx[:, i % 2, s:s + 1])\
                        .then_inc(a["biased"], 1)
                dve.wait_ge(a["biased"], 4 * (i + 1))
                v.tensor_scalar(neg[:, i % 2, :], mx[:, i % 2, :], -1.0, None, ALU.mult).then_inc(a["negmax"], 1)
                if kind == "A":
                    dve.wait_ge(a["negmax"], i + 1)
                    if i >= 2:
                        dve.wait_ge(a["sink_exp"], i - 1)
                    v.tensor_tensor(sk[:, i % 2, :], sinks[:, 4 * g:4 * g + 4], neg[:, i % 2, :], ALU.add)\
                        .then_inc(a["sink_arg"], 1)

            def pt_copy(a, units, i):
                nk = units[i][1] + 1
                dve.wait_ge(a["pt"], i + 1)
                if i >= 2:
                    dve.wait_ge(a["o"], i - 1)
                src = ps[4][:, :].rearrange("p (h k q) -> p h k q", h=2, k=2)[:, :, 0:nk, :]
                copy(pT[:, i % 2, 0:2, 0:nk, :], src).then_inc(a["pt_v"], 1)

            def mix_out(a, units, i):
                kind, qt, g = units[i]
                dve.wait_ge(a["exp"], 4 * (i + 1))
                cf = coef[:, i % 2, :]
                if kind == "A":
                    dve.wait_ge(a["sink_exp"], i + 1)
                    link(v.tensor_tensor(cf, sums[:, i % 2, :], ske[:, i % 2, :], ALU.add))
                    link(v.reciprocal(cf, cf))
                else:
                    link(v.reciprocal(cf, sums[:, i % 2, :]))
                if kind in "SW":
                    dve.wait_ge(gates_made, 1)
                    br = 8 * (1 if kind == "S" else 2) + 4 * g
                    link(v.tensor_tensor(cf, cf, gates[:, qt, br:br + 4], ALU.mult))
                dve.wait_ge(a["o"], i + 1)
                src = ps[6][:, 0:S].rearrange("p (h d) -> p h d", h=4)
                cfb = rep_last(cf, DH)
                if kind == "C":
                    dst = mix[:, qt, S * g:S * (g + 1)].rearrange("p (r f d) -> p f r d", r=2, f=2)
                    v.tensor_tensor(dst, src.rearrange("p (f r) d -> p f r d", f=2),
                                    cfb.rearrange("p (f r) d -> p f r d", f=2), ALU.mult).then_inc(a["o_out"], 1)
                    return
                base = (0 if kind == "A" else HALF) + S * g
                dst = mix[:, qt, base:base + S].rearrange("p (h d) -> p h d", h=4)
                if kind == "W":
                    tmp = otmp.rearrange("p (h d) -> p h d", h=4)
                    v.tensor_tensor(tmp, src, cfb, ALU.mult).then_inc(a["o_out"], 1)
                    dve.wait_ge(a["o_out"], i + 1)
                    link(v.tensor_tensor(dst, dst, tmp, ALU.add))
                else:
                    v.tensor_tensor(dst, src, cfb, ALU.mult).then_inc(a["o_out"], 1)

            cn = [0]

            def cstep(ins):
                cn[0] += 1
                ins.then_inc(cmp_v, 1)
                dve.wait_ge(cmp_v, cn[0])

            def cmp_step(k):
                if k == 0:
                    dve.wait_ge(cmp_pe, 1)
                    cstep(copy(gel[:, 0, :], ps[7][:, 0:120]))
                    cstep(v.tensor_tensor(gel[:, 1, :], gel[:, 0, :], gel[:, 0, :], ALU.mult))
                    cstep(v.tensor_scalar(gel[:, 2, :], gel[:, 1, :], 0.044715, 1.0, ALU.mult, ALU.add))
                    cstep(v.tensor_tensor(gel[:, 2, :], gel[:, 2, :], gel[:, 0, :], ALU.mult))
                elif k == 1:
                    dve.wait_ge(cmp_a, 1)
                    cstep(v.tensor_scalar(gel[:, 4, :], gel[:, 3, :], 1.0, None, ALU.add))
                    cstep(v.reciprocal(gel[:, 4, :], gel[:, 4, :]))
                    cstep(v.tensor_tensor(gel[:, 5, :], gel[:, 4, :], gel[:, 0, :], ALU.mult))
                    src = gel[:, 5, 60:120].rearrange("p (f n) -> p f n", f=2)
                    dst = hidv.rearrange("p f (r n) -> p f r n", r=4)
                    for f in range(2):
                        cstep(copy(dst[:, f], rep(src[:, f, :], 4)))
                elif k == 2:
                    dve.wait_ge(cmp_pe, 2)
                    cstep(copy(kcbd[0:DH, 0:N_CMP], ps[7][0:DH, 0:N_CMP]))
                    cstep(copy(kcbd[DH:P, N_CMP:2 * N_CMP], ps[7][DH:P, N_CMP:2 * N_CMP]))
                    cstep(v.tensor_tensor(vcbd.rearrange("p (h d) -> p h d", h=8), rep(ps[7][0:120, DH:2 * DH], 8),
                                          rep_last(bdmask[0:120, :], DH), ALU.mult))
                elif k == 3:
                    dve.wait_ge(cmp_pe, 3)
                    sc = csc.rearrange("p (a j g n) -> p a j g n", a=2, j=4, g=2)
                    src = ps[7][:, 0:240].rearrange("p (a j g n) -> p a j g n", a=2, j=4, g=2)
                    first = 2 * 16 - 1
                    bias = T8[:, 8:16, :].rearrange("p (g j) k -> p j g k", g=2)
                    cstep(v.tensor_tensor(sc[:, 0, :, :, 0:7], src[:, 0, :, :, 0:7],
                                          bias[:, :, :, P + first::16], ALU.add))
                    cstep(v.tensor_tensor(sc[:, 1], src[:, 1], bias[:, :, :, first::16], ALU.add))
                    sc3 = csc.rearrange("p (h n) -> p h n", n=N_CMP)
                    cstep(v.tensor_reduce(cmp_m, sc3, AX.X, ALU.max))
                    cstep(v.tensor_tensor(sc3, sc3, rep_last(cmp_m, N_CMP), ALU.subtract))
                elif k == 4:
                    dve.wait_ge(cmp_a, 2)
                    sc3 = csc.rearrange("p (h n) -> p h n", n=N_CMP)
                    cstep(v.tensor_reduce(cmp_s, sc3, AX.X, ALU.add))
                    cstep(v.reciprocal(cmp_c, cmp_s))
                    gate = gates[:, :, 0:8].rearrange("p a (g j) -> p a j g", g=2)
                    c4 = cmp_c.rearrange("p (a j g) -> p a j g", a=2, j=4)
                    dve.wait_ge(gates_made, 1)
                    cstep(v.tensor_tensor(c4, c4, gate, ALU.mult))
                    cstep(v.tensor_scalar(cmp_c[:, 0:8], cmp_c[:, 0:8], rowvalid, None, ALU.mult))
                elif k == 5:
                    dve.wait_ge(cmp_pe, 4)
                    cstep(copy(cPT, ps[7][0:120, 0:2 * P].rearrange("p (a q) -> p a q", a=2)))
                else:
                    qt = k - 6
                    dve.wait_ge(cmp_pe, 5 + qt)
                    cstep(v.tensor_tensor(ctmp.rearrange("p (h d) -> p h d", h=8),
                                          ps[7][:, :].rearrange("p (h d) -> p h d", h=8),
                                          rep_last(cmp_c[:, 8 * qt:8 * qt + 8], DH), ALU.mult))
                    dst = mix[:, qt, HALF:D].rearrange("p (g j d) -> p j g d", g=2, j=4)
                    cstep(v.tensor_tensor(dst, dst, ctmp.rearrange("p (j g d) -> p j g d", j=4, g=2), ALU.add))

            CMP_AT = {2: 0, 4: 1, 5: 2, 6: 3, 8: 4, 10: 5, 12: 6, 13: 7}
            n0 = len(units0)
            for i in range(n0 + 2):
                if i < n0:
                    bias_scores(at[0], units0, i)
                if 1 <= i <= n0:
                    pt_copy(at[0], units0, i - 1)
                if i >= 2:
                    mix_out(at[0], units0, i - 2)
                if i in CMP_AT:
                    cmp_step(CMP_AT[i])

            def out_add(i, sems, need, banks=4):
                for tt in range(TT):
                    for half in range(2):
                        n = 2 * tt + half
                        dve.wait_ge(sems, need(n))
                        dst = x[:, tt, half * HALF:(half + 1) * HALF]
                        link(v.scalar_tensor_tensor(out=dst, in0=dst, scalar=ALPHA, in1=ps[banks + n][:, :],
                                                    op0=ALU.mult, op1=ALU.add))

            def layer_norm(i, z):
                for tt in range(TT):
                    for half in range(2):
                        link(v.bn_stats(bnst[:, tt, half, :], z[:, tt, half * HALF:(half + 1) * HALF]))
                    link(v.bn_aggr(mv[:, tt, :], bnst[:, tt, :, :]))
                v.tensor_scalar(rstd, mv[:, :, 1], EPS, None, ALU.add).then_inc(lnx[i]["var"], 1)
                dve.wait_ge(lnx[i]["sd"], 1)
                link(v.reciprocal(rstd, rstd))
                dve.wait_ge(ld_lnp, 32 * (i + 1))
                for tt in range(TT):
                    link(v.tensor_scalar(z[:, tt, :], z[:, tt, :], mv[:, tt, 0:1], rstd[:, tt:tt + 1],
                                         ALU.subtract, ALU.mult))
                    link(v.tensor_tensor(z[:, tt, :], z[:, tt, :], lnp[:, 0, :], ALU.mult))
                    v.tensor_tensor(z[:, tt, :], z[:, tt, :], lnp[:, 1, :], ALU.add).then_inc(lnx[i]["x"], 1)

            for j in (0, 2):
                copy_tr(dve, copy, 1, j, tr[1]["v"])
            out_add(0, outp[0], lambda n: n + 1)
            layer_norm(0, x)
            def low(dst, src, hi):
                return v.tensor_tensor(dst, src, hi.bitcast(F32), ALU.subtract)

            for j in range(4):
                dve.wait_ge(xT_hi, j + 1)
                low(xTl[:, 2 * j:2 * j + 2, :], ps[j][:, :].rearrange("p (k s) -> p k s", k=2),
                    xTh[:, 2 * j:2 * j + 2, :]).then_inc(xT_lo, 1)

            def lo_up(slot, hi, h, count):
                dve.wait_ge(hi_made, count)
                cols = slice(h * DN, (h + 1) * DN)
                low(gu_lo[slot][:, cols], gu[slot][:, cols], hi[:, :]).then_inc(lo_made, 1)

            def lo_dn(slot, which, buf, count):
                dve.wait_ge(hi_made, count)
                low(dn_lo[slot][:, :], dn[slot][:, :], dn_hi[which][:, buf * DN:(buf + 1) * DN]).then_inc(lo_made, 1)

            def ffn_hTl_step(q):
                dve.wait_ge(ffn_hTh, q + 1)
                low(hTl[:, q % 2, :, :], ps[3][:, 0:2 * P].rearrange("p (s q) -> p s q", s=2),
                    hTh[:, q % 2, :, :]).then_inc(ffn_hTl, 1)

            def ffn_h_step(q):
                dve.wait_ge(ffn_silu, q + 1)
                if q >= 2:
                    dve.wait_ge(ffn_t, q - 1)
                v.tensor_tensor(hh[:, q % 2, :], sg[:, q % 2, :], ps[q % 3][:, FC:2 * FC], ALU.mult)\
                    .then_inc(ffn_h, 1)

            lo_up(0, ffn_up_hi[0], 0, ffn_up_part(0, 0))
            lo_up(0, ffn_up_hi[1], 1, ffn_up_part(0, 1))
            for q in range(2 * NC):
                c, tt = q // 2, q % 2
                if tt and c + 1 < NC:
                    lo_up((c + 1) % 2, ffn_up_hi[0], 0, ffn_up_part(c + 1, 0))
                if q >= 1:
                    ffn_hTl_step(q - 1)
                if tt and c + 1 < NC:
                    lo_up((c + 1) % 2, ffn_up_hi[1], 1, ffn_up_part(c + 1, 1))
                ffn_h_step(q)
                if tt == 0:
                    lo_dn(c % RING, 0, c % 2, ffn_dn_part(c))
            ffn_hTl_step(2 * NC - 1)
            dve.wait_ge(lnx[0]["x"], TT)
            out_add(1, dn_used, lambda n: NC)
            layer_norm(1, x)
            for j in (0, 2):
                copy_tr(dve, copy, 2, j, tr[2]["v"])
            for j in range(0, NP1, 2):
                copy_p1(dve, copy, j, pr_v)
            dve.wait_ge(pr_v, v_jobs(NP1))
            dve.wait_ge(pr_a, a_jobs(NP1))
            for qt in range(TT):
                wk = P * (qt + 1)
                sc = score[:, qt, 0:wk]
                for i in range(4):
                    n = 4 * qt + i
                    dve.wait_ge(idx_relu, n + 1)
                    for r in range(2):
                        h = i + 4 * r
                        src, w = relu[:, n % 2, r, 0:wk], wi[:, qt, h:h + 1]
                        if i == 0 and r == 0:
                            ins = v.tensor_scalar(sc, src, w, None, ALU.mult)
                        else:
                            ins = v.scalar_tensor_tensor(out=sc, in0=src, scalar=w, in1=sc, op0=ALU.mult,
                                                         op1=ALU.add)
                        ins.then_inc(idx_acc, 1)
                        dve.wait_ge(idx_acc, 2 * n + r + 1)
            for qt in range(TT):
                wk = P * (qt + 1)
                sc = score[:, qt, 0:wk]
                dve.wait_ge(idx_causal, qt + 1)
                for _ in range(TOPK // 8):
                    link(v.max(m8, sc))
                    link(v.match_replace(sc, m8, sc, TAKEN))
                v.tensor_scalar(sel[:, qt, 0:wk], sc, -2e38, INV_SCALE * NEG, ALU.is_gt, ALU.mult).then_inc(idx_sel, 1)
            n1 = len(units1)
            for i in range(n1 + 2):
                if i < n1:
                    bias_scores(at[1], units1, i)
                if 1 <= i <= n1:
                    pt_copy(at[1], units1, i - 1)
                if i >= 2:
                    mix_out(at[1], units1, i - 2)
            for j in (0, 2):
                copy_tr(dve, copy, 3, j, tr[3]["v"])
            dve.wait_ge(lnx[1]["x"], TT)
            out_add(2, outp[1], lambda n: n + 1)
            layer_norm(2, x)
            for j in (0, 2):
                copy_tr(dve, copy, 4, j, tr[4]["v"])
            dve.wait_ge(outp[1], 4)
            dve.wait_ge(lnx[2]["x"], TT)
            v.memset(ones, 1.0).then_inc(moe_ones, 1)
            for tt in range(TT):
                for half in range(2):
                    cols = slice(half * HALF, (half + 1) * HALF)
                    v.tensor_scalar(y[:, tt, cols], x[:, tt, cols], ALPHA, None, ALU.mult).then_inc(y_added, 1)
            dve.wait_ge(logits_pe, 1)
            link(copy(mask, ps[4][:, 0:16].rearrange("p (a e) -> p a e", a=2)))
            for tt in range(TT):
                lg = mask[:, tt, :]
                other, own = rep(lg, 8), rep_last(lg, 8)
                r8 = rt[:, 2 * tt, 0:64].rearrange("p (a b) -> p a b", b=8)
                e8 = rt[:, 2 * tt + 1, 0:64].rearrange("p (a b) -> p a b", b=8)
                link(v.tensor_tensor(r8, other, own, ALU.is_gt))
                link(v.tensor_tensor(e8, other, own, ALU.is_equal))
                link(v.tensor_tensor(e8, e8, tri8, ALU.mult))
                link(v.tensor_tensor(r8, r8, e8, ALU.add))
                link(v.tensor_reduce(rank[:, tt, 0:1], lg, AX.X, ALU.max))
                link(v.tensor_scalar(rank[:, tt, 0:1], rank[:, tt, 0:1], -1.0, None, ALU.mult))
                copy(comb[:, tt, :], lg).then_inc(logits_v, 1)
                dve.wait_ge(route_exp, tt + 1)
                link(v.tensor_reduce(rank[:, tt, :], r8, AX.X, ALU.add))
                link(v.tensor_scalar(mask[:, tt, :], rank[:, tt, :], 1.5, None, ALU.is_lt))
                link(v.tensor_tensor(comb[:, tt, :], comb[:, tt, :], mask[:, tt, :], ALU.mult))
                s1 = rt[:, 2 * tt, 64:65]
                link(v.tensor_reduce(s1, comb[:, tt, :], AX.X, ALU.add))
                link(v.reciprocal(s1, s1))
                v.tensor_scalar(comb[:, tt, :], comb[:, tt, :], s1, None, ALU.mult).then_inc(mask_made, 1)
            dve.wait_ge(mask_made, 2)
            dve.wait_ge(rank_pe, 1)
            link(copy(rank, ps[5][:, 0:16].rearrange("p (a e) -> p a e", a=2)))
            cnt = rt[:, 0, 66:67]
            link(v.tensor_reduce(cnt, ps[5][:, 16:24], AX.X, ALU.max))
            copy(overflow[:, :], cnt).then_inc(route_done, 1)

            def make_picks(e, base):
                col = slice(e, e + 1) if isinstance(e, int) else bass.ds(e, 1)
                for tt in range(TT):
                    v.tensor_scalar(pick[:, tt, :], iota[:, base:base + P], rank[:, tt, col], mask[:, tt, col],
                                    ALU.is_equal, ALU.mult).then_inc(pick_made, 1)

            def moe_lo_up(e, q, h):
                lo_up(UP_SLOT[q % NC], moe_up_hi[HI_BUF[2 * (q % NC) + h]], h, moe_up_part(e, q, h))

            def moe_lo_dn(e, q, last=False):
                lo_dn(DN_SLOT[q % NC], 1, q % NC % 2, moe_dn_part(e, q, last))

            def moe_hTl_step(e, q):
                dve.wait_ge(moe_hTh, NC * e + q + 1)
                low(hTl[:, q % NC % 2, :, :], ps[2][:, 0:2 * P].rearrange("p (s q) -> p s q", s=2),
                    hTh[:, q % NC % 2, :, :]).then_inc(moe_hTl, 1)

            def moe_h_step(e, q):
                c = q % NC
                dve.wait_ge(moe_silu, NC * e + q + 1)
                wait_for_chunks(dve, moe_t, moe_buffer_chunks(e, q))
                v.tensor_tensor(hh[:, c % 2, :], sg[:, c % 2, :], ps[3 if c == 0 else c % 2][:, FC:2 * FC],
                                ALU.mult).then_inc(moe_h, 1)

            def take_xg(e):
                for i in range(2):
                    dve.wait_ge(xg_a, 2 * e + i + 1)
                    low(xgl[:, 4 * i:4 * i + 4, :], ps[6 + i][:, :].rearrange("p (k q) -> p k q", k=4),
                        xgh[:, 4 * i:4 * i + 4, :]).then_inc(xg_v, 1)

            def take_ye(e):
                for half in range(2):
                    dve.wait_ge(ye_a, 2 * e + half + 1)
                    cols = slice(half * HALF, (half + 1) * HALF)
                    low(yel[:, cols], ps[4 + half][:, :], yeh[:, cols]).then_inc(ye_v, 1)

            def add_scattered(e, ex):
                col = slice(ex, ex + 1) if isinstance(ex, int) else bass.ds(ex, 1)
                for n, bank in enumerate((6, 7, 4, 5)):
                    tt, half = n // 2, n % 2
                    dve.wait_ge(scattered, 4 * e + n + 1)
                    dst = y[:, tt, half * HALF:(half + 1) * HALF]
                    v.scalar_tensor_tensor(out=dst, in0=ps[bank][:, :], scalar=comb[:, tt, col], in1=dst,
                                           op0=ALU.mult, op1=ALU.add).then_inc(y_added, 1)

            def expert(e, ex, base, last):
                for q in range(2, NC + 2):
                    up, more = q < NC or not last, q < NC - 1 or not last
                    if q == NC + 1:
                        take_ye(e)
                    if up or q == NC:
                        moe_lo_dn(e, q - 1, last)
                    if more:
                        moe_lo_up(e, q + 1, 0)
                    if up or q == NC:
                        moe_hTl_step(e, q - 1)
                    if q == NC - 1 and not last:
                        take_xg(e + 1)
                    if more:
                        moe_lo_up(e, q + 1, 1)
                    if up:
                        moe_h_step(e, q)
                    if q == 5 and not last:
                        dve.wait_ge(pickT_pe, e + 1)
                        make_picks(ex + 1, base)
                dve.wait_ge(y_added, 4 * e + 4)
                add_scattered(e, ex)

            def moe_pass(n):
                base = P * n
                first = NE * n
                made = moe_parts(first) - 7
                make_picks(0, base)
                lo_up(0, moe_up_hi[HI_BUF[0]], 0, made + 1)
                lo_up(0, moe_up_hi[HI_BUF[1]], 1, made + 2)
                take_xg(first)
                lo_up(1, moe_up_hi[HI_BUF[2]], 0, made + 3)
                lo_up(1, moe_up_hi[HI_BUF[3]], 1, made + 4)
                moe_h_step(first, 0)
                moe_lo_dn(first, 0)
                moe_lo_up(first, 2, 0)
                moe_hTl_step(first, 0)
                moe_lo_up(first, 2, 1)
                moe_h_step(first, 1)
                with dve.Fori(0, NE - 1) as e:
                    expert(e + first if n else e, e, base, False)
                expert(first + NE - 1, NE - 1, base, True)
                dve.wait_ge(y_added, 4 * NE * (n + 1) + 4)

            for tt in range(TT):
                dve.wait_ge(x_hi, tt + 1)
                low(xl[:, tt, :], x[:, tt, :], xh[:, tt, :]).then_inc(x_lo, 1)
            dve.wait_ge(vec_step, steps[0])
            moe_pass(0)
            dve.wait_ge(route_done, 1)
            over = dve.value_load(overflow[0:1, 0:1], min_val=0, max_val=S)
            with dve.If(over > CAP):
                moe_pass(1)
            layer_norm(3, y)

        @block.tensor
        def _(pe):
            mm = nc.tensor.matmul

            def over_k(dst, lhsT, rhs):
                for k in range(KD):
                    last = mm(dst, lhsT(k), rhs(k), start=(k == 0), stop=(k == KD - 1))
                return last

            def transposes(i, src):
                for j in range(4):
                    for kk in range(2):
                        for tt in range(TT):
                            n = 2 * kk + tt
                            last = nc.tensor.transpose(ps[j][:, n * P:(n + 1) * P],
                                                       src[:, tt, (2 * j + kk) * P:(2 * j + kk + 1) * P], ident)
                    last.then_inc(tr[i]["pe"], 1)

            pe.wait_ge(ld_cst, 16)
            seen = set()
            for j, job in enumerate(front):
                kind, bank = job[0], ps[j % 8]
                if j >= 8:
                    pe.wait_ge(front_v if j % 2 == 0 else front_a, (j - 8) // 2 + 1)
                if kind in ("colsA", "cols", "dup", "v") and "xT" not in seen:
                    seen.add("xT")
                    pe.wait_ge(front_v, v_jobs(6))
                    pe.wait_ge(front_a, a_jobs(6))
                piece = job[-1] if kind in ("colsA", "cols", "dup") else 3 if kind == "v" else None
                if piece is not None and piece not in seen:
                    seen.add(piece)
                    pe.wait_ge(ld_win[piece], 32 if piece == 2 else 16)
                if kind == "rvec":
                    pe.wait_ge(ld_vec, 48)
                    last = mm(bank[0:16, 0:VEC], relb, onehot, start=True, stop=True)
                elif kind == "pos":
                    pe.wait_ge(ld_pos, 32)
                    for n in range(2):
                        last = nc.tensor.transpose(bank[:, 16 * n:16 * n + 16], posrow[:, P * n:P * n + P],
                                                   ident[0:16, 0:16])
                elif kind == "xT":
                    pe.wait_ge(ld_x, 16)
                    for kk in range(2):
                        for tt in range(TT):
                            n = 2 * kk + tt
                            last = nc.tensor.transpose(bank[:, n * P:(n + 1) * P],
                                                       x[:, tt, (2 * job[1] + kk) * P:(2 * job[1] + kk + 1) * P],
                                                       ident)
                elif kind in ("colsA", "cols"):
                    c = job[-2]
                    last = over_k(bank[:, 0:S], lambda k: w_in0[:, k, c:c + P], lambda k: xT[:, k, :])
                elif kind == "dup":
                    c = P * job[3]
                    last = over_k(bank[:, 0:S], lambda k: w_cmp[k // 4][:, k % 4, c:c + P], lambda k: xT[:, k, :])
                elif kind == "v":
                    tt = job[1]
                    for at_col, c, n in ((0, VA0, P), (P, VS0, P), (2 * P, VW0, P + 24)):
                        last = over_k(bank[:, at_col:at_col + n], lambda k: xT[:, k, tt * P:(tt + 1) * P],
                                      lambda k: w_in0[:, k, c:c + n])
                elif kind == "flip":
                    pe.wait_ge(ld_flat, 16)
                    last = mm(bank[:, :], flip, flat_T[:, 2 * job[1]:2 * job[1] + 2, :], start=True, stop=True)
                last.then_inc(front_pe, 1)
            pe.wait_ge(front_v, v_jobs(NF))
            pe.wait_ge(front_a, a_jobs(NF))

            def scores(a, units, i):
                kind, qt, g = units[i]
                wk = P * (qt + 1)
                if i >= 2:
                    pe.wait_ge(a["biased"], 4 * (i - 1))
                order = (0, 2, 1, 3) if kind == "C" else range(4)
                for s in order:
                    h = heads_of(units[i])[s]
                    if kind == "C":
                        r = slice(DH * (h % 2), DH * (h % 2) + DH)
                        q, k = qbuf[r, h // 2, qt * P:(qt + 1) * P], kT1[r, 0:wk]
                    else:
                        r = slice(DH * g, DH * g + DH)
                        q = (qaT if kind == "A" else qbT)[r, s, qt * P:(qt + 1) * P]
                        k = {"A": kaT, "S": ksT, "W": kwT}[kind][r, 0:wk]
                    last = mm(ps[2 * (i % 2) + s // 2][:, (s % 2) * S:(s % 2) * S + wk], q, k, start=True, stop=True)
                last.then_inc(a["scores"], 1)

            def turn(a, units, i):
                u = units[i]
                pe.wait_ge(a["exp"], 4 * (i + 1))
                if i >= 1:
                    pe.wait_ge(a["pt_v"], i)
                    pe.wait_ge(a["pt_a"], i)
                for s in range(4):
                    for kt in range(u[1] + 1):
                        n = 2 * (s % 2) + kt
                        last = nc.tensor.transpose(ps[4 + s // 2][:, n * P:(n + 1) * P],
                                                   unit_p(u, i)[:, s, kt * P:(kt + 1) * P], ident)
                last.then_inc(a["pt"], 1)

            def sum_values(a, units, i):
                kind, qt, g = units[i]
                pe.wait_ge(a["pt_v"], i + 1)
                pe.wait_ge(a["pt_a"], i + 1)
                if i >= 1:
                    pe.wait_ge(a["o_out"], i)
                for s in range(4):
                    for kt in range(qt + 1):
                        vv = v1[:, kt, :] if kind == "C" else \
                            {"A": va, "S": vs, "W": vw}[kind][:, kt, DH * g:DH * g + DH]
                        last = mm(ps[6][:, s * DH:(s + 1) * DH], pT[:, i % 2, s, kt, :], vv,
                                  start=(kt == 0), stop=(kt == qt))
                last.then_inc(a["o"], 1)

            def compressed(k):
                if k == 0:
                    pe.wait_ge(blk_made, 8)
                    pe.wait_ge(ld_w1, 32)
                    for kv in range(2):
                        for f in range(2):
                            n = 30 * (2 * kv + f)
                            for i in range(CMP_PAIRS):
                                last = mm(ps[7][:, n:n + 30], (w1k, w1v)[kv][:, i, f * P:(f + 1) * P],
                                          blk[:, kv, i, :], start=(i == 0), stop=(i == CMP_PAIRS - 1))
                elif k == 1:
                    pe.wait_ge(cmp_v, CMP_DONE["gelu"])
                    pe.wait_ge(ld_w2, 48)
                    hid = gel[:, 5, :].rearrange("p (v f n) -> p v f n", v=2, f=2)
                    for f in range(2):
                        mm(ps[7][:, 0:30], w2k[:, f, :], hid[:, 0, f, :], start=(f == 0), stop=(f == 1))
                    for f in range(2):
                        last = mm(ps[7][0:120, DH:2 * DH], hidv[:, f, :], w2v[:, f, :],
                                  start=(f == 0), stop=(f == 1))
                elif k == 2:
                    pe.wait_ge(cmp_v, CMP_DONE["kv"])
                    for qt in range(TT):
                        for j in range(4):
                            n = 120 * qt + 30 * j
                            last = mm(ps[7][:, n:n + 30], qbT[:, j, qt * P:(qt + 1) * P], kcbd, start=True, stop=True)
                elif k == 3:
                    pe.wait_ge(cmp_a, 2)
                    for qt in range(TT):
                        last = nc.tensor.transpose(ps[7][0:120, qt * P:(qt + 1) * P], csc[:, 120 * qt:120 * qt + 120],
                                                   ident)
                else:
                    qt = k - 4
                    pe.wait_ge(cmp_v, CMP_DONE["taken0" if qt else "turned"])
                    last = mm(ps[7][:, :], cPT[:, qt, :], vcbd, start=True, stop=True)
                last.then_inc(cmp_pe, 1)

            CMP_AT = {1: 0, 4: 1, 5: 2, 8: 3, 11: 4, 12: 5}
            n0 = len(units0)
            for i in range(n0 + 2):
                if i < n0:
                    scores(at[0], units0, i)
                if 1 <= i <= n0:
                    turn(at[0], units0, i - 1)
                if i >= 2:
                    sum_values(at[0], units0, i - 2)
                if i in CMP_AT:
                    compressed(CMP_AT[i])

            def out_proj(i):
                pe.wait_ge(tr[2 * i + 1]["v"], 2)
                pe.wait_ge(tr[2 * i + 1]["a"], 2)
                pe.wait_ge(ld_wout, 16 * (i + 1))
                for tt in range(TT):
                    for half in range(2):
                        over_k(ps[4 + 2 * tt + half][:, :], lambda k: xT[:, k, tt * P:(tt + 1) * P],
                               lambda k: w_out[:, k, half * HALF:(half + 1) * HALF]).then_inc(outp[i], 1)

            pe.wait_ge(cmp_v, CMP_DONE["mixed1"])
            transposes(1, mix)
            out_proj(0)

            pe.wait_ge(lnx[0]["x"], TT)
            transposes(0, x)
            pe.wait_ge(xT_lo, 4)

            def three(dst, a_hi, a_lo, b_hi, b_lo, start, stop):
                mm(dst, a_hi, b_hi, start=start, stop=False)
                mm(dst, a_hi, b_lo, start=False, stop=False)
                return mm(dst, a_lo, b_hi, start=False, stop=stop)

            def up_products(dst, a_hi, a_lo, high, slot, need, used):
                for h in range(2):
                    if need is not None:
                        pe.wait_ge(lo_made, need[h])
                    for k in range(4 * h, 4 * h + 4):
                        last = three(dst, a_hi(k), a_lo(k), high[h][:, k % 4 * HALF:(k % 4 + 1) * HALF],
                                     gu_lo[slot][:, k * HALF:(k + 1) * HALF],
                                     k == 0, k == KD - 1)
                    if used[h] is not None:
                        last.then_inc(used[h], 1)

            def down_products(banks, buf, which, buf_dn, slot, first, final):
                for s in range(2):
                    for half in range(2):
                        c = s * D + half * HALF
                        last = three(ps[banks + half][:, :], hTh[:, buf, s, :], hTl[:, buf, s, :],
                                     dn_hi[which][:, buf_dn * DN + c:buf_dn * DN + c + HALF],
                                     dn_lo[slot][:, c:c + HALF], first and s == 0, final and s == 1)
                return last

            def ffn_up(q):
                c, tt = q // 2, q % 2
                if q >= 3:
                    pe.wait_ge(ffn_h, q - 2)
                up_products(ps[q % 3][:, :], lambda k: xTh[:, k, tt * P:(tt + 1) * P],
                            lambda k: xTl[:, k, tt * P:(tt + 1) * P], ffn_up_hi, c % 2,
                            None if tt else [ffn_up_part(c, 0), ffn_up_part(c, 1)],
                            [gu_first_used, gu_used] if tt else [None, ffn_g0])

            def ffn_turn(q):
                pe.wait_ge(ffn_h, q + 1)
                if q >= 1:
                    pe.wait_ge(ffn_hTl, q)
                for s in range(2):
                    last = nc.tensor.transpose(ps[3][:, s * P:(s + 1) * P], hh[:, q % 2, s * P:(s + 1) * P], ident)
                last.then_inc(ffn_t, 1)

            def ffn_down(q):
                c, tt = q // 2, q % 2
                pe.wait_ge(ffn_hTl, q + 1)
                if tt == 0:
                    pe.wait_ge(lo_made, ffn_dn_part(c))
                last = down_products(4 + 2 * tt, q % 2, 0, c % 2, c % RING, c == 0, c == NC - 1)
                if tt:
                    last.then_inc(dn_used, 1)

            for q in range(2 * NC + 2):
                if q < 2 * NC:
                    ffn_up(q)
                if 1 <= q <= 2 * NC:
                    ffn_turn(q - 1)
                if q >= 2:
                    ffn_down(q - 2)

            pe.wait_ge(lnx[1]["x"], TT)
            transposes(2, x)
            pe.wait_ge(tr[2]["v"], 2)
            pe.wait_ge(tr[2]["a"], 2)
            pe.wait_ge(ld_win1, 16)
            for j, job in enumerate(proj1):
                bank = ps[j % 8]
                if j >= 8:
                    pe.wait_ge(pr_v if j % 2 == 0 else pr_a, (j - 8) // 2 + 1)
                if job[0] == "v":
                    tt = job[1]
                    for at_col, c, n in ((0, V1, DH), (DH, WI1, 8)):
                        last = over_k(bank[:, at_col:at_col + n], lambda k: xT[:, k, tt * P:(tt + 1) * P],
                                      lambda k: w_in1[:, k, c:c + n])
                else:
                    if job[0] == "q":
                        def lhsT(k):
                            return w_in1[:, k, job[1] * P:(job[1] + 1) * P]
                    elif job[0] == "k":
                        def lhsT(k):
                            return w_in1[:, k, K1:K1 + P]
                    elif job[0] == "qi":
                        def lhsT(k):
                            return w_in1[:, k, QI1 + job[1] * P:QI1 + (job[1] + 1) * P]
                    else:
                        def lhsT(k):
                            return w_in1[:, k, KI1:KI1 + P]
                    last = over_k(bank[:, 0:S], lhsT, lambda k: xT[:, k, :])
                last.then_inc(pr_pe, 1)
            pe.wait_ge(pr_v, v_jobs(NP1))
            pe.wait_ge(pr_a, a_jobs(NP1))
            for qt in range(TT):
                wk = P * (qt + 1)
                if qt:
                    pe.wait_ge(idx_relu, 4)
                for h in range(8):
                    r = slice(32 * (h % 4), 32 * (h % 4) + 32)
                    last = mm(ps[h % 4][:, (h // 4) * S:(h // 4) * S + wk], qiT[r, h // 4, qt * P:(qt + 1) * P],
                              kiT[r, 0:wk], start=True, stop=True)
                last.then_inc(idx_pe, 1)
            pe.wait_ge(idx_relu, 8)
            n1 = len(units1)
            for i in range(n1 + 2):
                if i < n1:
                    scores(at[1], units1, i)
                if 1 <= i <= n1:
                    turn(at[1], units1, i - 1)
                if i >= 2:
                    sum_values(at[1], units1, i - 2)
            pe.wait_ge(at[1]["o_out"], n1)
            transposes(3, mix)
            out_proj(1)

            pe.wait_ge(lnx[2]["x"], TT)
            transposes(4, x)
            pe.wait_ge(tr[4]["v"], 2)
            pe.wait_ge(tr[4]["a"], 2)
            pe.wait_ge(ld_wr, 16)
            for tt in range(TT):
                last = over_k(ps[4][:, 8 * tt:8 * tt + 8], lambda k: xT[:, k, tt * P:(tt + 1) * P],
                              lambda k: wr[:, k, :])
            last.then_inc(logits_pe, 1)
            pe.wait_ge(mask_made, 2)
            pe.wait_ge(moe_ones, 1)
            mm(ps[5][:, 0:8], upper, mask[:, 0, :], start=True, stop=True)
            mm(ps[5][:, 8:16], ones, mask[:, 0, :], start=True, stop=False)
            mm(ps[5][:, 8:16], upper, mask[:, 1, :], start=False, stop=True)
            mm(ps[5][:, 16:24], ones, mask[:, 0, :], start=True, stop=False)
            mm(ps[5][:, 16:24], ones, mask[:, 1, :], start=False, stop=True).then_inc(rank_pe, 1)

            def moe_up(e, q, need):
                c = q % NC
                up_products(ps[3 if c == 0 else c % 2][:, :], lambda k: xgh[:, k, :], lambda k: xgl[:, k, :],
                            [moe_up_hi[HI_BUF[2 * c + h]] for h in range(2)], UP_SLOT[c], need, [gu_first_used, gu_used])

            def moe_turn(e, q):
                pe.wait_ge(moe_h, NC * e + q + 1)
                wait_for_chunks(pe, moe_hTl, NC * e + q)
                for s in range(2):
                    last = nc.tensor.transpose(ps[2][:, s * P:(s + 1) * P], hh[:, q % NC % 2, s * P:(s + 1) * P],
                                               ident)
                last.then_inc(moe_t, 1)

            def moe_down(e, q, last):
                if q == 0:
                    pe.wait_ge(y_added, 4 * e + 4)
                pe.wait_ge(moe_hTl, NC * e + q + 1)
                pe.wait_ge(lo_made, moe_dn_part(e, q, last))
                down_products(4, q % 2, 1, q % 2, DN_SLOT[q], q == 0, q == NC - 1).then_inc(dn_used, 1)

            def gather(e):
                pe.wait_ge(pick_made, 2 * e + 2)
                for k in range(KD):
                    for tt in range(TT):
                        for src in (xh, xl):
                            last = mm(ps[6 + k // 4][:, (k % 4) * P:(k % 4 + 1) * P],
                                      src[:, tt, k * P:(k + 1) * P], pick[:, tt, :],
                                      start=(tt == 0 and src is xh), stop=(tt == TT - 1 and src is xl))
                last.then_inc(gathered, 1)

            def turn_picks(e):
                for tt in range(TT):
                    last = nc.tensor.transpose(ps[3][:, tt * P:(tt + 1) * P], pick[:, tt, :].bitcast(F32), ident)
                last.then_inc(pickT_pe, 1)

            def scatter(e):
                pe.wait_ge(pickT_a, e + 1)
                for n, bank in enumerate((6, 7, 4, 5)):
                    tt, half = n // 2, n % 2
                    if n < 2:
                        pe.wait_ge(ye_v, 2 * e + half + 1)
                    cols = slice(half * HALF, (half + 1) * HALF)
                    mm(ps[bank][:, :], pickT[:, tt, :], yeh[:, cols], start=True, stop=False)
                    mm(ps[bank][:, :], pickT[:, tt, :], yel[:, cols], start=False, stop=True)\
                        .then_inc(scattered, 1)

            def expert(e, last):
                for q in range(2, NC + 2):
                    up = q < NC or not last
                    if q == NC + 1:
                        moe_down(e, NC - 1, last)
                    if q == NC and not last:
                        pe.wait_ge(xg_v, 2 * e + 4)
                        pe.wait_ge(pickT_a, e + 1)
                    if up:
                        moe_up(e, q, [moe_up_part(e, q, h) for h in range(2)])
                    if up or q == NC:
                        moe_turn(e, q - 1)
                    if q <= NC:
                        moe_down(e, q - 2, last)
                    if q == 3:
                        turn_picks(e)
                    if q == 7 and not last:
                        gather(e + 1)
                scatter(e)

            def moe_pass(n):
                first = NE * n
                made = moe_parts(first) - 7
                pe.wait_ge(y_added, 4 * first + 4)
                if n == 0:
                    pe.wait_ge(x_lo, TT)
                gather(first)
                pe.wait_ge(xg_v, 2 * first + 2)
                moe_up(first, 0, [made + 1, made + 2])
                moe_up(first, 1, [made + 3, made + 4])
                moe_turn(first, 0)
                with pe.Fori(first, first + NE - 1) as e:
                    expert(e, False)
                expert(first + NE - 1, True)

            moe_pass(0)
            pe.wait_ge(route_done, 1)
            over = pe.value_load(overflow[0:1, 0:1], min_val=0, max_val=S)
            with pe.If(over > CAP):
                moe_pass(1)


def constants():
    c = np.zeros((P, C_COLS), np.float32)
    i = np.arange(P)
    c[:, C_ID:C_ID + P] = np.eye(P)
    c[:, C_FLIP:C_FLIP + P] = np.eye(P)[::-1]
    c[:, C_UP:C_UP + P] = i[:, None] < i[None, :]
    c[:, C_IOTA:C_IOTA + S] = np.arange(S)
    c[:, C_TRI:C_TRI + 64] = (np.arange(8)[None, :] < np.arange(8)[:, None]).reshape(-1)
    c[:, C_ROW] = i >= 31
    c[:, C_BD:C_BD + 8] = (i[:, None] // N_CMP) == np.arange(8)[None, :]
    return c


def bias_vectors():
    dist = S - 1 - np.arange(VEC)
    n = np.maximum(dist, 0)
    large = NB // 2 + (np.log(np.maximum(n, 1).astype(np.float32) / np.float32(NB // 2))
                       / np.float32(math.log(MAXDIST / (NB // 2))) * (NB - NB // 2)).astype(np.int32)
    bucket = np.where(n < NB // 2, n, np.minimum(large, NB - 1))
    v = np.zeros((NB, 2 * VEC), np.float32)
    v[:, 0:VEC] = (bucket[None, :] == np.arange(NB)[:, None]) & (dist >= 0)[None, :]
    v[0:16, VEC:2 * VEC] = np.where(dist >= 0, 0.0, INV_SCALE * NEG)
    return v


def laid_out(a):
    w0 = a.pop("l0_w_in")
    cuts = np.cumsum([512, 128, 128, 512, 128, 128, 128, 128, 128, 128])
    qa, ka, va, qb, kc, vc, ks, vs, kw, vw, g = np.split(w0, cuts, axis=1)

    def by_pair(q):
        return q.reshape(D, 2, 4, DH).transpose(0, 2, 1, 3).reshape(D, 8 * DH)

    a["l0_w_in"] = np.concatenate([by_pair(qa), ka, va, by_pair(qb), ks, vs, kw, vw, g], axis=1)
    a["l0_w_cmp"] = np.concatenate([c[:, DH * i:DH * i + DH] for c in (kc, vc) for i in (0, 0, 1, 1)], axis=1)
    a["l0_cmpk_w2"] = np.concatenate([a["l0_cmpk_w2"]] * 2, axis=1)
    q, k, v, qi, ki, wi = np.split(a["l1_w_in"], np.cumsum([D, DH, DH, 256, 32]), axis=1)
    a["l1_w_in"] = np.concatenate([q, k, k, v, qi, ki, ki, ki, ki, wi], axis=1)

    def up_chunks(gate, up):
        both = np.stack([w.reshape(*w.shape[:-2], KD, P, NC, FC) for w in (gate, up)], axis=-2)
        n = both.ndim
        order = list(range(n - 5)) + [n - 3, n - 4, n - 5, n - 2, n - 1]
        return np.ascontiguousarray(both.transpose(order)).reshape(*gate.shape[:-2], NC, P, GU)

    def down_chunks(w):
        w = w.reshape(*w.shape[:-2], NC, FC // P, P, D)
        return np.ascontiguousarray(np.swapaxes(w, -3, -2)).reshape(*w.shape[:-4], NC, P, DN)

    a["l0_ffn_gate_up"] = up_chunks(a.pop("l0_ffn_gate"), a.pop("l0_ffn_up"))
    a["l1_exp_gate_up"] = up_chunks(a.pop("l1_exp_gate"), a.pop("l1_exp_up"))
    a["l0_ffn_down"] = down_chunks(a["l0_ffn_down"])
    a["l1_exp_down"] = down_chunks(a["l1_exp_down"])
    return {n: np.ascontiguousarray(w) for n, w in a.items()}


def kernel(**inputs):
    import concourse.bacc as bacc
    from concourse.bass_utils import run_bass_kernel_spmd

    nc = bacc.Bacc("TRN2", target_bir_lowering=False, num_devices=1)
    arrays = laid_out({n: np.asarray(a) for n, a in inputs.items()})
    arrays["consts"] = constants()
    arrays["vecs"] = bias_vectors()
    t = {n: nc.dram_tensor(f"in_{n}", a.shape, mybir.dt.from_np(a.dtype), kind="ExternalInput").ap()
         for n, a in arrays.items()}
    out = nc.dram_tensor("out", (1, S, D), F32, kind="ExternalOutput").ap()
    scratch = nc.dram_tensor("bias_rows", (16, VEC), F32, kind="Internal").ap()
    build(nc, t, out, scratch)
    r = run_bass_kernel_spmd(nc, [{f"in_{n}": a for n, a in arrays.items()}], core_ids=[0])
    return r.results[0]["out"]
```

```python
import math
from contextlib import ExitStack

import numpy as np

import concourse.bass as bass
from concourse import mybir

F32 = mybir.dt.float32
F32R = mybir.dt.float32r
I32 = mybir.dt.int32
ALU = mybir.AluOpType
ACT = mybir.ActivationFunctionType
AX = mybir.AxisListType

P = 128
S = 256
TT = S // P
D = 1024
KD = D // P
DH = 64
F = 2816
FC = 256
NC = F // FC
NE = 8
CAP = P
HALF = 512
NB = 32
N_CMP = 15
CMP_HID = 256
CMP_PAIRS = 16
TOPK = S // 4
ALPHA = (2.0 * 2) ** 0.25
EPS = 1e-5
SCALE = DH ** -0.5
INV_SCALE = 8.0
NEG = -1e30
TAKEN = -3e38
MAXDIST = 128

W0_COLS = 1816
QA0, KA0, QB0, KS0, KW0, V0 = 0, 512, 640, 1152, 1280, 1408
W1_COLS = 1608
K1, V1, QI1, KI1 = 1024, 1152, 1224, 1480
W_FLOATS = 16576

RING = 4
UP_SLOT = (0, 1, 2, 3, 0, 1, 2, 0, 3, 1, 2)
HI_BUF = (0, 1, 2, 3) * 4 + (0, 1, 2) * 2
DN_SLOT = tuple(q % RING for q in range(NC))
GU = KD * 2 * FC
DN = (FC // P) * D

C_ID, C_FLIP, C_UP, C_IOTA, C_TRI, C_ROW, C_BD = 0, 128, 256, 384, 640, 704, 705
C_COLS = 713
VEC = 384


def rep(ap, n):
    return bass.AP(ap.tensor, ap.offset, [list(ap.ap[0]), [0, n]] + [list(d) for d in ap.ap[1:]])


def rep_last(ap, n):
    return bass.AP(ap.tensor, ap.offset, [list(d) for d in ap.ap] + [[0, n]])


def to_all(vec, n):
    return bass.AP(vec.tensor, vec.offset, [[0, P], [1, n]])


def loads_up_to(slots, q):
    return slots[:q + 1].count(slots[q])


def chunks_before(slots, block, q, size=NC):
    same = [n for n in range(size) if slots[n] == slots[q]]
    at = same.index(q)
    return size * block + same[at - 1] + 1 if at else size * (block - 1) + same[-1] + 1


def build(nc, t, out, scratch):
    with ExitStack() as ctx:
        def sb(name, shape, dt=F32):
            return ctx.enter_context(nc.sbuf_tensor(name, shape, dt))

        starts = {}

        def area(name, shape):
            made = sb(name, shape)
            starts[name] = nc.sbuf_base - 4 * int(np.prod(shape[1:]))
            return made

        def part(name, over, first, size):
            return nc.alloc_sbuf_tensor_at(name, [P, size], F32R, offset=starts[over] + 4 * first)

        def sem(name):
            return ctx.enter_context(nc.semaphore(name))

        W = area("W", [P, W_FLOATS])
        gu = [area(f"gu{i}", [P, GU]) for i in range(RING)]
        dn = [area(f"dn{i}", [P, DN]) for i in range(RING)]
        T8 = area("T8", [P, 16, S])
        x = area("x", [P, TT, D])
        xT = area("xT", [P, KD, S])
        qbuf = sb("qbuf", [P, 8, S])
        kvbuf = sb("kvbuf", [P, 3, S])
        cst = sb("cst", [P, C_COLS])
        ident = cst[:, C_ID:C_ID + P]
        flip = cst[:, C_FLIP:C_FLIP + P]
        upper = cst[:, C_UP:C_UP + P]
        iota = cst[:, C_IOTA:C_IOTA + S]
        tri8 = cst[:, C_TRI:C_TRI + 64].rearrange("p (a b) -> p a b", b=8)
        rowvalid = cst[:, C_ROW:C_ROW + 1]
        bdmask = cst[:, C_BD:C_BD + 8]
        small = sb("small", [P, 152])
        mx = small[:, 0:8].rearrange("p (a b) -> p a b", b=4)
        neg = small[:, 8:16].rearrange("p (a b) -> p a b", b=4)
        sums = small[:, 136:152].rearrange("p (a b) -> p a b", b=4)
        sk = small[:, 16:24].rearrange("p (a b) -> p a b", b=4)
        ske = small[:, 24:40].rearrange("p (a b) -> p a b", b=4)
        coef = small[:, 40:48].rearrange("p (a b) -> p a b", b=4)
        gates = small[:, 48:96].rearrange("p (a b) -> p a b", b=24)
        sinks = small[:, 96:104]
        bnst = small[:, 104:128].rearrange("p (a b c) -> p a b c", a=2, b=2)
        mv = small[:, 128:132].rearrange("p (a b) -> p a b", b=2)
        rstd = small[:, 132:134]
        wi = sb("wi", [P, TT, 8])
        overflow = sb("overflow", [P, 1], I32)
        route = sb("route", [P, 64])
        comb = route[:, 0:16].rearrange("p (a b) -> p a b", b=8)
        mask = route[:, 16:32].rearrange("p (a b) -> p a b", b=8)
        rank = route[:, 32:48].rearrange("p (a b) -> p a b", b=8)
        cmp_m = route[:, 0:16]
        cmp_s = route[:, 16:32]
        cmp_c = route[:, 32:48]

        ps = [ctx.enter_context(nc.psum_tensor(f"ps{i}", [P, HALF], F32)) for i in range(8)]

        w_in0 = W[:, 0:KD * W0_COLS].rearrange("p (k c) -> p k c", c=W0_COLS)
        w_out = W[:, 0:KD * D].rearrange("p (k c) -> p k c", c=D)
        o = KD * D
        s_sb = W[:, o:o + 4096].rearrange("p (b h k) -> p b h k", b=4, h=4)
        pT = W[:, o + 4096:o + 6144].rearrange("p (b h k q) -> p b h k q", b=2, h=4, k=2)
        mix = W[:, o + 6144:o + 8192].rearrange("p (a d) -> p a d", a=2)
        flat_T = gu[0][:, :].rearrange("p (h k) -> p h k", h=16)
        w1k = gu[2][:, :].rearrange("p (i n) -> p i n", i=CMP_PAIRS)
        w1v = gu[3][:, :].rearrange("p (i n) -> p i n", i=CMP_PAIRS)
        g1 = gu[1]
        onehot = g1[0:NB, 0:VEC]
        negvec = g1[0:16, VEC:2 * VEC]
        rvec = g1[0:16, 2 * VEC:3 * VEC]
        posrow = g1[0:16, 1152:1408]
        vcbd = g1[0:120, 0:512]
        cPT = g1[0:120, 512:768].rearrange("p (a q) -> p a q", a=2)
        ctmp = g1[:, 768:1280]
        hid_rows = ctmp[0:2 * N_CMP, :]
        va = g1[:, 1408:1664].rearrange("p (a d) -> p a d", a=2)
        vs = g1[:, 1664:1920].rearrange("p (a d) -> p a d", a=2)
        vw = g1[:, 1920:2176].rearrange("p (a d) -> p a d", a=2)
        w2k = g1[:, 2176:2432].rearrange("p (f d) -> p f d", f=2)
        w2v = g1[:, 3728:3856].rearrange("p (f d) -> p f d", f=2)
        hidv = g1[:, 3856:4096].rearrange("p (f n) -> p f n", f=2)
        w_cmp = dn[0][:, :].rearrange("p (k c) -> p k c", c=2 * P)
        gel = g1[:, 2432:3152].rearrange("p (a n) -> p a n", n=120)
        kcbd = g1[:, 3152:3182]
        csc = g1[:, 3184:3424]
        otmp = g1[:, 3424:3680]
        pos2 = g1[:, 3680:3712].rearrange("p (v i) -> p v i", v=2)
        relb = g1[0:NB, 3712:3728]
        T8a = dn[2][:, :].rearrange("p (h k) -> p h k", h=8)
        kt2 = dn[3][:, 0:1024].rearrange("p (v g s) -> p v g s", v=2, g=2)
        blk = dn[3][:, 1024:1984].rearrange("p (v i n) -> p v i n", v=2, i=CMP_PAIRS)
        qaT, qbT = qbuf[:, 0:4, :], qbuf[:, 4:8, :]
        kaT, ksT, kwT = kvbuf[:, 0, :], kvbuf[:, 1, :], kvbuf[:, 2, :]
        lnp = qbuf[:, :, :].rearrange("p (a h) s -> p a (h s)", a=2)
        sg = kvbuf[:, 0:2, :]
        hh = W[:, 14912:15424].rearrange("p (b f) -> p b f", b=2)
        gu_lo = [part(f"gu_lo{i}", f"gu{i}", 0, GU) for i in range(RING)]
        dn_lo = [part(f"dn_lo{i}", f"dn{i}", 0, DN) for i in range(RING)]
        ffn_up_hi = [part(f"ffn_up_hi{i}", over, first, DN)
                     for i, (over, first) in enumerate((("dn2", 0), ("dn3", 0), ("gu2", 0), ("gu2", DN)))]
        moe_up_hi = [part(f"moe_up_hi{i}", over, first, DN)
                     for i, (over, first) in enumerate((("W", 0), ("W", DN), ("x", 0), ("xT", 0)))]
        dn_hi = [part("ffn_dn_hi", "gu3", 0, 2 * DN), part("moe_dn_hi", "W", GU, 2 * DN)]
        xTh = part("xT_hi", "xT", 0, KD * S)[:, :].rearrange("p (k s) -> p k s", k=KD)
        xTl = part("xT_lo", "W", KD * W1_COLS, KD * S)[:, :].rearrange("p (k s) -> p k s", k=KD)
        hTh = part("hT_hi", "W", 15424, 512)[:, :].rearrange("p (b s q) -> p b s q", b=2, s=2)
        hTl = part("hT_lo", "W", 15936, 512)[:, :].rearrange("p (b s q) -> p b s q", b=2, s=2)
        w_in0_lo = part("w_in0_lo", "W", 0, KD * W0_COLS)[:, :].rearrange("p (k c) -> p k c", c=W0_COLS)
        w_cmp_lo = dn_lo[0][:, :].rearrange("p (k c) -> p k c", c=2 * P)
        w0_hi = [part(f"w0_hi{i}", over, first, KD * P) for i, (over, first) in enumerate(
            [("gu3", KD * P * n) for n in range(4)] + [("T8", 2048 + KD * P * n) for n in range(2)])]
        x0_lo = part("x0_lo", "T8", 0, KD * S)[:, :].rearrange("p (k s) -> p k s", k=KD)
        w_out_hi = part("w_out_hi", "gu2", 0, KD * D)[:, :].rearrange("p (k c) -> p k c", c=D)
        w_out_lo = part("w_out_lo", "W", 0, KD * D)[:, :].rearrange("p (k c) -> p k c", c=D)
        mixT_lo = part("mixT_lo", "W", KD * D, KD * S)[:, :].rearrange("p (k s) -> p k s", k=KD)
        w_in1 = W[:, 0:KD * W1_COLS].rearrange("p (k c) -> p k c", c=W1_COLS)
        kT1, kiT = kvbuf[:, 0, :], kvbuf[:, 1, :]
        v1 = kvbuf[:, 2, 0:TT * DH].rearrange("p (a d) -> p a d", a=2)
        g3 = gu[3]
        ts8 = g3[:, 0:2048].rearrange("p (b n) -> p b n", b=2)
        sel = g3[:, 2048:2560].rearrange("p (a k) -> p a k", a=2)
        qiT = g3[:, 2560:3072].rearrange("p (a k) -> p a k", a=2)
        relu = g3[:, 3072:4096].rearrange("p (b h k) -> p b h k", b=2, h=2)
        score = dn[3][:, 0:512].rearrange("p (a k) -> p a k", a=2)
        m8 = dn[3][:, 512:520]
        y = W[:, 8192:10240].rearrange("p (a d) -> p a d", a=2)
        xh = part("x_hi", "T8", 0, 2 * D)[:, :].rearrange("p (a d) -> p a d", a=2)
        xl = part("x_lo", "T8", 2 * D, 2 * D)[:, :].rearrange("p (a d) -> p a d", a=2)
        xgh = part("xg_hi", "W", 10240, D)[:, :].rearrange("p (k q) -> p k q", k=KD)
        xgl = part("xg_lo", "W", 11264, D)[:, :].rearrange("p (k q) -> p k q", k=KD)
        yeh = part("ye_hi", "W", 12288, D)
        yel = part("ye_lo", "W", 13312, D)
        pick = part("pick", "W", 14336, 2 * P)[:, :].rearrange("p (a q) -> p a q", a=2)
        pickT = part("pickT", "W", 14592, 2 * P)[:, :].rearrange("p (a q) -> p a q", a=2)
        rt = W[:, 10240:11264].rearrange("p (b n) -> p b n", b=4)
        wr = W[:, 12288:12352].rearrange("p (k e) -> p k e", e=8)
        ones = W[:, 12352:12480]

        ld_x, ld_cst, ld_vec, ld_pos, ld_w2, ld_w1, ld_flat = [sem(n) for n in (
            "ld_x", "ld_cst", "ld_vec", "ld_pos", "ld_w2", "ld_w1", "ld_flat")]
        ld_win = [sem(f"ld_win_part{i}") for i in range(4)]
        ld_wout, ld_win1, ld_lnp, ld_wr, rvec_stored = [sem(n) for n in (
            "ld_wout", "ld_win1", "ld_lnp", "ld_wr", "rvec_stored")]
        gu_loaded = [sem(f"gu_loaded{i}") for i in range(RING)]
        dn_loaded = [sem(f"dn_loaded{i}") for i in range(RING)]
        gu_used, dn_used = sem("gu_used"), sem("dn_used")
        front_pe, front_v, front_a = sem("front_pe"), sem("front_v"), sem("front_a")
        x0_hi_made, w0_hi_made, w0_lo_made = sem("x0_hi_made"), sem("w0_hi_made"), sem("w0_lo_made")
        t8a_made, vec_step = sem("t8a_made"), sem("vec_step")
        blk_made, cmp_pe, cmp_v, cmp_a = sem("blk_made"), sem("cmp_pe"), sem("cmp_v"), sem("cmp_a")
        w_added = sem("w_added")
        wo_hi_made, wo_lo_made = sem("wo_hi_made"), sem("wo_lo_made")
        gates_exp, gates_made = sem("gates_exp"), sem("gates_made")
        at = [{n: sem(f"at{layer}_{n}") for n in (
            "scores", "biased", "negmax", "sink_arg", "exp", "sink_exp", "pt", "pt_v", "pt_a", "o", "o_out")} for layer in range(2)]
        lnx = [{n: sem(f"ln{i}_{n}") for n in ("var", "sd", "x")} for i in range(4)]
        tr = [{n: sem(f"tr{i}_{n}") for n in ("pe", "v", "a")} for i in range(5)]
        outp = [sem("outp0"), sem("outp1")]
        ffn_g0, ffn_silu, ffn_h, ffn_t, ffn_hTh, ffn_hTl = [sem(n) for n in (
            "ffn_g0", "ffn_silu", "ffn_h", "ffn_t", "ffn_hTh", "ffn_hTl")]
        hi_made, lo_made, gu_first_used = sem("hi_made"), sem("lo_made"), sem("gu_first_used")
        ffn_out0 = sem("ffn_out0")
        xT_hi, xT_lo, x_hi, x_lo = sem("xT_hi"), sem("xT_lo"), sem("x_hi"), sem("x_lo")
        pr_pe, pr_v, pr_a = sem("pr_pe"), sem("pr_v"), sem("pr_a")
        idx_pe, idx_relu, idx_acc, idx_causal, idx_sel, ts_made = [sem(n) for n in (
            "idx_pe", "idx_relu", "idx_acc", "idx_causal", "idx_sel", "ts_made")]
        logits_pe, logits_v, route_exp, mask_made, rank_pe, route_done, moe_ones = [sem(n) for n in (
            "logits_pe", "logits_v", "route_exp", "mask_made", "rank_pe", "route_done", "moe_ones")]
        moe_silu, moe_h, moe_t, moe_hTh, moe_hTl = [sem(n) for n in (
            "moe_silu", "moe_h", "moe_t", "moe_hTh", "moe_hTl")]
        pick_made, gathered, xg_a, xg_v = [sem(n) for n in ("pick_made", "gathered", "xg_a", "xg_v")]
        pickT_pe, pickT_a, ye_a, ye_v, scattered, y_added = [sem(n) for n in (
            "pickT_pe", "pickT_a", "ye_a", "ye_v", "scattered", "y_added")]
        stored = sem("stored")

        front = [("xT", j) for j in range(4)]
        front += [("colsA", qaT, j, QA0 + P * j, 0) for j in range(4)]
        front += [("rvec",), ("pos",), ("cols", kaT, KA0, 0)]
        front += [("colsA", qbT, j, QB0 + P * j, 1) for j in range(4)]
        front += [("cmp", kv, P * kv, 2) for kv in range(2)]
        front += [("cols", ksT, KS0, 3), ("cols", kwT, KW0, 3)]
        front += [("v", tt) for tt in range(TT)] + [("flip", j) for j in range(8)]
        NF = len(front)

        def by_v(j):
            return front[j][0] == "xT" or j % 2 == 0

        def v_jobs(n):
            return sum(by_v(j) for j in range(n))

        def a_jobs(n):
            return n - v_jobs(n)

        pieces = []
        for j, job in enumerate(front):
            if job[0] in ("colsA", "cols", "cmp"):
                pieces.append((j, j, job[-1], job[0] == "cmp", slice(0, KD), slice(job[-2], job[-2] + P)))
            elif job == ("v", 0):
                pieces += [(j, j + 1, 3, False, slice(k, k + 2), slice(V0, W0_COLS)) for k in range(0, KD, 2)]

        def piece_views(p):
            _, _, _, cmp, rows, cols = pieces[p]
            n = rows.stop - rows.start
            hi = w0_hi[p % 6][:, 0:n * (cols.stop - cols.start)].rearrange("p (k c) -> p k c", k=n)
            return (w_cmp if cmp else w_in0)[:, rows, cols], hi, (w_cmp_lo if cmp else w_in0_lo)[:, rows, cols]

        def pieces_for(j):
            return [p for p in range(len(pieces)) if pieces[p][0] == j + 3 or (j == 0 and pieces[p][0] < 3)]

        units0 = [(kind, qt, g) for kind in "ASW" for qt in range(2) for g in range(2)]
        units1 = [("C", qt, c) for qt in range(2) for c in range(4)]

        def heads_of(u):
            kind, qt, g = u
            return [4 * g, 4 * g + 2, 4 * g + 1, 4 * g + 3] if kind == "C" else list(range(4 * g, 4 * g + 4))

        proj1 = [("qi", 0), ("qi", 1), ("ki",), ("v", 0), ("v", 1), ("k",)] + [("q", m) for m in range(8)]
        NP1, N_FIRST = len(proj1), 6
        CMP_DONE = {"hidden": 1, "z": 5, "gelu": 10, "kv": 13, "centred": 17, "coef": 21, "turned": 22,
                    "taken0": 23, "mixed0": 24, "mixed1": 26}

        FFN_PARTS = 3 * NC

        def ffn_up_part(c, h):
            return 3 * c + h + 1 if c else h + 1

        def ffn_dn_part(c):
            return 3 * c + 3

        def moe_parts(e):
            return FFN_PARTS + 7 + 3 * NC * e

        def moe_up_part(e, q, h):
            return moe_parts(e) + 3 * (q - 3) + h + 2

        def moe_dn_part(e, q, last):
            return moe_parts(e) + (3 * (NC - 3) + q - (NC - 3) if last and q >= NC - 2 else 3 * q - 2)

        def moe_buffer_chunks(e, q):
            if q < 2:
                e, q = e - 1, q + NC
            n = NC * e + (q - 1 if q < NC else 2 * NC - q)
            return max(n, 0) if isinstance(n, int) else n

        def wait_for_chunks(eng, sem, n):
            if not isinstance(n, int) or n > 0:
                eng.wait_ge(sem, n)

        block = ctx.enter_context(nc.Block())

        @block.sync
        def _(sp):
            w = t["l0_w_in"].rearrange("(k p) c -> p k c", p=P)
            sp.dma_start(cst[:, :], t["consts"]).then_inc(ld_cst, 16)
            sp.dma_start(x[:, :, :], t["x"][0].rearrange("(a p) d -> p a d", p=P)).then_inc(ld_x, 16)
            for i in range(4):
                if i == 2:
                    sp.dma_start(w_cmp, t["l0_w_cmp"].rearrange("(k p) c -> p k c", p=P)).then_inc(ld_win[2], 16)
                    continue
                a, b = (0, QB0, 0, KS0)[i], (QB0, KS0, 0, W0_COLS)[i]
                sp.dma_start(w_in0[:, :, a:b], w[:, :, a:b]).then_inc(ld_win[i], 16)
                if i == 3:
                    sp.wait_ge(front_v, v_jobs(front.index(("rvec",)) + 1))
                    sp.dma_start(scratch, rvec).then_inc(rvec_stored, 16)
                    sp.wait_ge(rvec_stored, 16)
                    src = bass.AP(scratch.tensor, scratch.offset, [[1, P], [VEC, 16], [1, S]])
                    sp.dma_start(flat_T, src).then_inc(ld_flat, 16)
            sp.dma_start(w1k, t["l0_cmpk_w1"].rearrange("(i p) n -> p i n", p=P)).then_inc(ld_w1, 16)
            sp.wait_ge(front_pe, front.index(("flip", 0)))
            sp.dma_start(w1v, t["l0_cmpv_w1"].rearrange("(i p) n -> p i n", p=P)).then_inc(ld_w1, 16)

            sp.wait_ge(front_pe, NF)
            for q in range(NC):
                if q == 1:
                    sp.wait_ge(tr[1]["pe"], 4)
                if q >= 2:
                    sp.wait_ge(gu_used, q - 1)
                sp.dma_start(gu[q % 2][:, :], t["l0_ffn_gate_up"][q]).then_inc(gu_loaded[q % 2], 16)
                if q in (3, 5, 7, 9):
                    sp.wait_ge(outp[0], 4)
                    k = slice(q - 3, q - 1)
                    w = t["l1_w_in"].rearrange("(k p) c -> p k c", p=P)
                    sp.dma_start(w_in1[:, k, :], w[:, k, :]).then_inc(ld_win1, 16)
                if q >= 2:
                    sp.wait_ge(dn_used, q - 1)
                sp.dma_start(dn[q % 2][:, :], t["l0_ffn_down"][q]).then_inc(dn_loaded[q % 2], 16)

            def weights(name, e, q):
                w = t[name][bass.ds(e, 1)] if not isinstance(e, int) else t[name][e:e + 1]
                return w.rearrange("o c p n -> (o c) p n")[q]

            def load_up(e, count, q):
                s = UP_SLOT[q]
                if isinstance(count, int) and count == 0 and q < RING:
                    if s < 2:
                        sp.wait_ge(gu_used, NC if (NC - 1) % 2 == s else NC - 1)
                    else:
                        sp.wait_ge(dn_used, NC)
                else:
                    sp.wait_ge(gu_used, chunks_before(UP_SLOT, count + 1, q))
                sp.dma_start(gu[s][:, :], weights("l1_exp_gate_up", e, q)).then_inc(gu_loaded[s], 16)

            def load_down(e, count, q):
                s = DN_SLOT[q]
                if isinstance(count, int) and count == 0 and q < RING:
                    if s < 2:
                        sp.wait_ge(dn_used, NC if (NC - 1) % 2 == s else NC - 1)
                    else:
                        sp.wait_ge(gu_used, NC)
                else:
                    sp.wait_ge(dn_used, chunks_before(DN_SLOT, count + 1, q))
                sp.dma_start(dn[s][:, :], weights("l1_exp_down", e, q)).then_inc(dn_loaded[s], 16)

            def expert(e, count, last, start=0):
                for q in range(start, NC):
                    if q + 2 < NC:
                        load_up(e, count, q + 2)
                    elif not last:
                        load_up(e + 1, count + 1, q + 2 - NC)
                    load_down(e, count, q)

            for q in range(RING - 1):
                load_up(0, 0, q)
                load_down(0, 0, q)
            sp.wait_ge(tr[3]["pe"], 4)
            load_up(0, 0, RING - 1)
            load_down(0, 0, RING - 1)
            load_up(0, 0, RING)
            load_up(0, 0, RING + 1)
            expert(0, 0, False, start=RING)
            with sp.Fori(1, NE - 1) as e:
                expert(e, e, False)
            expert(NE - 1, NE - 1, True)

            sp.wait_ge(route_done, 1)
            over = sp.value_load(overflow[0:1, 0:1], min_val=0, max_val=S)
            with sp.If(over > CAP):
                for q in range(2):
                    load_up(0, NE, q)
                with sp.Fori(0, NE - 1) as e:
                    expert(e, e + NE, False)
                expert(NE - 1, 2 * NE - 1, True)
            for tt in range(TT):
                sp.wait_ge(lnx[3]["x"], tt + 1)
                sp.dma_start(out[0].rearrange("(a p) d -> p a d", p=P)[:, tt, :], y[:, tt, :]).then_inc(stored, 16)
            sp.wait_ge(stored, 16 * TT)

        @block.gpsimd
        def _(pool):
            pool.wait_ge(front_v, v_jobs(NF))
            pool.wait_ge(front_a, a_jobs(NF))
            nc.gpsimd.affine_select(out=T8a[:, :, 0:P], in_=T8[:, 0:8, 0:P], pattern=[[0, 8], [1, P]],
                                    compare_op=ALU.is_gt, fill=INV_SCALE * NEG, base=0,
                                    channel_multiplier=-1).then_inc(t8a_made, 1)
            nc.gpsimd.tensor_copy(T8a[:, :, P:S], T8[:, 0:8, P:S]).then_inc(t8a_made, 1)
            for qt in range(TT):
                wk = P * (qt + 1)
                pool.wait_ge(idx_acc, 8 * (qt + 1))
                nc.gpsimd.affine_select(out=score[:, qt, 0:wk], in_=score[:, qt, 0:wk], pattern=[[-1, wk]],
                                        compare_op=ALU.is_ge, fill=NEG, base=P * qt,
                                        channel_multiplier=1).then_inc(idx_causal, 1)
            for i, (_, qt, c) in enumerate(units1):
                wk = P * (qt + 1)
                pool.wait_ge(idx_sel, qt + 1)
                if i >= 2:
                    pool.wait_ge(at[1]["biased"], 4 * (i - 1))
                dst = ts8[:, i % 2, 0:4 * wk].rearrange("p (h k) -> p h k", h=4)
                nc.gpsimd.tensor_tensor(dst, T8[:, 4 * c:4 * c + 4, S - wk:S], rep(sel[:, qt, 0:wk], 4),
                                        ALU.add).then_inc(ts_made, 1)

        def copy_front(eng, copy, j, ready):
            bank, job = ps[j % 8], front[j]
            eng.wait_ge(front_pe, j + 1)
            kind = job[0]
            if kind == "pos":
                copy(pos2, bank[:, 0:32].rearrange("p (v i) -> p v i", v=2)).then_inc(ready, 1)
            elif kind == "colsA":
                copy(job[1][:, job[2], :], bank[:, 0:S]).then_inc(ready, 1)
            elif kind == "cols":
                copy(job[1], bank[:, 0:S]).then_inc(ready, 1)
            elif kind == "cmp":
                for g in range(2):
                    dst, src = kt2[:, job[1], g, :], bank[DH * g:DH * (g + 1), :]
                    copy(dst[0:DH, :], src[:, 0:S])
                    last = copy(dst[DH:P, 0:S - 1], src[:, 1:S])
                last.then_inc(ready, 1)
            elif kind == "v":
                tt = job[1]
                copy(va[:, tt, :], bank[:, 0:P])
                copy(vs[:, tt, :], bank[:, P:2 * P])
                copy(vw[:, tt, :], bank[:, 2 * P:3 * P])
                copy(gates[:, tt, :], bank[:, 3 * P:3 * P + 24]).then_inc(ready, 1)
            elif kind == "flip":
                copy(T8[:, 2 * job[1]:2 * job[1] + 2, :], bank[:, :].rearrange("p (h k) -> p h k", h=2))\
                    .then_inc(ready, 1)

        def copy_p1(eng, copy, j, ready):
            bank, job = ps[j if j < N_FIRST else j - N_FIRST], proj1[j]
            eng.wait_ge(pr_pe, j + 1)
            if job[0] == "q":
                copy(qbuf[:, job[1], :], bank[:, 0:S]).then_inc(ready, 1)
            elif job[0] == "k":
                copy(kT1, bank[:, 0:S]).then_inc(ready, 1)
            elif job[0] == "qi":
                copy(qiT[:, job[1], :], bank[:, 0:S]).then_inc(ready, 1)
            elif job[0] == "ki":
                copy(kiT, bank[:, 0:S]).then_inc(ready, 1)
            else:
                copy(v1[:, job[1], :], bank[:, 0:DH])
                copy(wi[:, job[1], :], bank[:, DH:DH + 8]).then_inc(ready, 1)

        def of_bank(xt, j):
            return xt[:, 4 * (j % 2):4 * (j % 2) + 4, j // 2 * P:(j // 2 + 1) * P]

        def copy_tr(eng, copy, i, j, ready):
            eng.wait_ge(tr[i]["pe"], j + 1)
            copy(of_bank(xT, j), ps[j][:, :].rearrange("p (k s) -> p k s", k=4)).then_inc(ready, 1)

        @block.scalar
        def _(act):
            def copy(dst, src):
                return nc.scalar.copy(dst, src)

            act.dma_start(relb, t["rel_bias"]).then_inc(ld_vec, 16)
            act.dma_start(onehot, t["vecs"][:, 0:VEC]).then_inc(ld_vec, 16)
            act.dma_start(negvec, t["vecs"][0:16, VEC:2 * VEC]).then_inc(ld_vec, 16)
            act.dma_start(posrow[:, 0:P], t["l0_cmpk_pos"].rearrange("(i j) d -> i (j d)", j=2)).then_inc(ld_pos, 16)
            act.dma_start(posrow[:, P:2 * P], t["l0_cmpv_pos"].rearrange("(i j) d -> i (j d)", j=2))\
                .then_inc(ld_pos, 16)
            act.dma_start(w2k, t["l0_cmpk_w2"].rearrange("(f p) d -> p f d", p=P)).then_inc(ld_w2, 16)
            act.dma_start(w2v, t["l0_cmpv_w2"].rearrange("(f p) d -> p f d", p=P)).then_inc(ld_w2, 16)
            act.dma_start(sinks, to_all(t["l0_sinks"], 8)).then_inc(ld_w2, 16)
            for j in range(NF):
                for p in pieces_for(j):
                    act.wait_ge(ld_win[pieces[p][2]], 16)
                    if p >= 6:
                        act.wait_ge(front_pe, pieces[p - 6][1] + 1)
                    src, hi, _ = piece_views(p)
                    copy(hi, src).then_inc(w0_hi_made, 1)
                if front[j][0] == "xT":
                    act.wait_ge(front_pe, j + 1)
                    copy(xTh[:, 2 * j:2 * j + 2, :], ps[j][:, :].rearrange("p (k s) -> p k s", k=2))\
                        .then_inc(x0_hi_made, 1)
                elif not by_v(j):
                    copy_front(act, copy, j, front_a)
            act.wait_ge(front_pe, NF)
            act.dma_start(w_out, t["l0_w_out"].rearrange("(k p) c -> p k c", p=P)).then_inc(ld_wout, 16)
            act.wait_ge(front_v, v_jobs(NF))
            act.wait_ge(front_a, a_jobs(NF))
            nc.scalar.activation(gates, gates, ACT.Exp, scale=-1.0).then_inc(gates_exp, 1)

            def exps(a, units, i):
                u = units[i]
                wk = P * (u[1] + 1)
                act.wait_ge(a["negmax"], i + 1)
                if i >= 4:
                    act.wait_ge(a["o_out"], i - 3)
                for h in range(4):
                    nc.scalar.activation(s_sb[:, i % 4, h, 0:wk], s_sb[:, i % 4, h, 0:wk], ACT.Exp,
                                         bias=neg[:, i % 2, h:h + 1],
                                         accum_out=sums[:, i % 4, h:h + 1]).then_inc(a["exp"], 1)
                if u[0] == "A":
                    act.wait_ge(a["sink_arg"], i + 1)
                    nc.scalar.activation(ske[:, i % 4, :], sk[:, i % 2, :], ACT.Exp).then_inc(a["sink_exp"], 1)

            def pt_copy(a, units, i):
                nk = units[i][1] + 1
                act.wait_ge(a["pt"], i + 1)
                if i >= 2:
                    act.wait_ge(a["o"], i - 1)
                src = ps[5][:, :].rearrange("p (h k q) -> p h k q", h=2, k=2)[:, :, 0:nk, :]
                copy(pT[:, i % 2, 2:4, 0:nk, :], src).then_inc(a["pt_a"], 1)

            for i in range(len(units0) + 2):
                if i < len(units0):
                    exps(at[0], units0, i)
                if i >= 2:
                    pt_copy(at[0], units0, i - 2)
                if i == 4:
                    act.wait_ge(cmp_v, CMP_DONE["z"])
                    nc.scalar.activation(gel[:, 3, :], gel[:, 2, :], ACT.Exp,
                                         scale=-2.0 * math.sqrt(2.0 / math.pi)).then_inc(cmp_a, 1)
                if i == 8:
                    act.wait_ge(cmp_v, CMP_DONE["centred"])
                    nc.scalar.activation(csc, csc, ACT.Exp, scale=SCALE).then_inc(cmp_a, 1)
                if 5 <= i < 5 + KD:
                    if i == 5:
                        act.wait_ge(ld_wout, 16)
                        act.wait_ge(cmp_pe, 1)
                    copy(w_out_hi[:, i - 5, :], w_out[:, i - 5, :]).then_inc(wo_hi_made, 1)

            def layer_norm_sd(i, tt):
                act.wait_ge(lnx[i]["var"], tt + 1)
                sd = rstd[:, tt:tt + 1]
                nc.scalar.activation(sd, sd, ACT.Sqrt).then_inc(lnx[i]["sd"], 1)

            def ln_params(i, g, b):
                act.dma_start(lnp[:, 0, :], to_all(t[g], D)).then_inc(ld_lnp, 16)
                act.dma_start(lnp[:, 1, :], to_all(t[b], D)).then_inc(ld_lnp, 16)

            def hi_up(slot, dst, h, count, free, free_h):
                act.wait_ge(gu_loaded[slot], 16 * count)
                if free is not None:
                    act.wait_ge(gu_used if free_h else gu_first_used, free)
                copy(dst[:, :], gu[slot][:, h * DN:(h + 1) * DN]).then_inc(hi_made, 1)

            def hi_dn(slot, which, buf, count, free):
                act.wait_ge(dn_loaded[slot], 16 * count)
                if free is not None:
                    act.wait_ge(dn_used, free)
                copy(dn_hi[which][:, buf * DN:(buf + 1) * DN], dn[slot][:, :]).then_inc(hi_made, 1)

            def ffn_hi_up(c, h):
                hi_up(c % 2, ffn_up_hi[(2 * c + h) % 4], h, c // 2 + 1, c - 1 if c >= 2 else None, h)

            def ffn_silu_step(q):
                c, tt = q // 2, q % 2
                act.wait_ge(gu_used if tt else ffn_g0, c + 1)
                if q >= 2:
                    act.wait_ge(ffn_h, q - 1)
                nc.scalar.activation(sg[:, q % 2, :], ps[q % 3][:, 0:FC], ACT.Silu).then_inc(ffn_silu, 1)

            def ffn_hT_step(q):
                c = q // 2
                act.wait_ge(ffn_t, q + 1)
                if c >= 1:
                    act.wait_ge(dn_used, c)
                copy(hTh[:, q % 2, :, :], ps[3][:, 0:2 * P].rearrange("p (s q) -> p s q", s=2)).then_inc(ffn_hTh, 1)

            def mix_hi(j):
                act.wait_ge(tr[1]["pe"], j + 1)
                copy(of_bank(xTh, j), ps[j][:, :].rearrange("p (k s) -> p k s", k=4)).then_inc(tr[1]["a"], 1)

            act.wait_ge(at[0]["scores"], len(units0))
            act.wait_ge(cmp_pe, 5)
            ln_params(0, "l0_ln1_g", "l0_ln1_b")
            mix_hi(0)
            mix_hi(1)
            ffn_hi_up(0, 0)
            ffn_hi_up(0, 1)
            mix_hi(2)
            mix_hi(3)
            for tt in range(TT):
                layer_norm_sd(0, tt)
                for j in (2 * tt, 2 * tt + 1):
                    act.wait_ge(tr[0]["pe"], j + 1)
                    copy(of_bank(xTh, j), ps[j][:, :].rearrange("p (k s) -> p k s", k=4)).then_inc(xT_hi, 1)
            hi_dn(0, 0, 0, 1, None)
            act.wait_ge(lnx[0]["x"], TT)
            ln_params(1, "l0_ln2_g", "l0_ln2_b")
            for q in range(2 * NC):
                c, tt = q // 2, q % 2
                if tt and c + 1 < NC:
                    ffn_hi_up(c + 1, 0)
                    ffn_hi_up(c + 1, 1)
                if q >= 1:
                    ffn_hT_step(q - 1)
                ffn_silu_step(q)
                if tt == 0 and c:
                    hi_dn(c % 2, 0, c % 2, c // 2 + 1, c - 1 if c >= 2 else None)
            ffn_hT_step(2 * NC - 1)
            for tt in range(TT):
                layer_norm_sd(1, tt)
                for j in (3,) if tt else (0, 1):
                    copy_tr(act, copy, 2, j, tr[2]["a"])
            for j in range(1, N_FIRST, 2):
                copy_p1(act, copy, j, pr_a)
            for qt in range(TT):
                wk = P * (qt + 1)
                for i in range(4):
                    n = 4 * qt + i
                    act.wait_ge(idx_pe, qt + 1)
                    if n >= 2:
                        act.wait_ge(idx_acc, 2 * (n - 1))
                    src = ps[n][:, :].rearrange("p (h k) -> p h k", h=2)[:, :, 0:wk]
                    nc.scalar.activation(relu[:, n % 2, :, 0:wk], src, ACT.Relu).then_inc(idx_relu, 1)
            for j in range(N_FIRST, NP1):
                copy_p1(act, copy, j, pr_a)
            act.dma_start(w_out, t["l1_w_out"].rearrange("(k p) c -> p k c", p=P)).then_inc(ld_wout, 16)
            for i in range(len(units1) + 2):
                if i < len(units1):
                    exps(at[1], units1, i)
                if i >= 2:
                    pt_copy(at[1], units1, i - 2)
            act.wait_ge(at[1]["scores"], len(units1))
            ln_params(2, "l1_ln1_g", "l1_ln1_b")
            for j in (0, 1):
                copy_tr(act, copy, 3, j, tr[3]["a"])
            copy_tr(act, copy, 3, 3, tr[3]["a"])
            act.wait_ge(at[1]["o"], len(units1))
            act.dma_start(wr, t["l1_router"].rearrange("(k p) e -> p k e", p=P)).then_inc(ld_wr, 16)
            for tt in range(TT):
                layer_norm_sd(2, tt)
                for j in (3,) if tt else (0, 1):
                    copy_tr(act, copy, 4, j, tr[4]["a"])
            act.wait_ge(lnx[2]["x"], TT)
            ln_params(3, "l1_ln2_g", "l1_ln2_b")
            def loads(slots, e, q):
                s = slots[q]
                return len(range(s, NC, 2)) * (s < 2) + slots.count(s) * e + loads_up_to(slots, q)

            def moe_hi_up(e, q, h):
                c = q % NC
                n = chunks_before(HI_BUF, 0, 2 * c + h, 2 * NC) + 2 * NC * (q // NC) - 1
                hi_up(UP_SLOT[c], moe_up_hi[HI_BUF[2 * c + h]], h, loads(UP_SLOT, e + q // NC, c),
                      NC * (e + 1) + n // 2 + 1, n % 2)

            def moe_hi_dn(e, q):
                c = q % NC
                hi_dn(DN_SLOT[c], 1, c % 2, loads(DN_SLOT, e + q // NC, c),
                      NC + moe_buffer_chunks(e, q))

            def moe_silu_step(e, q):
                c = q % NC
                act.wait_ge(gu_used, NC * (e + 1) + q + 1)
                wait_for_chunks(act, moe_h, moe_buffer_chunks(e, q))
                nc.scalar.activation(sg[:, c % 2, :], ps[3 if c == 0 else c % 2][:, 0:FC], ACT.Silu)\
                    .then_inc(moe_silu, 1)

            def moe_hT_step(e, q):
                act.wait_ge(moe_t, NC * e + q + 1)
                act.wait_ge(dn_used, NC + moe_buffer_chunks(e, q))
                copy(hTh[:, q % NC % 2, :, :], ps[2][:, 0:2 * P].rearrange("p (s q) -> p s q", s=2))\
                    .then_inc(moe_hTh, 1)

            def take_xg(e):
                act.wait_ge(gathered, e + 1)
                act.wait_ge(gu_used, NC * (e + 1))
                for i in range(2):
                    copy(xgh[:, 4 * i:4 * i + 4, :], ps[6 + i][:, :].rearrange("p (k q) -> p k q", k=4))\
                        .then_inc(xg_a, 1)

            def take_ye(e):
                act.wait_ge(dn_used, NC * (e + 2))
                for half in range(2):
                    copy(yeh[:, half * HALF:(half + 1) * HALF], ps[4 + half][:, :]).then_inc(ye_a, 1)

            def expert(e, last):
                for q in range(2, NC + 2):
                    up, more = q < NC or not last, q < NC - 1 or not last
                    if q == NC + 1:
                        take_ye(e)
                    if up or q == NC:
                        moe_hi_dn(e, q - 1)
                    if more:
                        moe_hi_up(e, q + 1, 0)
                    if up or q == NC:
                        moe_hT_step(e, q - 1)
                    if q == NC - 1 and not last:
                        take_xg(e + 1)
                    if more:
                        moe_hi_up(e, q + 1, 1)
                    if up:
                        moe_silu_step(e, q)
                    if q == 4:
                        act.wait_ge(pickT_pe, e + 1)
                        copy(pickT, ps[3][:, 0:2 * P].rearrange("p (a q) -> p a q", a=2)).then_inc(pickT_a, 1)

            def moe_pass(n):
                first = NE * n
                if n:
                    moe_hi_up(first, 0, 0)
                    moe_hi_up(first, 0, 1)
                take_xg(first)
                if n == 0:
                    act.wait_ge(x_lo, TT)
                    act.wait_ge(y_added, 4)
                    act.wait_ge(logits_pe, 1)
                moe_hi_up(first, 1, 0)
                moe_hi_up(first, 1, 1)
                moe_silu_step(first, 0)
                moe_hi_dn(first, 0)
                moe_hi_up(first, 2, 0)
                moe_hT_step(first, 0)
                moe_hi_up(first, 2, 1)
                moe_silu_step(first, 1)
                with act.Fori(first, first + NE - 1) as e:
                    expert(e, False)
                expert(first + NE - 1, True)

            act.wait_ge(lnx[2]["x"], TT)
            for tt in range(TT):
                copy(xh[:, tt, :], x[:, tt, :]).then_inc(x_hi, 1)
            act.wait_ge(outp[1], 4)
            moe_hi_up(0, 0, 0)
            moe_hi_up(0, 0, 1)
            act.wait_ge(logits_v, 1)
            nc.scalar.activation(comb, comb, ACT.Exp).then_inc(route_exp, 1)
            moe_pass(0)
            act.wait_ge(route_done, 1)
            over = act.value_load(overflow[0:1, 0:1], min_val=0, max_val=S)
            with act.If(over > CAP):
                moe_pass(1)
            for tt in range(TT):
                layer_norm_sd(3, tt)

        @block.vector
        def _(dve):
            steps = [0]

            def link(ins):
                steps[0] += 1
                ins.then_inc(vec_step, 1)
                dve.wait_ge(vec_step, steps[0])

            def note(ins):
                steps[0] += 1
                ins.then_inc(vec_step, 1)

            def copy(dst, src):
                return nc.vector.tensor_copy(dst, src)

            v = nc.vector

            def low(dst, src, hi):
                return v.tensor_tensor(dst, src, hi.bitcast(F32), ALU.subtract)

            link(v.memset(kcbd, 0.0))
            link(v.memset(csc, INV_SCALE * NEG))
            for j in range(NF):
                for p in pieces_for(j):
                    dve.wait_ge(w0_hi_made, p + 1)
                    src, hi, lo = piece_views(p)
                    low(lo, src, hi).then_inc(w0_lo_made, 1)
                if front[j][0] == "xT":
                    dve.wait_ge(x0_hi_made, j + 1)
                    low(x0_lo[:, 2 * j:2 * j + 2, :], ps[j][:, :].rearrange("p (k s) -> p k s", k=2),
                        xTh[:, 2 * j:2 * j + 2, :]).then_inc(front_v, 1)
                elif front[j] == ("rvec",):
                    dve.wait_ge(front_pe, j + 1)
                    dve.wait_ge(ld_vec, 48)
                    v.scalar_tensor_tensor(out=rvec, in0=ps[j % 8][0:16, 0:VEC], scalar=INV_SCALE, in1=negvec,
                                           op0=ALU.mult, op1=ALU.add).then_inc(front_v, 1)
                elif by_v(j):
                    copy_front(dve, copy, j, front_v)
            dve.wait_ge(front_v, v_jobs(NF))
            dve.wait_ge(front_a, a_jobs(NF))
            for kv in range(2):
                for half in range(2):
                    src = kt2[:, kv].rearrange("p g (n i two) -> p i g n two", i=8, two=2)
                    src = src[:, :, :, half:half + N_CMP, 0]
                    dst = blk[:, kv, 8 * half:8 * half + 8, :].rearrange("p i (g n) -> p i g n", g=2)
                    pos = rep_last(pos2[:, kv, 8 * half:8 * half + 8], N_CMP)
                    for g in range(2):
                        v.tensor_tensor(dst[:, :, g, :], src[:, :, g, :], pos, ALU.add)\
                            .then_inc(blk_made, 1)
            dve.wait_ge(gates_exp, 1)
            link(v.tensor_scalar(gates, gates, 1.0, None, ALU.add))
            v.reciprocal(gates, gates).then_inc(gates_made, 1)

            def bias_scores(a, units, i):
                u = units[i]
                kind, qt, g = u
                wk = P * (qt + 1)
                dve.wait_ge(a["scores"], i + 1)
                if i >= 2:
                    dve.wait_ge(a["exp"], 4 * (i - 1))
                if i >= 4:
                    dve.wait_ge(a["pt"], i - 3)
                if kind == "A" and i < 4:
                    if qt:
                        dve.wait_ge(t8a_made, 2)
                    if i == 0:
                        dve.wait_ge(ld_w2, 48)
                if kind == "C":
                    dve.wait_ge(ts_made, i + 1)
                for s, h in enumerate(heads_of(u)):
                    if kind == "A":
                        bias = T8a[:, h, :] if qt else T8[:, h, P:S]
                    elif kind == "C":
                        bias = ts8[:, i % 2, (h - 4 * g) * wk:(h - 4 * g + 1) * wk]
                    else:
                        bias = T8[:, 8 + h, S - wk:S]
                    src = ps[2 * (i % 2) + s // 2][:, (s % 2) * S:(s % 2) * S + wk]
                    init = sinks[:, h:h + 1] if kind == "A" else -3e38
                    v.tensor_tensor_reduce(out=s_sb[:, i % 4, s, 0:wk], in0=src, in1=bias, scale=SCALE, scalar=init,
                                           op0=ALU.add, op1=ALU.max, accum_out=mx[:, i % 2, s:s + 1])\
                        .then_inc(a["biased"], 1)
                dve.wait_ge(a["biased"], 4 * (i + 1))
                v.tensor_scalar(neg[:, i % 2, :], mx[:, i % 2, :], -1.0, None, ALU.mult).then_inc(a["negmax"], 1)
                if kind == "A":
                    dve.wait_ge(a["negmax"], i + 1)
                    if i >= 2:
                        dve.wait_ge(a["sink_exp"], i - 1)
                    v.tensor_tensor(sk[:, i % 2, :], sinks[:, 4 * g:4 * g + 4], neg[:, i % 2, :], ALU.add)\
                        .then_inc(a["sink_arg"], 1)

            def pt_copy(a, units, i):
                nk = units[i][1] + 1
                dve.wait_ge(a["pt"], i + 1)
                if i >= 2:
                    dve.wait_ge(a["o"], i - 1)
                src = ps[4][:, :].rearrange("p (h k q) -> p h k q", h=2, k=2)[:, :, 0:nk, :]
                copy(pT[:, i % 2, 0:2, 0:nk, :], src).then_inc(a["pt_v"], 1)

            def mix_out(a, units, i):
                kind, qt, g = units[i]
                dve.wait_ge(a["exp"], 4 * (i + 1))
                cf = coef[:, i % 2, :]
                if kind == "A":
                    dve.wait_ge(a["sink_exp"], i + 1)
                    link(v.tensor_tensor(cf, sums[:, i % 4, :], ske[:, i % 4, :], ALU.add))
                    link(v.reciprocal(cf, cf))
                else:
                    link(v.reciprocal(cf, sums[:, i % 4, :]))
                if kind in "SW":
                    dve.wait_ge(gates_made, 1)
                    br = 8 * (1 if kind == "S" else 2) + 4 * g
                    link(v.tensor_tensor(cf, cf, gates[:, qt, br:br + 4], ALU.mult))
                dve.wait_ge(a["o"], i + 1)
                src = ps[6][:, 0:S].rearrange("p (h d) -> p h d", h=4)
                cfb = rep_last(cf, DH)
                if kind == "C":
                    dst = mix[:, qt, S * g:S * (g + 1)].rearrange("p (r f d) -> p f r d", r=2, f=2)
                    v.tensor_tensor(dst, src.rearrange("p (f r) d -> p f r d", f=2),
                                    cfb.rearrange("p (f r) d -> p f r d", f=2), ALU.mult).then_inc(a["o_out"], 1)
                    return
                base = (0 if kind == "A" else HALF) + S * g
                dst = mix[:, qt, base:base + S].rearrange("p (h d) -> p h d", h=4)
                if kind == "W":
                    tmp = otmp.rearrange("p (h d) -> p h d", h=4)
                    v.tensor_tensor(tmp, src, cfb, ALU.mult).then_inc(a["o_out"], 1)
                    dve.wait_ge(a["o_out"], i + 1)
                    v.tensor_tensor(dst, dst, tmp, ALU.add).then_inc(w_added, 1)
                    dve.wait_ge(w_added, i - 7)
                else:
                    v.tensor_tensor(dst, src, cfb, ALU.mult).then_inc(a["o_out"], 1)

            cn = [0]

            def cstep(ins):
                cn[0] += 1
                ins.then_inc(cmp_v, 1)
                dve.wait_ge(cmp_v, cn[0])

            def cmp_step(k):
                if k == 0:
                    dve.wait_ge(cmp_pe, 1)
                    cstep(copy(hid_rows, ps[7][0:2 * N_CMP, :]))
                elif k == 1:
                    dve.wait_ge(cmp_pe, 2)
                    cstep(copy(gel[:, 0, :], ps[7][:, 0:120]))
                    cstep(v.tensor_tensor(gel[:, 1, :], gel[:, 0, :], gel[:, 0, :], ALU.mult))
                    cstep(v.tensor_scalar(gel[:, 2, :], gel[:, 1, :], 0.044715, 1.0, ALU.mult, ALU.add))
                    cstep(v.tensor_tensor(gel[:, 2, :], gel[:, 2, :], gel[:, 0, :], ALU.mult))
                elif k == 2:
                    dve.wait_ge(cmp_a, 1)
                    cstep(v.tensor_scalar(gel[:, 4, :], gel[:, 3, :], 1.0, None, ALU.add))
                    cstep(v.reciprocal(gel[:, 4, :], gel[:, 4, :]))
                    cstep(v.tensor_tensor(gel[:, 5, :], gel[:, 4, :], gel[:, 0, :], ALU.mult))
                    src = gel[:, 5, 60:120].rearrange("p (f n) -> p f n", f=2)
                    dst = hidv.rearrange("p f (r n) -> p f r n", r=4)
                    for f in range(2):
                        cstep(copy(dst[:, f], rep(src[:, f, :], 4)))
                elif k == 3:
                    dve.wait_ge(cmp_pe, 3)
                    cstep(copy(kcbd[0:DH, 0:N_CMP], ps[7][0:DH, 0:N_CMP]))
                    cstep(copy(kcbd[DH:P, N_CMP:2 * N_CMP], ps[7][DH:P, N_CMP:2 * N_CMP]))
                    cstep(v.tensor_tensor(vcbd.rearrange("p (h d) -> p h d", h=8), rep(ps[7][0:120, DH:2 * DH], 8),
                                          rep_last(bdmask[0:120, :], DH), ALU.mult))
                elif k == 4:
                    dve.wait_ge(cmp_pe, 4)
                    sc = csc.rearrange("p (a j g n) -> p a j g n", a=2, j=4, g=2)
                    src = ps[7][:, 0:240].rearrange("p (a j g n) -> p a j g n", a=2, j=4, g=2)
                    first = 2 * 16 - 1
                    bias = T8[:, 8:16, :].rearrange("p (g j) k -> p j g k", g=2)
                    cstep(v.tensor_tensor(sc[:, 0, :, :, 0:7], src[:, 0, :, :, 0:7],
                                          bias[:, :, :, P + first::16], ALU.add))
                    cstep(v.tensor_tensor(sc[:, 1], src[:, 1], bias[:, :, :, first::16], ALU.add))
                    sc3 = csc.rearrange("p (h n) -> p h n", n=N_CMP)
                    cstep(v.tensor_reduce(cmp_m, sc3, AX.X, ALU.max))
                    cstep(v.tensor_tensor(sc3, sc3, rep_last(cmp_m, N_CMP), ALU.subtract))
                elif k == 5:
                    dve.wait_ge(cmp_a, 2)
                    sc3 = csc.rearrange("p (h n) -> p h n", n=N_CMP)
                    cstep(v.tensor_reduce(cmp_s, sc3, AX.X, ALU.add))
                    cstep(v.reciprocal(cmp_c, cmp_s))
                    gate = gates[:, :, 0:8].rearrange("p a (g j) -> p a j g", g=2)
                    c4 = cmp_c.rearrange("p (a j g) -> p a j g", a=2, j=4)
                    dve.wait_ge(gates_made, 1)
                    cstep(v.tensor_tensor(c4, c4, gate, ALU.mult))
                    cstep(v.tensor_scalar(cmp_c[:, 0:8], cmp_c[:, 0:8], rowvalid, None, ALU.mult))
                elif k == 6:
                    dve.wait_ge(cmp_pe, 5)
                    cstep(copy(cPT, ps[7][0:120, 0:2 * P].rearrange("p (a q) -> p a q", a=2)))
                else:
                    qt = k - 7
                    dve.wait_ge(cmp_pe, 6 + qt)
                    cstep(v.tensor_tensor(ctmp.rearrange("p (h d) -> p h d", h=8),
                                          ps[7][:, :].rearrange("p (h d) -> p h d", h=8),
                                          rep_last(cmp_c[:, 8 * qt:8 * qt + 8], DH), ALU.mult))
                    dst = mix[:, qt, HALF:D].rearrange("p (g j d) -> p j g d", g=2, j=4)
                    cstep(v.tensor_tensor(dst, dst, ctmp.rearrange("p (j g d) -> p j g d", j=4, g=2), ALU.add))

            CMP_AT = {2: 0, 3: 1, 5: 2, 6: 3, 7: 4, 9: 5, 10: 6, 11: 7, 12: 8}
            n0 = len(units0)
            def mix_lo(j):
                dve.wait_ge(tr[1]["a"], j + 1)
                low(of_bank(mixT_lo, j), ps[j][:, :].rearrange("p (k s) -> p k s", k=4), of_bank(xTh, j))\
                    .then_inc(tr[1]["v"], 1)

            for i in range(n0 + 3):
                if i < n0:
                    bias_scores(at[0], units0, i)
                if i == n0 + 2:
                    mix_lo(0)
                    mix_lo(1)
                if 2 <= i <= n0 + 1:
                    pt_copy(at[0], units0, i - 2)
                if i >= 3:
                    mix_out(at[0], units0, i - 3)
                if i in CMP_AT:
                    cmp_step(CMP_AT[i])
                if 6 <= i < 6 + KD:
                    dve.wait_ge(wo_hi_made, i - 5)
                    low(w_out_lo[:, i - 6, :], w_out[:, i - 6, :], w_out_hi[:, i - 6, :]).then_inc(wo_lo_made, 1)

            def out_add(sems, need, tt):
                for half in range(2):
                    n = 2 * tt + half
                    dve.wait_ge(sems, need(n))
                    dst = x[:, tt, half * HALF:(half + 1) * HALF]
                    link(v.scalar_tensor_tensor(out=dst, in0=dst, scalar=ALPHA, in1=ps[4 + n][:, :],
                                                op0=ALU.mult, op1=ALU.add))

            def layer_norm(i, z, tt):
                note(v.bn_stats(bnst[:, tt, 0, :], z[:, tt, 0:HALF]))
                link(v.bn_stats(bnst[:, tt, 1, :], z[:, tt, HALF:D]))
                link(v.bn_aggr(mv[:, tt, :], bnst[:, tt, :, :]))
                r1 = rstd[:, tt:tt + 1]
                v.tensor_scalar(r1, mv[:, tt, 1:2], EPS, None, ALU.add).then_inc(lnx[i]["var"], 1)
                if tt == 0:
                    dve.wait_ge(ld_lnp, 32 * (i + 1))
                note(v.scalar_tensor_tensor(out=z[:, tt, :], in0=z[:, tt, :], scalar=mv[:, tt, 0:1],
                                            in1=lnp[:, 0, :], op0=ALU.subtract, op1=ALU.mult))
                dve.wait_ge(lnx[i]["sd"], tt + 1)
                link(v.reciprocal(r1, r1))
                v.scalar_tensor_tensor(out=z[:, tt, :], in0=z[:, tt, :], scalar=r1, in1=lnp[:, 1, :],
                                       op0=ALU.mult, op1=ALU.add).then_inc(lnx[i]["x"], 1)



            def lo_up(slot, hi, h, count):
                dve.wait_ge(hi_made, count)
                cols = slice(h * DN, (h + 1) * DN)
                low(gu_lo[slot][:, cols], gu[slot][:, cols], hi[:, :]).then_inc(lo_made, 1)

            def lo_dn(slot, which, buf, count):
                dve.wait_ge(hi_made, count)
                low(dn_lo[slot][:, :], dn[slot][:, :], dn_hi[which][:, buf * DN:(buf + 1) * DN]).then_inc(lo_made, 1)

            def ffn_hTl_step(q):
                dve.wait_ge(ffn_hTh, q + 1)
                low(hTl[:, q % 2, :, :], ps[3][:, 0:2 * P].rearrange("p (s q) -> p s q", s=2),
                    hTh[:, q % 2, :, :]).then_inc(ffn_hTl, 1)

            def ffn_h_step(q):
                dve.wait_ge(ffn_silu, q + 1)
                if q >= 2:
                    dve.wait_ge(ffn_t, q - 1)
                v.tensor_tensor(hh[:, q % 2, :], sg[:, q % 2, :], ps[q % 3][:, FC:2 * FC], ALU.mult)\
                    .then_inc(ffn_h, 1)

            lo_up(0, ffn_up_hi[0], 0, ffn_up_part(0, 0))
            lo_up(0, ffn_up_hi[1], 1, ffn_up_part(0, 1))
            mix_lo(2)
            mix_lo(3)
            for tt in range(TT):
                out_add(outp[0], lambda n: n + 1, tt)
                layer_norm(0, x, tt)
                for j in (2 * tt, 2 * tt + 1):
                    dve.wait_ge(xT_hi, j + 1)
                    low(of_bank(xTl, j), ps[j][:, :].rearrange("p (k s) -> p k s", k=4), of_bank(xTh, j))\
                        .then_inc(xT_lo, 1)
            lo_dn(0, 0, 0, ffn_dn_part(0))
            for q in range(2 * NC):
                c, tt = q // 2, q % 2
                if tt and c + 1 < NC:
                    lo_up((c + 1) % 2, ffn_up_hi[(2 * c + 2) % 4], 0, ffn_up_part(c + 1, 0))
                    lo_up((c + 1) % 2, ffn_up_hi[(2 * c + 3) % 4], 1, ffn_up_part(c + 1, 1))
                if q >= 1:
                    ffn_hTl_step(q - 1)
                ffn_h_step(q)
                if tt == 0 and c:
                    lo_dn(c % 2, 0, c % 2, ffn_dn_part(c))
            ffn_hTl_step(2 * NC - 1)
            dve.wait_ge(lnx[0]["x"], TT)
            for tt in range(TT):
                out_add(dn_used if tt else ffn_out0, lambda n: NC if tt else 1, tt)
                layer_norm(1, x, tt)
            copy_tr(dve, copy, 2, 2, tr[2]["v"])
            for j in range(0, N_FIRST, 2):
                copy_p1(dve, copy, j, pr_v)
            dve.wait_ge(pr_v, N_FIRST // 2)
            dve.wait_ge(pr_a, N_FIRST // 2)
            for qt in range(TT):
                wk = P * (qt + 1)
                sc = score[:, qt, 0:wk]
                for i in range(4):
                    n = 4 * qt + i
                    dve.wait_ge(idx_relu, n + 1)
                    for r in range(2):
                        h = i + 4 * r
                        src, w = relu[:, n % 2, r, 0:wk], wi[:, qt, h:h + 1]
                        if i == 0 and r == 0:
                            ins = v.tensor_scalar(sc, src, w, None, ALU.mult)
                        else:
                            ins = v.scalar_tensor_tensor(out=sc, in0=src, scalar=w, in1=sc, op0=ALU.mult,
                                                         op1=ALU.add)
                        ins.then_inc(idx_acc, 1)
                        dve.wait_ge(idx_acc, 2 * n + r + 1)
            for qt in range(TT):
                wk = P * (qt + 1)
                sc = score[:, qt, 0:wk]
                dve.wait_ge(idx_causal, qt + 1)
                for _ in range(TOPK // 8):
                    link(v.max(m8, sc))
                    link(v.match_replace(sc, m8, sc, TAKEN))
                v.tensor_scalar(sel[:, qt, 0:wk], sc, -2e38, INV_SCALE * NEG, ALU.is_gt, ALU.mult).then_inc(idx_sel, 1)
            n1 = len(units1)
            for i in range(n1 + 3):
                if i < n1:
                    bias_scores(at[1], units1, i)
                if 2 <= i <= n1 + 1:
                    pt_copy(at[1], units1, i - 2)
                if i >= 3:
                    mix_out(at[1], units1, i - 3)
            copy_tr(dve, copy, 3, 2, tr[3]["v"])
            dve.wait_ge(lnx[1]["x"], TT)
            for tt in range(TT):
                out_add(outp[1], lambda n: n + 1, tt)
                layer_norm(2, x, tt)
            copy_tr(dve, copy, 4, 2, tr[4]["v"])
            v.memset(ones, 1.0).then_inc(moe_ones, 1)
            for tt in range(TT):
                dve.wait_ge(x_hi, tt + 1)
                low(xl[:, tt, :], x[:, tt, :], xh[:, tt, :]).then_inc(x_lo, 1)
            lo_up(0, moe_up_hi[HI_BUF[0]], 0, FFN_PARTS + 1)
            dve.wait_ge(logits_pe, 1)
            link(copy(mask, ps[4][:, 0:16].rearrange("p (a e) -> p a e", a=2)))
            other = bass.AP(mask.tensor, mask.offset, [list(mask.ap[0]), [8, TT], [0, 8], [1, 8]])
            own = rep_last(mask, 8)
            tri = rep(tri8, TT)
            r8, e8 = [rt[:, n, 0:128].rearrange("p (a b c) -> p a b c", a=2, b=8) for n in range(2)]
            s1, top = rt[:, 2, 0:2], rt[:, 2, 2:4]
            link(v.tensor_reduce(top, mask, AX.X, ALU.max))
            v.tensor_tensor(comb, mask, rep_last(top, 8), ALU.subtract).then_inc(logits_v, 1)
            link(v.tensor_tensor(e8, other, own, ALU.is_equal))
            note(v.tensor_tensor(r8, other, own, ALU.is_gt))
            link(v.tensor_tensor(e8, e8, tri, ALU.mult))
            link(v.tensor_tensor(r8, r8, e8, ALU.add))
            link(v.tensor_reduce(rank, r8, AX.X, ALU.add))
            v.tensor_scalar(mask, rank, 1.5, None, ALU.is_lt).then_inc(mask_made, 1)
            dve.wait_ge(mask_made, 1)
            dve.wait_ge(route_exp, 1)
            link(v.tensor_tensor(comb, comb, mask, ALU.mult))
            link(v.tensor_reduce(s1, comb, AX.X, ALU.add))
            link(v.reciprocal(s1, s1))
            link(v.tensor_tensor(comb, comb, rep_last(s1, 8), ALU.mult))
            dve.wait_ge(rank_pe, 1)
            link(copy(rank, ps[5][:, 0:16].rearrange("p (a e) -> p a e", a=2)))
            cnt = rt[:, 0, 66:67]
            link(v.tensor_reduce(cnt, ps[5][:, 16:24], AX.X, ALU.max))
            copy(overflow[:, :], cnt).then_inc(route_done, 1)

            def make_picks(e, base):
                col = slice(e, e + 1) if isinstance(e, int) else bass.ds(e, 1)
                for tt in range(TT):
                    v.tensor_scalar(pick[:, tt, :], iota[:, base:base + P], rank[:, tt, col], mask[:, tt, col],
                                    ALU.is_equal, ALU.mult).then_inc(pick_made, 1)

            def moe_lo_up(e, q, h):
                lo_up(UP_SLOT[q % NC], moe_up_hi[HI_BUF[2 * (q % NC) + h]], h, moe_up_part(e, q, h))

            def moe_lo_dn(e, q, last=False):
                lo_dn(DN_SLOT[q % NC], 1, q % NC % 2, moe_dn_part(e, q, last))

            def moe_hTl_step(e, q):
                dve.wait_ge(moe_hTh, NC * e + q + 1)
                low(hTl[:, q % NC % 2, :, :], ps[2][:, 0:2 * P].rearrange("p (s q) -> p s q", s=2),
                    hTh[:, q % NC % 2, :, :]).then_inc(moe_hTl, 1)

            def moe_h_step(e, q):
                c = q % NC
                dve.wait_ge(moe_silu, NC * e + q + 1)
                wait_for_chunks(dve, moe_t, moe_buffer_chunks(e, q))
                v.tensor_tensor(hh[:, c % 2, :], sg[:, c % 2, :], ps[3 if c == 0 else c % 2][:, FC:2 * FC],
                                ALU.mult).then_inc(moe_h, 1)

            def take_xg(e):
                for i in range(2):
                    dve.wait_ge(xg_a, 2 * e + i + 1)
                    low(xgl[:, 4 * i:4 * i + 4, :], ps[6 + i][:, :].rearrange("p (k q) -> p k q", k=4),
                        xgh[:, 4 * i:4 * i + 4, :]).then_inc(xg_v, 1)

            def take_ye(e):
                for half in range(2):
                    dve.wait_ge(ye_a, 2 * e + half + 1)
                    cols = slice(half * HALF, (half + 1) * HALF)
                    low(yel[:, cols], ps[4 + half][:, :], yeh[:, cols]).then_inc(ye_v, 1)

            def add_scattered(e, ex):
                col = slice(ex, ex + 1) if isinstance(ex, int) else bass.ds(ex, 1)
                for n, bank in enumerate((6, 7, 4, 5)):
                    tt, half = n // 2, n % 2
                    dve.wait_ge(scattered, 4 * e + n + 1)
                    dst = y[:, tt, half * HALF:(half + 1) * HALF]
                    v.scalar_tensor_tensor(out=dst, in0=ps[bank][:, :], scalar=comb[:, tt, col], in1=dst,
                                           op0=ALU.mult, op1=ALU.add).then_inc(y_added, 1)

            def expert(e, ex, base, last):
                for q in range(2, NC + 2):
                    up, more = q < NC or not last, q < NC - 1 or not last
                    if q == NC + 1:
                        take_ye(e)
                    if up or q == NC:
                        moe_lo_dn(e, q - 1, last)
                    if more:
                        moe_lo_up(e, q + 1, 0)
                    if up or q == NC:
                        moe_hTl_step(e, q - 1)
                    if q == NC - 1 and not last:
                        take_xg(e + 1)
                    if more:
                        moe_lo_up(e, q + 1, 1)
                    if up:
                        moe_h_step(e, q)
                    if q == 5 and not last:
                        dve.wait_ge(pickT_pe, e + 1)
                        make_picks(ex + 1, base)
                dve.wait_ge(y_added, 4 * e + 4)
                add_scattered(e, ex)

            def moe_pass(n):
                base = P * n
                first = NE * n
                made = moe_parts(first) - 7
                make_picks(0, base)
                if n == 0:
                    for tt in range(TT):
                        v.tensor_scalar(y[:, tt, :], x[:, tt, :], ALPHA, None, ALU.mult).then_inc(y_added, 2)
                else:
                    lo_up(0, moe_up_hi[HI_BUF[0]], 0, made + 1)
                lo_up(0, moe_up_hi[HI_BUF[1]], 1, made + 2)
                take_xg(first)
                lo_up(1, moe_up_hi[HI_BUF[2]], 0, made + 3)
                lo_up(1, moe_up_hi[HI_BUF[3]], 1, made + 4)
                moe_h_step(first, 0)
                moe_lo_dn(first, 0)
                moe_lo_up(first, 2, 0)
                moe_hTl_step(first, 0)
                moe_lo_up(first, 2, 1)
                moe_h_step(first, 1)
                with dve.Fori(0, NE - 1) as e:
                    expert(e + first if n else e, e, base, False)
                expert(first + NE - 1, NE - 1, base, True)
                dve.wait_ge(y_added, 4 * NE * (n + 1) + 4)

            dve.wait_ge(vec_step, steps[0])
            moe_pass(0)
            dve.wait_ge(route_done, 1)
            over = dve.value_load(overflow[0:1, 0:1], min_val=0, max_val=S)
            with dve.If(over > CAP):
                moe_pass(1)
            for tt in range(TT):
                layer_norm(3, y, tt)

        @block.tensor
        def _(pe):
            mm = nc.tensor.matmul

            def over_k(dst, lhsT, rhs):
                for k in range(KD):
                    last = mm(dst, lhsT(k), rhs(k), start=(k == 0), stop=(k == KD - 1))
                return last

            def transposes(i, src, tt):
                for r in range(2):
                    for k in range(4):
                        last = nc.tensor.transpose(ps[2 * tt + r][:, k * P:(k + 1) * P],
                                                   src[:, tt, (4 * r + k) * P:(4 * r + k + 1) * P], ident)
                    last.then_inc(tr[i]["pe"], 1)

            def transposed(i, tt):
                pe.wait_ge(tr[i]["a"], 3 if tt else 2)
                if tt:
                    pe.wait_ge(tr[i]["v"], 1)

            def three(dst, a_hi, a_lo, b_hi, b_lo, start, stop):
                mm(dst, a_hi, b_hi, start=start, stop=False)
                mm(dst, a_hi, b_lo, start=False, stop=False)
                return mm(dst, a_lo, b_hi, start=False, stop=stop)

            pe.wait_ge(ld_cst, 16)
            for j, job in enumerate(front):
                kind, bank = job[0], ps[j % 8]
                if j >= 8:
                    pe.wait_ge(front_v if by_v(j - 8) else front_a, (v_jobs if by_v(j - 8) else a_jobs)(j - 7))
                mine = [p for p in range(len(pieces)) if pieces[p][0] <= j <= pieces[p][1]]
                if mine:
                    pe.wait_ge(front_v, v_jobs(4))
                    pe.wait_ge(w0_lo_made, mine[-1] + 1)
                if kind == "rvec":
                    pe.wait_ge(ld_vec, 48)
                    last = mm(bank[0:16, 0:VEC], relb, onehot, start=True, stop=True)
                elif kind == "pos":
                    pe.wait_ge(ld_pos, 32)
                    for n in range(2):
                        last = nc.tensor.transpose(bank[:, 16 * n:16 * n + 16], posrow[:, P * n:P * n + P],
                                                   ident[0:16, 0:16])
                elif kind == "xT":
                    pe.wait_ge(ld_x, 16)
                    for kk in range(2):
                        for tt in range(TT):
                            n = 2 * kk + tt
                            last = nc.tensor.transpose(bank[:, n * P:(n + 1) * P],
                                                       x[:, tt, (2 * job[1] + kk) * P:(2 * job[1] + kk + 1) * P],
                                                       ident)
                elif kind in ("colsA", "cols", "cmp"):
                    _, hi, lo = piece_views(mine[0])
                    for k in range(KD):
                        last = three(bank[:, 0:S], hi[:, k, :], lo[:, k, :], xTh[:, k, :], x0_lo[:, k, :],
                                     k == 0, k == KD - 1)
                elif kind == "v":
                    tok = slice(job[1] * P, (job[1] + 1) * P)
                    for k in range(KD):
                        _, hi, lo = piece_views(mine[k // 2])
                        last = three(bank[:, 0:W0_COLS - V0], xTh[:, k, tok], x0_lo[:, k, tok], hi[:, k % 2, :],
                                     lo[:, k % 2, :], k == 0, k == KD - 1)
                elif kind == "flip":
                    pe.wait_ge(ld_flat, 16)
                    last = mm(bank[:, :], flip, flat_T[:, 2 * job[1]:2 * job[1] + 2, :], start=True, stop=True)
                last.then_inc(front_pe, 1)
            pe.wait_ge(front_v, v_jobs(NF))
            pe.wait_ge(front_a, a_jobs(NF))

            def scores(a, units, i):
                kind, qt, g = units[i]
                wk = P * (qt + 1)
                if i >= 2:
                    pe.wait_ge(a["biased"], 4 * (i - 1))
                order = (0, 2, 1, 3) if kind == "C" else range(4)
                for s in order:
                    h = heads_of(units[i])[s]
                    if kind == "C":
                        r = slice(DH * (h % 2), DH * (h % 2) + DH)
                        q, k = qbuf[r, h // 2, qt * P:(qt + 1) * P], kT1[r, 0:wk]
                    else:
                        r = slice(DH * g, DH * g + DH)
                        q = (qaT if kind == "A" else qbT)[r, s, qt * P:(qt + 1) * P]
                        k = {"A": kaT, "S": ksT, "W": kwT}[kind][r, 0:wk]
                    last = mm(ps[2 * (i % 2) + s // 2][:, (s % 2) * S:(s % 2) * S + wk], q, k, start=True, stop=True)
                last.then_inc(a["scores"], 1)

            def turn(a, units, i):
                u = units[i]
                pe.wait_ge(a["exp"], 4 * (i + 1))
                if i >= 1:
                    pe.wait_ge(a["pt_v"], i)
                    pe.wait_ge(a["pt_a"], i)
                for s in range(4):
                    for kt in range(u[1] + 1):
                        n = 2 * (s % 2) + kt
                        last = nc.tensor.transpose(ps[4 + s // 2][:, n * P:(n + 1) * P],
                                                   s_sb[:, i % 4, s, kt * P:(kt + 1) * P], ident)
                last.then_inc(a["pt"], 1)

            def sum_values(a, units, i):
                kind, qt, g = units[i]
                pe.wait_ge(a["pt_v"], i + 1)
                pe.wait_ge(a["pt_a"], i + 1)
                if i >= 1:
                    pe.wait_ge(a["o_out"], i)
                for s in range(4):
                    for kt in range(qt + 1):
                        vv = v1[:, kt, :] if kind == "C" else \
                            {"A": va, "S": vs, "W": vw}[kind][:, kt, DH * g:DH * g + DH]
                        last = mm(ps[6][:, s * DH:(s + 1) * DH], pT[:, i % 2, s, kt, :], vv,
                                  start=(kt == 0), stop=(kt == qt))
                last.then_inc(a["o"], 1)

            def compressed(k):
                if k <= 1:
                    if k == 0:
                        pe.wait_ge(blk_made, 8)
                        pe.wait_ge(ld_w1, 32)
                    for i in range(CMP_PAIRS):
                        last = mm(ps[7][0:2 * N_CMP, CMP_HID * k:CMP_HID * (k + 1)], blk[:, k, i, :],
                                  (w1k, w1v)[k][:, i, :], start=(i == 0), stop=(i == CMP_PAIRS - 1))
                    if k == 0:
                        return
                elif k == 2:
                    pe.wait_ge(cmp_v, CMP_DONE["hidden"])
                    for n in range(4):
                        last = nc.tensor.transpose(ps[7][:, 2 * N_CMP * n:2 * N_CMP * (n + 1)],
                                                   hid_rows[:, P * n:P * (n + 1)], ident[0:2 * N_CMP, 0:2 * N_CMP])
                elif k == 3:
                    pe.wait_ge(cmp_v, CMP_DONE["gelu"])
                    pe.wait_ge(ld_w2, 48)
                    hid = gel[:, 5, :].rearrange("p (v f n) -> p v f n", v=2, f=2)
                    for f in range(2):
                        mm(ps[7][:, 0:30], w2k[:, f, :], hid[:, 0, f, :], start=(f == 0), stop=(f == 1))
                    for f in range(2):
                        last = mm(ps[7][0:120, DH:2 * DH], hidv[:, f, :], w2v[:, f, :],
                                  start=(f == 0), stop=(f == 1))
                elif k == 4:
                    pe.wait_ge(cmp_v, CMP_DONE["kv"])
                    for qt in range(TT):
                        for j in range(4):
                            n = 120 * qt + 30 * j
                            last = mm(ps[7][:, n:n + 30], qbT[:, j, qt * P:(qt + 1) * P], kcbd, start=True, stop=True)
                elif k == 5:
                    pe.wait_ge(cmp_a, 2)
                    for qt in range(TT):
                        last = nc.tensor.transpose(ps[7][0:120, qt * P:(qt + 1) * P], csc[:, 120 * qt:120 * qt + 120],
                                                   ident)
                else:
                    qt = k - 6
                    pe.wait_ge(cmp_v, CMP_DONE["taken0" if qt else "turned"])
                    last = mm(ps[7][:, :], cPT[:, qt, :], vcbd, start=True, stop=True)
                last.then_inc(cmp_pe, 1)

            def out_proj(i, tt):
                pe.wait_ge(ld_wout, 16 * (i + 1))
                tok = slice(tt * P, (tt + 1) * P)
                if i == 0:
                    pe.wait_ge(tr[1]["v"], 2 * tt + 2)
                    pe.wait_ge(wo_lo_made, KD)
                else:
                    transposed(3, tt)
                for half in range(2):
                    if tt and half:
                        pe.wait_ge(lnx[2 * i]["x"], 1)
                        transposes(4 * i, x, 0)
                    bank, cols = ps[4 + 2 * tt + half][:, :], slice(half * HALF, (half + 1) * HALF)
                    if i == 0:
                        for k in range(KD):
                            last = three(bank, xTh[:, k, tok], mixT_lo[:, k, tok], w_out_hi[:, k, cols],
                                         w_out_lo[:, k, cols], k == 0, k == KD - 1)
                    else:
                        last = over_k(bank, lambda k: xT[:, k, tok], lambda k: w_out[:, k, cols])
                    last.then_inc(outp[i], 1)

            CMP_AT = {0: 0, 1: 1, 3: 2, 5: 3, 6: 4, 9: 5, 11: 6, 12: 7}
            n0 = len(units0)
            for i in range(n0 + 3):
                if i < n0:
                    scores(at[0], units0, i)
                if 2 <= i <= n0 + 1:
                    turn(at[0], units0, i - 2)
                if i >= 3:
                    sum_values(at[0], units0, i - 3)
                if i in CMP_AT:
                    compressed(CMP_AT[i])
                if i == n0 + 1:
                    pe.wait_ge(at[0]["biased"], 4 * n0)
                    pe.wait_ge(w_added, 2)
                    pe.wait_ge(cmp_v, CMP_DONE["mixed0"])
                    transposes(1, mix, 0)
            out_proj(0, 0)
            pe.wait_ge(w_added, 4)
            pe.wait_ge(cmp_v, CMP_DONE["mixed1"])
            transposes(1, mix, 1)
            out_proj(0, 1)


            def up_products(dst, a_hi, a_lo, high, slot, need, used):
                for h in range(2):
                    if need is not None:
                        pe.wait_ge(lo_made, need[h])
                    for k in range(4 * h, 4 * h + 4):
                        last = three(dst, a_hi(k), a_lo(k), high[h][:, k % 4 * HALF:(k % 4 + 1) * HALF],
                                     gu_lo[slot][:, k * HALF:(k + 1) * HALF],
                                     k == 0, k == KD - 1)
                    if used[h] is not None:
                        last.then_inc(used[h], 1)

            def down_products(banks, buf, which, buf_dn, slot, first, final):
                for s in range(2):
                    for half in range(2):
                        c = s * D + half * HALF
                        last = three(ps[banks + half][:, :], hTh[:, buf, s, :], hTl[:, buf, s, :],
                                     dn_hi[which][:, buf_dn * DN + c:buf_dn * DN + c + HALF],
                                     dn_lo[slot][:, c:c + HALF], first and s == 0, final and s == 1)
                return last

            def ffn_up(q):
                c, tt = q // 2, q % 2
                if q == 1:
                    pe.wait_ge(lnx[0]["x"], TT)
                    transposes(0, x, 1)
                if q < 2:
                    pe.wait_ge(xT_lo, 2 * q + 2)
                if q >= 3:
                    pe.wait_ge(ffn_h, q - 2)
                up_products(ps[q % 3][:, :], lambda k: xTh[:, k, tt * P:(tt + 1) * P],
                            lambda k: xTl[:, k, tt * P:(tt + 1) * P],
                            [ffn_up_hi[(2 * c + h) % 4] for h in range(2)], c % 2,
                            None if tt else [ffn_up_part(c, 0), ffn_up_part(c, 1)],
                            [gu_first_used, gu_used] if tt else [None, ffn_g0])

            def ffn_turn(q):
                pe.wait_ge(ffn_h, q + 1)
                if q >= 1:
                    pe.wait_ge(ffn_hTl, q)
                for s in range(2):
                    last = nc.tensor.transpose(ps[3][:, s * P:(s + 1) * P], hh[:, q % 2, s * P:(s + 1) * P], ident)
                last.then_inc(ffn_t, 1)

            def ffn_down(q):
                c, tt = q // 2, q % 2
                pe.wait_ge(ffn_hTl, q + 1)
                if tt == 0:
                    pe.wait_ge(lo_made, ffn_dn_part(c))
                last = down_products(4 + 2 * tt, q % 2, 0, c % 2, c % 2, c == 0, c == NC - 1)
                if tt:
                    last.then_inc(dn_used, 1)
                elif c == NC - 1:
                    last.then_inc(ffn_out0, 1)

            for q in range(2 * NC + 2):
                if q < 2 * NC:
                    ffn_up(q)
                if 1 <= q <= 2 * NC:
                    ffn_turn(q - 1)
                if q >= 2:
                    ffn_down(q - 2)

            for tt in range(TT):
                pe.wait_ge(lnx[1]["x"], tt + 1)
                transposes(2, x, tt)
            for tt in range(TT):
                transposed(2, tt)
            pe.wait_ge(ld_win1, 64)
            def index_scores():
                pe.wait_ge(pr_v, N_FIRST // 2)
                pe.wait_ge(pr_a, N_FIRST // 2)
                for qt in range(TT):
                    wk = P * (qt + 1)
                    for h in range(8):
                        r = slice(32 * (h % 4), 32 * (h % 4) + 32)
                        last = mm(ps[4 * qt + h % 4][:, (h // 4) * S:(h // 4) * S + wk],
                                  qiT[r, h // 4, qt * P:(qt + 1) * P], kiT[r, 0:wk], start=True, stop=True)
                    last.then_inc(idx_pe, 1)

            for j, job in enumerate(proj1):
                if j == N_FIRST:
                    index_scores()
                bank = ps[j if j < N_FIRST else j - N_FIRST]
                if j >= N_FIRST:
                    pe.wait_ge(idx_relu, j - N_FIRST + 1)
                if job[0] == "v":
                    tt = job[1]
                    last = over_k(bank[:, 0:DH + 8], lambda k: xT[:, k, tt * P:(tt + 1) * P],
                                  lambda k: w_in1[:, k, V1:V1 + DH + 8])
                else:
                    c = {"q": 0, "k": K1, "qi": QI1, "ki": KI1}[job[0]] + (P * job[1] if len(job) > 1 else 0)
                    last = over_k(bank[:, 0:S], lambda k: w_in1[:, k, c:c + P], lambda k: xT[:, k, :])
                last.then_inc(pr_pe, 1)
            pe.wait_ge(pr_a, N_FIRST // 2 + NP1 - N_FIRST)
            n1 = len(units1)
            for i in range(n1 + 3):
                if i < n1:
                    scores(at[1], units1, i)
                if 2 <= i <= n1 + 1:
                    turn(at[1], units1, i - 2)
                if i >= 3:
                    sum_values(at[1], units1, i - 3)
                if i == n1 + 1:
                    pe.wait_ge(at[1]["biased"], 4 * n1)
                    pe.wait_ge(at[1]["o_out"], n1 // 2)
                    transposes(3, mix, 0)
            out_proj(1, 0)
            pe.wait_ge(at[1]["o_out"], n1)
            transposes(3, mix, 1)
            out_proj(1, 1)

            pe.wait_ge(ld_wr, 16)
            for tt in range(TT):
                if tt:
                    pe.wait_ge(lnx[2]["x"], TT)
                    transposes(4, x, tt)
                transposed(4, tt)
                last = over_k(ps[4][:, 8 * tt:8 * tt + 8], lambda k: xT[:, k, tt * P:(tt + 1) * P],
                              lambda k: wr[:, k, :])
            last.then_inc(logits_pe, 1)
            pe.wait_ge(mask_made, 1)
            pe.wait_ge(moe_ones, 1)
            mm(ps[5][:, 0:8], upper, mask[:, 0, :], start=True, stop=True)
            mm(ps[5][:, 8:16], ones, mask[:, 0, :], start=True, stop=False)
            mm(ps[5][:, 8:16], upper, mask[:, 1, :], start=False, stop=True)
            mm(ps[5][:, 16:24], ones, mask[:, 0, :], start=True, stop=False)
            mm(ps[5][:, 16:24], ones, mask[:, 1, :], start=False, stop=True).then_inc(rank_pe, 1)

            def moe_up(e, q, need):
                c = q % NC
                up_products(ps[3 if c == 0 else c % 2][:, :], lambda k: xgh[:, k, :], lambda k: xgl[:, k, :],
                            [moe_up_hi[HI_BUF[2 * c + h]] for h in range(2)], UP_SLOT[c], need, [gu_first_used, gu_used])

            def moe_turn(e, q):
                pe.wait_ge(moe_h, NC * e + q + 1)
                wait_for_chunks(pe, moe_hTl, NC * e + q)
                for s in range(2):
                    last = nc.tensor.transpose(ps[2][:, s * P:(s + 1) * P], hh[:, q % NC % 2, s * P:(s + 1) * P],
                                               ident)
                last.then_inc(moe_t, 1)

            def moe_down(e, q, last):
                if q == 0:
                    pe.wait_ge(y_added, 4 * e + 4)
                pe.wait_ge(moe_hTl, NC * e + q + 1)
                pe.wait_ge(lo_made, moe_dn_part(e, q, last))
                down_products(4, q % 2, 1, q % 2, DN_SLOT[q], q == 0, q == NC - 1).then_inc(dn_used, 1)

            def gather(e):
                pe.wait_ge(pick_made, 2 * e + 2)
                for k in range(KD):
                    for tt in range(TT):
                        for src in (xh, xl):
                            last = mm(ps[6 + k // 4][:, (k % 4) * P:(k % 4 + 1) * P],
                                      src[:, tt, k * P:(k + 1) * P], pick[:, tt, :],
                                      start=(tt == 0 and src is xh), stop=(tt == TT - 1 and src is xl))
                last.then_inc(gathered, 1)

            def turn_picks(e):
                for tt in range(TT):
                    last = nc.tensor.transpose(ps[3][:, tt * P:(tt + 1) * P], pick[:, tt, :].bitcast(F32), ident)
                last.then_inc(pickT_pe, 1)

            def scatter(e):
                pe.wait_ge(pickT_a, e + 1)
                for n, bank in enumerate((6, 7, 4, 5)):
                    tt, half = n // 2, n % 2
                    if n < 2:
                        pe.wait_ge(ye_v, 2 * e + half + 1)
                    cols = slice(half * HALF, (half + 1) * HALF)
                    mm(ps[bank][:, :], pickT[:, tt, :], yeh[:, cols], start=True, stop=False)
                    mm(ps[bank][:, :], pickT[:, tt, :], yel[:, cols], start=False, stop=True)\
                        .then_inc(scattered, 1)

            def expert(e, last):
                for q in range(2, NC + 2):
                    up = q < NC or not last
                    if q == NC + 1:
                        moe_down(e, NC - 1, last)
                    if q == NC and not last:
                        pe.wait_ge(xg_v, 2 * e + 4)
                        pe.wait_ge(pickT_a, e + 1)
                    if up:
                        moe_up(e, q, [moe_up_part(e, q, h) for h in range(2)])
                    if up or q == NC:
                        moe_turn(e, q - 1)
                    if q <= NC:
                        moe_down(e, q - 2, last)
                    if q == 3:
                        turn_picks(e)
                    if q == 7 and not last:
                        gather(e + 1)
                scatter(e)

            def moe_pass(n):
                first = NE * n
                made = moe_parts(first) - 7
                if n:
                    pe.wait_ge(y_added, 4 * first + 4)
                else:
                    pe.wait_ge(x_lo, TT)
                gather(first)
                pe.wait_ge(xg_v, 2 * first + 2)
                moe_up(first, 0, [made + 1, made + 2])
                moe_up(first, 1, [made + 3, made + 4])
                moe_turn(first, 0)
                with pe.Fori(first, first + NE - 1) as e:
                    expert(e, False)
                expert(first + NE - 1, True)

            moe_pass(0)
            pe.wait_ge(route_done, 1)
            over = pe.value_load(overflow[0:1, 0:1], min_val=0, max_val=S)
            with pe.If(over > CAP):
                moe_pass(1)


def constants():
    c = np.zeros((P, C_COLS), np.float32)
    i = np.arange(P)
    c[:, C_ID:C_ID + P] = np.eye(P)
    c[:, C_FLIP:C_FLIP + P] = np.eye(P)[::-1]
    c[:, C_UP:C_UP + P] = i[:, None] < i[None, :]
    c[:, C_IOTA:C_IOTA + S] = np.arange(S)
    c[:, C_TRI:C_TRI + 64] = (np.arange(8)[None, :] < np.arange(8)[:, None]).reshape(-1)
    c[:, C_ROW] = i >= 31
    c[:, C_BD:C_BD + 8] = (i[:, None] // N_CMP) == np.arange(8)[None, :]
    return c


def bias_vectors():
    dist = S - 1 - np.arange(VEC)
    n = np.maximum(dist, 0)
    large = NB // 2 + (np.log(np.maximum(n, 1).astype(np.float32) / np.float32(NB // 2))
                       / np.float32(math.log(MAXDIST / (NB // 2))) * (NB - NB // 2)).astype(np.int32)
    bucket = np.where(n < NB // 2, n, np.minimum(large, NB - 1))
    v = np.zeros((NB, 2 * VEC), np.float32)
    v[:, 0:VEC] = (bucket[None, :] == np.arange(NB)[:, None]) & (dist >= 0)[None, :]
    v[0:16, VEC:2 * VEC] = np.where(dist >= 0, 0.0, INV_SCALE * NEG)
    return v


def laid_out(a):
    w0 = a.pop("l0_w_in")
    cuts = np.cumsum([512, 128, 128, 512, 128, 128, 128, 128, 128, 128])
    qa, ka, va, qb, kc, vc, ks, vs, kw, vw, g = np.split(w0, cuts, axis=1)

    def by_pair(q):
        return q.reshape(D, 2, 4, DH).transpose(0, 2, 1, 3).reshape(D, 8 * DH)

    a["l0_w_in"] = np.concatenate([by_pair(qa), ka, by_pair(qb), ks, kw, va, vs, vw, g], axis=1)
    a["l0_w_cmp"] = np.concatenate([kc, vc], axis=1)
    a["l0_cmpk_w2"] = np.concatenate([a["l0_cmpk_w2"]] * 2, axis=1)
    q, k, v, qi, ki, wi = np.split(a["l1_w_in"], np.cumsum([D, DH, DH, 256, 32]), axis=1)
    a["l1_w_in"] = np.concatenate([q, k, k, v, wi, qi, ki, ki, ki, ki], axis=1)

    def up_chunks(gate, up):
        both = np.stack([w.reshape(*w.shape[:-2], KD, P, NC, FC) for w in (gate, up)], axis=-2)
        n = both.ndim
        order = list(range(n - 5)) + [n - 3, n - 4, n - 5, n - 2, n - 1]
        return np.ascontiguousarray(both.transpose(order)).reshape(*gate.shape[:-2], NC, P, GU)

    def down_chunks(w):
        w = w.reshape(*w.shape[:-2], NC, FC // P, P, D)
        return np.ascontiguousarray(np.swapaxes(w, -3, -2)).reshape(*w.shape[:-4], NC, P, DN)

    a["l0_ffn_gate_up"] = up_chunks(a.pop("l0_ffn_gate"), a.pop("l0_ffn_up"))
    a["l1_exp_gate_up"] = up_chunks(a.pop("l1_exp_gate"), a.pop("l1_exp_up"))
    a["l0_ffn_down"] = down_chunks(a["l0_ffn_down"])
    a["l1_exp_down"] = down_chunks(a["l1_exp_down"])
    return {n: np.ascontiguousarray(w) for n, w in a.items()}


def kernel(**inputs):
    import concourse.bacc as bacc
    from concourse.bass_utils import run_bass_kernel_spmd

    nc = bacc.Bacc("TRN2", target_bir_lowering=False, num_devices=1)
    arrays = laid_out({n: np.asarray(a) for n, a in inputs.items()})
    arrays["consts"] = constants()
    arrays["vecs"] = bias_vectors()
    t = {n: nc.dram_tensor(f"in_{n}", a.shape, mybir.dt.from_np(a.dtype), kind="ExternalInput").ap()
         for n, a in arrays.items()}
    out = nc.dram_tensor("out", (1, S, D), F32, kind="ExternalOutput").ap()
    scratch = nc.dram_tensor("bias_rows", (16, VEC), F32, kind="Internal").ap()
    build(nc, t, out, scratch)
    r = run_bass_kernel_spmd(nc, [{f"in_{n}": a for n, a in arrays.items()}], core_ids=[0])
    return r.results[0]["out"]
```
